# Optimizing a Trainium2 kernel written in Bass

```python
import math
import jax, jax.numpy as jnp
from jax import lax
import numpy as np

D_MODEL = 1024
BATCH = 1
SEQ = 2048
DEPTH = 1
DEC_BATCH = 8
DEC_SEQ = 4
PAST_LEN = 2048
PAGE_SIZE = 128

A_HEADS = 4
A_HD = 64
A_QK = 2 * A_HD
A_VD = 2 * A_HD
A_WIDTH = A_HEADS * A_VD
B_HEADS = 8
B_HD = 64
B_WIDTH = B_HEADS * B_HD
DIL_PATTERNS = ((128, 1), (512, 4), (2048, 16))
B_WIN_MAX = 2048
MIX_WIDTH = A_WIDTH + B_WIDTH
PROJ_SIZES = (A_HEADS * A_QK, A_HEADS * A_QK, A_HEADS * A_VD, B_WIDTH, B_WIDTH, B_WIDTH)
PROJ_WIDTH = sum(PROJ_SIZES)
D_FF = 2816
CONV_W = 3
BLK = 128
NORM_EPS = 1e-6

kernel_name = 'hymba_diffattn_dilated_convffn_step'

def rms_norm(x, g):
    xf = x.astype(jnp.float32)
    y = xf * lax.rsqrt(jnp.mean(xf * xf, axis=-1, keepdims=True) + NORM_EPS)
    return (y * g.astype(jnp.float32)).astype(x.dtype)

def alibi_slopes(n):
    return jnp.asarray(np.array([2.0 ** (-8.0 * (h + 1) / n) for h in range(n)], np.float32))

def diff_lambda(lq1, lk1, lq2, lk2, lam_init):
    f = lambda a, b: jnp.exp(jnp.sum(a.astype(jnp.float32) * b.astype(jnp.float32)))
    return f(lq1, lk1) - f(lq2, lk2) + lam_init

def mix_project(h, w_in_l):
    b_, t_ = h.shape[:2]
    p = jnp.einsum('btd,de->bte', h, w_in_l)
    qa, ka, va, qb, kb, vb = jnp.split(p, np.cumsum(PROJ_SIZES)[:-1].tolist(), axis=-1)
    return (qa.reshape(b_, t_, A_HEADS, A_QK), ka.reshape(b_, t_, A_HEADS, A_QK),
            va.reshape(b_, t_, A_HEADS, A_VD), qb.reshape(b_, t_, B_HEADS, B_HD),
            kb.reshape(b_, t_, B_HEADS, B_HD), vb.reshape(b_, t_, B_HEADS, B_HD))

def diff_attn_core(q, k, v, q_pos, k_pos, lam, slopes):
    q2 = q.reshape(q.shape[:3] + (2, A_HD))
    k2 = k.reshape(k.shape[:3] + (2, A_HD))
    s = jnp.einsum('bqhme,bkhme->bhmqk', q2, k2).astype(jnp.float32) * (A_HD ** -0.5)
    dist = q_pos[:, None] - k_pos[None, :]
    bias = -slopes[:, None, None] * dist.astype(jnp.float32)
    s = jnp.where(dist >= 0, s + bias[:, None], -jnp.inf)
    p = jax.nn.softmax(s, axis=-1)
    w = p[:, :, 0] - lam * p[:, :, 1]
    return jnp.einsum('bhqk,bkhe->bqhe', w, v.astype(jnp.float32))

def diff_attn_prompt(q, k, v, lam, slopes):
    b_, s_ = q.shape[:2]
    nblk = s_ // BLK
    qb = q.reshape(b_, nblk, BLK, A_HEADS, A_QK).transpose(1, 0, 2, 3, 4)
    k_pos = jnp.arange(s_)

    def one_block(args):
        qi, i = args
        q_pos = i * BLK + jnp.arange(BLK)
        return diff_attn_core(qi, k, v, q_pos, k_pos, lam, slopes)

    o = lax.map(one_block, (qb, jnp.arange(nblk)))
    return o.transpose(1, 0, 2, 3, 4).reshape(b_, s_, A_HEADS, A_VD)

def combine_branches(outs, lses):
    wts = jax.nn.softmax(jnp.stack(lses), axis=0)
    return jnp.sum(wts[..., None] * jnp.stack(outs), axis=0)

def dilated_branch_prompt(q, k, v, window, dil, slopes):
    b_, s_, h_, e_ = q.shape
    span = dil * BLK
    sp = -(-s_ // span) * span
    n_sub = sp // dil
    nblk = n_sub // BLK

    def to_blocks(a):
        a = jnp.pad(a, ((0, 0), (0, sp - s_), (0, 0), (0, 0)))
        a = a.reshape(b_, n_sub, dil, h_, e_).transpose(0, 2, 1, 3, 4)
        return a.reshape(b_, dil, nblk, BLK, h_, e_)

    def band(a):
        prev = jnp.pad(a, ((0, 0), (0, 0), (1, 0), (0, 0), (0, 0), (0, 0)))[:, :, :-1]
        return jnp.concatenate([prev, a], axis=3)

    qb, kb, vb = to_blocks(q), to_blocks(k), to_blocks(v)
    kk, vv = band(kb), band(vb)
    s = jnp.einsum('brnqhe,brnkhe->brnhqk', qb, kk).astype(jnp.float32) * (B_HD ** -0.5)
    a_idx = jnp.arange(BLK)[:, None]
    b_idx = jnp.arange(2 * BLK)[None, :]
    steps = a_idx + BLK - b_idx
    n_idx = jnp.arange(nblk)[:, None, None]
    valid = (steps >= 0) & (steps <= window // dil) & ((n_idx > 0) | (b_idx >= BLK))
    bias = -slopes[:, None, None] * (dil * steps).astype(jnp.float32)[None]
    s = jnp.where(valid[:, None], s + bias, -jnp.inf)
    lse = jax.nn.logsumexp(s, axis=-1)
    p = jnp.exp(s - lse[..., None])
    o = jnp.einsum('brnhqk,brnkhe->brnqhe', p, vv.astype(jnp.float32))
    o = o.reshape(b_, dil, n_sub, h_, e_).transpose(0, 2, 1, 3, 4).reshape(b_, sp, h_, e_)[:, :s_]
    lse = lse.transpose(0, 1, 2, 4, 3).reshape(b_, dil, n_sub, h_).transpose(0, 2, 1, 3).reshape(b_, sp, h_)[:, :s_]
    return o, lse

def dilated_prompt(q, k, v, slopes):
    outs, lses = [], []
    for window, dil in DIL_PATTERNS:
        o, lse = dilated_branch_prompt(q, k, v, window, dil, slopes)
        outs.append(o)
        lses.append(lse)
    return combine_branches(outs, lses)

def dilated_sample(q, kc, vc, buf_len, slopes):
    t_ = q.shape[1]
    outs, lses = [], []
    for window, dil in DIL_PATTERNS:
        steps = jnp.arange(window // dil + 1)
        idx = buf_len + jnp.arange(t_)[:, None] - dil * steps[None, :]
        valid = idx >= 0
        idx_c = jnp.maximum(idx, 0)
        kg = kc[:, idx_c]
        vg = vc[:, idx_c]
        s = jnp.einsum('bqhe,bqkhe->bhqk', q, kg).astype(jnp.float32) * (B_HD ** -0.5)
        s = s - slopes[:, None, None] * (dil * steps).astype(jnp.float32)[None, None, :]
        s = jnp.where(valid, s, -jnp.inf)
        lse = jax.nn.logsumexp(s, axis=-1)
        p = jnp.exp(s - lse[..., None])
        outs.append(jnp.einsum('bhqk,bqkhe->bqhe', p, vg.astype(jnp.float32)))
        lses.append(lse.transpose(0, 2, 1))
    return combine_branches(outs, lses)

def mix_output(oa, ob, subln_g, lam_init, norm_b_g, w_out_l, dtype):
    b_, t_ = oa.shape[:2]
    oa = rms_norm(oa, subln_g) * (1.0 - lam_init)
    ob = rms_norm(ob, norm_b_g)
    o = jnp.concatenate([oa.reshape(b_, t_, A_WIDTH), ob.reshape(b_, t_, B_WIDTH)], axis=-1).astype(dtype)
    return jnp.einsum('btm,md->btd', o, w_out_l)

def conv_ffn(h, conv_prev, w_gate_l, w_up_l, w_conv_l, b_conv_l, w_down_l):
    t_ = h.shape[1]
    g = jnp.einsum('btd,df->btf', h, w_gate_l)
    u = jnp.einsum('btd,df->btf', h, w_up_l)
    gp = jnp.concatenate([conv_prev.astype(g.dtype), g], axis=1)
    gc = sum(gp[:, j:j + t_] * w_conv_l[j] for j in range(CONV_W)) + b_conv_l
    a = (jax.nn.gelu(gc.astype(jnp.float32)) * u.astype(jnp.float32)).astype(h.dtype)
    return jnp.einsum('btf,fd->btd', a, w_down_l), gp[:, -(CONV_W - 1):]

def setup_inputs(seed: int = 0) -> dict:
    key = jax.random.key(seed)
    ks = iter(jax.random.split(key, 32))
    nrm = lambda shape, scale: scale * jax.random.normal(next(ks), shape, jnp.float32)
    gain = lambda shape: 1.0 + 0.05 * jax.random.normal(next(ks), shape, jnp.float32)
    n_pages = PAST_LEN // PAGE_SIZE
    n_used = DEC_BATCH * n_pages
    n_phys = n_used + (n_used + 3) // 4
    w_len = min(B_WIN_MAX, PAST_LEN)
    x_prompt = nrm((BATCH, SEQ, D_MODEL), 1.0)
    x_sample = nrm((DEC_BATCH, DEC_SEQ, D_MODEL), 1.0)
    cache_a_k = nrm((DEPTH, n_phys, PAGE_SIZE, A_HEADS, A_QK), 1.0)
    cache_a_v = nrm((DEPTH, n_phys, PAGE_SIZE, A_HEADS, A_VD), 1.0)
    page_table = jax.random.permutation(next(ks), n_phys)[:n_used].reshape(DEC_BATCH, n_pages).astype(jnp.int32)
    cache_win_k = nrm((DEPTH, DEC_BATCH, w_len, B_HEADS, B_HD), 1.0)
    cache_win_v = nrm((DEPTH, DEC_BATCH, w_len, B_HEADS, B_HD), 1.0)
    state_conv = nrm((DEPTH, DEC_BATCH, CONV_W - 1, D_FF), 1.0)
    return {
        'x_prompt': x_prompt, 'x_sample': x_sample,
        'cache_a_k': cache_a_k, 'cache_a_v': cache_a_v, 'page_table': page_table,
        'cache_win_k': cache_win_k, 'cache_win_v': cache_win_v, 'state_conv': state_conv,
        'norm_mix_pre': gain((DEPTH, D_MODEL)),
        'w_in': nrm((DEPTH, D_MODEL, PROJ_WIDTH), D_MODEL ** -0.5),
        'lambda_q1': nrm((DEPTH, A_HD), 0.1), 'lambda_k1': nrm((DEPTH, A_HD), 0.1),
        'lambda_q2': nrm((DEPTH, A_HD), 0.1), 'lambda_k2': nrm((DEPTH, A_HD), 0.1),
        'subln_a': gain((DEPTH, A_VD)),
        'norm_b_out': gain((DEPTH, B_HD)),
        'w_out': nrm((DEPTH, MIX_WIDTH, D_MODEL), MIX_WIDTH ** -0.5),
        'norm_mix_post': gain((DEPTH, D_MODEL)),
        'norm_ffn_pre': gain((DEPTH, D_MODEL)),
        'w_gate': nrm((DEPTH, D_MODEL, D_FF), D_MODEL ** -0.5),
        'w_up': nrm((DEPTH, D_MODEL, D_FF), D_MODEL ** -0.5),
        'w_conv': nrm((DEPTH, CONV_W, D_FF), CONV_W ** -0.5),
        'b_conv': nrm((DEPTH, D_FF), 0.01),
        'w_down': nrm((DEPTH, D_FF, D_MODEL), D_FF ** -0.5),
        'norm_ffn_post': gain((DEPTH, D_MODEL)),
    }

def reference(x_prompt, x_sample, cache_a_k, cache_a_v, page_table, cache_win_k, cache_win_v, state_conv,
              norm_mix_pre, w_in, lambda_q1, lambda_k1, lambda_q2, lambda_k2, subln_a, norm_b_out, w_out,
              norm_mix_post, norm_ffn_pre, w_gate, w_up, w_conv, b_conv, w_down, norm_ffn_post):
    slopes_a = alibi_slopes(A_HEADS)
    slopes_b = alibi_slopes(B_HEADS)
    db, t_new = x_sample.shape[:2]
    past = page_table.shape[1] * cache_a_k.shape[2]
    buf_len = cache_win_k.shape[2]
    p_win = min(B_WIN_MAX, x_prompt.shape[1])
    q_pos_s = past + jnp.arange(t_new)
    k_pos_s = jnp.arange(past + t_new)
    xp, xs = x_prompt, x_sample
    akp, avp, aks, avs, wkp, wvp, wks, wvs, cvp, cvs = ([] for _ in range(10))
    for l in range(DEPTH):
        lam_init = 0.8 - 0.6 * math.exp(-0.3 * l)
        lam = diff_lambda(lambda_q1[l], lambda_k1[l], lambda_q2[l], lambda_k2[l], lam_init)
        h = rms_norm(xp, norm_mix_pre[l])
        qa, ka, va, qb, kb, vb = mix_project(h, w_in[l])
        oa = diff_attn_prompt(qa, ka, va, lam, slopes_a)
        ob = dilated_prompt(qb, kb, vb, slopes_b)
        m = mix_output(oa, ob, subln_a[l], lam_init, norm_b_out[l], w_out[l], xp.dtype)
        xp = xp + rms_norm(m, norm_mix_post[l])
        akp.append(ka)
        avp.append(va)
        wkp.append(kb[:, -p_win:])
        wvp.append(vb[:, -p_win:])
        h = rms_norm(xs, norm_mix_pre[l])
        qa, ka, va, qb, kb, vb = mix_project(h, w_in[l])
        k_all = jnp.concatenate([cache_a_k[l][page_table].reshape(db, past, A_HEADS, A_QK).astype(ka.dtype), ka], axis=1)
        v_all = jnp.concatenate([cache_a_v[l][page_table].reshape(db, past, A_HEADS, A_VD).astype(va.dtype), va], axis=1)
        oa = diff_attn_core(qa, k_all, v_all, q_pos_s, k_pos_s, lam, slopes_a)
        kc = jnp.concatenate([cache_win_k[l].astype(kb.dtype), kb], axis=1)
        vc = jnp.concatenate([cache_win_v[l].astype(vb.dtype), vb], axis=1)
        ob = dilated_sample(qb, kc, vc, buf_len, slopes_b)
        m = mix_output(oa, ob, subln_a[l], lam_init, norm_b_out[l], w_out[l], xs.dtype)
        xs = xs + rms_norm(m, norm_mix_post[l])
        aks.append(ka)
        avs.append(va)
        wks.append(kc[:, -buf_len:])
        wvs.append(vc[:, -buf_len:])
        zeros_prev = jnp.zeros((xp.shape[0], CONV_W - 1, D_FF), xp.dtype)
        f, buf = conv_ffn(rms_norm(xp, norm_ffn_pre[l]), zeros_prev, w_gate[l], w_up[l], w_conv[l], b_conv[l], w_down[l])
        xp = xp + rms_norm(f, norm_ffn_post[l])
        cvp.append(buf)
        f, buf = conv_ffn(rms_norm(xs, norm_ffn_pre[l]), state_conv[l], w_gate[l], w_up[l], w_conv[l], b_conv[l], w_down[l])
        xs = xs + rms_norm(f, norm_ffn_post[l])
        cvs.append(buf)
    a_k_prompt, a_v_prompt = jnp.stack(akp), jnp.stack(avp)
    a_k_sample, a_v_sample = jnp.stack(aks), jnp.stack(avs)
    win_k_prompt, win_v_prompt = jnp.stack(wkp), jnp.stack(wvp)
    win_k_sample, win_v_sample = jnp.stack(wks), jnp.stack(wvs)
    conv_prompt, conv_sample = jnp.stack(cvp), jnp.stack(cvs)
    return (xp, xs, a_k_prompt, a_v_prompt, a_k_sample, a_v_sample, win_k_prompt, win_v_prompt,
            win_k_sample, win_v_sample, conv_prompt, conv_sample)


_drawn_inputs = setup_inputs


def setup_inputs(seed=0):
    import zlib

    import numpy as np

    out = dict(_drawn_inputs(seed))
    spreads = {}
    factors = {'lambda_q1': 200.0, 'b_conv': 8.0, 'lambda_q2': 42.672, 'lambda_k2': 8.0}
    for name, (base, spread) in spreads.items():
        noise = np.random.default_rng([zlib.crc32(name.encode()), seed]).standard_normal(out[name].shape)
        drawn = base * np.exp(spread * noise) if base else spread * noise
        out[name] = __import__('jax').numpy.asarray(drawn.astype(out[name].dtype))
    for name, factor in factors.items():
        out[name] = (out[name] * factor).astype(out[name].dtype)
    return out
```

```python
import concourse.bass as bass
from concourse import mybir
from contextlib import ExitStack

F32 = mybir.dt.float32
F32R = mybir.dt.float32r
I32 = mybir.dt.int32
ALU = mybir.AluOpType
ACT = mybir.ActivationFunctionType
AX = mybir.AxisListType

P = 128
D = 1024
DC = D // P
SEQ = 2048
NT = SEQ // P
DEC_B, DEC_T = 8, 4
NS = DEC_B * DEC_T
TOK = SEQ + NS
GRP = 512
NG = SEQ // GRP
TPG = GRP // P
A_HEADS, B_HEADS = 4, 8
PAST = 2048
PAGES = PAST // P
D_FF = 2816
FT = D_FF // P
EPS = 1e-6
QK_SCALE = 0.125
MASKED = -1.0e30
LAM_INIT = 0.8 - 0.6
ds = bass.ds


class Stage:

    def __init__(self, nc, name):
        self.nc, self.name, self.stack, self.sems = nc, name, ExitStack(), []

    def __enter__(self):
        self.stack.__enter__()
        return self

    def __exit__(self, *a):
        self.stack.__exit__(*a)
        self.nc.clear_and_free_semaphores(self.sems)
        self.nc.all_engine_barrier()

    def sb(self, name, shape, dt=F32):
        return self.stack.enter_context(self.nc.sbuf_tensor(f"{self.name}_{name}", shape, dt))

    def ps(self, name):
        return self.stack.enter_context(self.nc.psum_tensor(f"{self.name}_{name}", [P, 512], F32))

    def sem(self, name):
        self.sems.append(self.nc.alloc_semaphore(name=f"{self.name}_{name}"))
        return self.sems[-1]

    def block(self):
        return self.stack.enter_context(self.nc.Block())


class Waiter:

    def __init__(self, eng, passed):
        self.eng, self.passed = eng, passed

    def __call__(self, sem, value):
        self.eng.wait_ge(sem, value)

    def apart(self, sem, value):
        self.eng.wait_ge(sem, value)
        if not isinstance(value, int):
            self.eng.sem_inc(self.passed, 1)


def done(marks, size, i, pos):
    back, p = divmod(pos, size)
    return len(marks) * (i + back + 1) + sum(m <= p for m in marks)


PROJ = [(4, "k", 0), (8, "v", 1), (0, "q", None), (16, "k", 2), (20, "v", 3), (12, "q", None)]
NU = len(PROJ)
NAT = 5


def stage_norm_project(nc, t):
    with Stage(nc, "hT") as outer:
        hTh = outer.sb("h", [P, DC, TOK], F32R)
        hTl = outer.sb("l", [P, DC, TOK], F32R)
        norm_transpose(nc, t, hTh, hTl)
        project(nc, t, hTh, hTl)


def norm_transpose(nc, t, hTh, hTl):
    with Stage(nc, "nt") as s:
        xt = s.sb("x", [P, 2, D])
        hn = s.sb("hn", [P, 2, D])
        junk = s.sb("junk", [P, D])
        gain = s.sb("gain", [P, D])
        ident = s.sb("ident", [P, P])
        ss = s.sb("ss", [P, 2])
        eps = s.sb("eps", [P, 1])
        vr = s.sb("vr", [P, 2])
        rs = s.sb("rs", [P, 2])
        pt = [s.ps(f"t{i}") for i in range(4)]
        const_in, x_in = s.sem("const_in"), [s.sem("x_in0"), s.sem("x_in1")]
        sq, var, rstd, normed, turned, hi, lo = (s.sem(n) for n in ("sq", "var", "rstd", "normed", "turned", "hi", "lo"))
        block = s.block()
        LAST = NT // 2

        @block.sync
        def _(sp):
            wait = Waiter(sp, s.sem("passed_sp"))
            sp.dma_start(gain[:], t["norm_mix_pre"].partition_broadcast(P)).then_inc(const_in, 16)
            sp.dma_start(ident[:], t["c_ident"]).then_inc(const_in, 16)
            for k in range(2):
                sp.dma_start(xt[:, k], t["x_prompt"][k * P:(k + 1) * P]).then_inc(x_in[k], 16)
            with sp.Fori(0, LAST - 1) as i:
                for k in range(2):
                    wait.apart(normed, 2 * i + k + 1)
                    sp.dma_start(xt[:, k], t["x_prompt"][ds((2 * i + 2 + k) * P, P)]).then_inc(x_in[k], 16)
            sp.wait_ge(normed, NT - 1)
            sp.dma_start(xt[0:NS, 0], t["x_sample"]).then_inc(x_in[0], 16)

        @block.scalar
        def _(act):
            wait = Waiter(act, s.sem("passed_act"))
            act.wait_ge(const_in, 33)

            def square(k, n, n_in, rows=P):
                wait(x_in[k], n_in)
                if not (isinstance(n, int) and n == 0):
                    wait(normed, n)
                act.activation(junk[0:rows], xt[0:rows, k], ACT.Square,
                               accum_out=ss[0:rows, k:k + 1]).then_inc(sq, 1)
                wait(sq, n + 1)
                act.activation(vr[0:rows, k:k + 1], ss[0:rows, k:k + 1], ACT.Sqrt, scale=1.0 / D,
                               bias=eps[0:rows, :]).then_inc(var, 1)

            def high(half, n, cols, w):
                wait.apart(turned, 2 * n + half + 3)
                src = pt[half][:, :].rearrange("p (c x) -> p c x", c=4)[:, :, 0:w]
                act.activation(hTh[:, 4 * half:4 * half + 4, cols], src, ACT.Copy).then_inc(hi, 1)

            with act.Fori(0, LAST) as i:
                for k in range(2):
                    square(k, 2 * i + k, 16 * i + 16)
                    for half in range(2):
                        high(half, 2 * i + k, ds((2 * i + k) * P, P), P)
            square(0, NT, 16 * LAST + 16, NS)
            for half in range(2):
                high(half, NT, slice(SEQ, TOK), NS)

        @block.vector
        def _(dve):
            wait = Waiter(dve, s.sem("passed_dve"))
            dve.memset(eps[:], EPS).then_inc(const_in, 1)
            dve.wait_ge(const_in, 33)

            def norm(k, n, rows=P):
                wait(var, n + 1)
                dve.reciprocal(rs[0:rows, k:k + 1], vr[0:rows, k:k + 1]).then_inc(rstd, 1)
                wait(rstd, n + 1)
                wait(turned, 2 * n)
                dve.scalar_tensor_tensor(hn[0:rows, k], xt[0:rows, k], rs[0:rows, k:k + 1], gain[0:rows, :],
                                         ALU.mult, ALU.mult).then_inc(normed, 1)

            def low(half, n, cols, w):
                wait(hi, 2 * n + half + 1)
                src = pt[half][:, :].rearrange("p (c x) -> p c x", c=4)[:, :, 0:w]
                dve.tensor_tensor(hTl[:, 4 * half:4 * half + 4, cols], src,
                                  hTh[:, 4 * half:4 * half + 4, cols].bitcast(F32), ALU.subtract).then_inc(lo, 1)

            with dve.Fori(0, LAST) as i:
                for k in range(2):
                    norm(k, 2 * i + k)
                    for half in range(2):
                        low(half, 2 * i + k, ds((2 * i + k) * P, P), P)
            norm(0, NT, NS)
            for half in range(2):
                low(half, NT, slice(SEQ, TOK), NS)

        @block.tensor
        def _(pe):
            wait = Waiter(pe, s.sem("passed_pe"))
            pe.sem_inc(turned, 2)
            pe.wait_ge(const_in, 32)

            def turn(k, n, rows=P):
                wait(normed, n + 1)
                for half in range(2):
                    if not isinstance(n, int) or n >= 1:
                        wait(lo, 2 * n + half - 1)
                    for c in range(4):
                        cc = 4 * half + c
                        last = pe.transpose(pt[half][:, c * P:c * P + rows], hn[0:rows, k, cc * P:(cc + 1) * P],
                                            ident[0:rows, 0:rows])
                    last.then_inc(turned, 1)

            turn(0, 0)
            turn(1, 1)
            with pe.Fori(1, LAST) as i:
                for k in range(2):
                    turn(k, 2 * i + k)
            turn(0, NT, NS)


def project(nc, t, hTh, hTl):
    with Stage(nc, "pj") as s:
        wr = s.sb("wr", [P, 2, DC, P])
        wh = s.sb("wh", [P, 2, DC, P], F32R)
        wl = s.sb("wl", [P, 2, DC, P], F32R)
        st = s.sb("st", [P, 2, TOK])
        qh = s.sb("qh", [P, 2, GRP], F32R)
        ql = s.sb("ql", [P, 2, GRP], F32R)
        nat = s.sb("nat", [P, 2, TPG, P])
        vh = s.sb("vh", [P, 2, TPG, P], F32R)
        vl = s.sb("vl", [P, 2, TPG, P], F32R)
        ident = s.sb("ident", [P, P])
        acc = [s.ps(f"acc{i}") for i in range(NAT)]
        tb = [s.ps(f"tb{i}") for i in range(2)]
        const_in = s.sem("const_in")
        w_in = [s.sem("w_in0"), s.sem("w_in1")]
        w_hi, w_lo, mm, ev, qk_hi, qk_lo, turned, nat_ok, v_hi, v_lo = (s.sem(n) for n in (
            "w_hi", "w_lo", "mm", "ev", "qk_hi", "qk_lo", "turned", "nat_ok", "v_hi", "v_lo"))
        st_out = [s.sem("st_out0"), s.sem("st_out1")]
        qk_out = [s.sem("qk_out0"), s.sem("qk_out1")]
        nat_out = [s.sem("nat_out0"), s.sem("nat_out1")]
        v_out = [s.sem("v_out0"), s.sem("v_out1")]
        block = s.block()
        J = 4
        SIZE = NAT * NU
        ALL = list(range(SIZE))
        SPLIT = [NAT * u + g for u in range(NU) if PROJ[u][1] != "v" for g in range(NG)]
        TURN = [NAT * u + g for u in range(NU) if PROJ[u][1] != "q" for g in range(NAT)]
        VSPL = [NAT * u + g for u in range(NU) if PROJ[u][1] == "v" for g in range(NG)]
        STO = [NAT * u for u in range(NU) if PROJ[u][1] != "v"]

        def nth(marks, pos):
            return marks.index(pos)

        w_view = t["w_in"].rearrange("(c p) f -> p c f", p=P)
        first = {"q": t["qT"], "k": t["kT"]}

        def width(g):
            return GRP if g < NG else NS

        @block.sync
        def _(sp):
            wait = Waiter(sp, s.sem("passed_sp"))
            for k in range(2):
                sp.sem_inc(st_out[k], 16 * len(STO) // 2)
            sp.dma_start(ident[:], t["c_ident"]).then_inc(const_in, 16)
            for u in range(2):
                sp.dma_start(wr[:, u], w_view[:, :, PROJ[u][0] * P:(PROJ[u][0] + 1) * P]).then_inc(w_in[u], 16)

            def rows_out(j, u, g):
                kind, which = PROJ[u][1:]
                pos = NAT * u + g
                wait.apart(nat_ok, done(TURN, SIZE, j, pos))
                k, cols = nth(TURN, pos) % 2, ds(j * P, P)
                if g == NG:
                    sp.dma_start(t["s_rows"][which][:, cols], nat[0:NS, k, 0]).then_inc(nat_out[k], 16)
                    return
                rows = slice(g * GRP, (g + 1) * GRP)
                sp.dma_start(t["kv_out"][which][rows, cols].rearrange("(b p) e -> p b e", p=P),
                             nat[:, k]).then_inc(nat_out[k], 16)
                if kind == "v":
                    wait.apart(v_lo, done(VSPL, SIZE, j, pos))
                    for part, src in enumerate((vh, vl)):
                        sp.dma_start(t["v_split"][which // 2, part][rows, cols].rearrange("(b p) e -> p b e", p=P),
                                     src[:, g % 2].bitcast(F32)).then_inc(v_out[g % 2], 16)

            def split_out(j, u, g):
                kind = PROJ[u][1]
                wait.apart(qk_lo, done(SPLIT, SIZE, j, NAT * u + g))
                for part, src in enumerate((qh, ql)):
                    sp.dma_start(first[kind][part][ds(4 * (u // 3) + j, 1)][0][:, g * GRP:(g + 1) * GRP],
                                 src[:, g % 2].bitcast(F32)).then_inc(qk_out[g % 2], 16)

            with sp.Fori(0, J) as j:
                for u in range(NU):
                    kind, before = PROJ[u][1], PROJ[u - 1][1]
                    wait.apart(w_lo, NU * j + u + 1)
                    ahead = (PROJ[u + 2][0] + j) if u + 2 < NU else (PROJ[u + 2 - NU][0] + 1 + j)
                    sp.dma_start(wr[:, u % 2], w_view[:, :, ds(ahead * P, P)]).then_inc(w_in[u % 2], 16)
                    if before != "q":
                        for g in (2, 3, 4):
                            rows_out(j, u - 1, g)
                    for pair in ((0, 1), (2, 3)):
                        if kind != "v":
                            for g in pair:
                                split_out(j, u, g)
                        if kind != "q" and pair == (0, 1):
                            for g in pair:
                                rows_out(j, u, g)
                    if kind != "v":
                        wait.apart(ev, NAT * (NU * j + u) + NG + 1 + NAT)
                        sp.dma_start(t["s_feat"][0 if kind == "q" else 1][ds(4 * (u // 3) + j, 1)][0],
                                     st[:, u % 2, SEQ:TOK]).then_inc(st_out[u % 2], 16)
            for k in range(2):
                sp.wait_ge(w_in[k], 16 * (J * NU // 2 + 1))
                sp.wait_ge(qk_out[k], 32 * J * len(SPLIT) // 2)
                sp.wait_ge(nat_out[k], 16 * J * len(TURN) // 2)
                sp.wait_ge(v_out[k], 32 * J * len(VSPL) // 2)
                sp.wait_ge(st_out[k], 16 * (J + 1) * len(STO) // 2)

        @block.gpsimd
        def _(pool):
            wait = Waiter(pool, s.sem("passed_pool"))
            pool.sem_inc(v_lo, len(VSPL))

            def weights_low(n, k):
                wait(w_hi, n + 1)
                pool.tensor_tensor(wl[:, k], wr[:, k], wh[:, k].bitcast(F32), ALU.subtract).then_inc(w_lo, 1)

            def v_split(j, u, g):
                pos = NAT * u + g
                r = nth(VSPL, pos)
                wait(nat_ok, done(TURN, SIZE, j, pos))
                wait.apart(v_out[g % 2], 32 * (len(VSPL) // 2 * j + r // 2))
                k = nth(TURN, pos) % 2
                pool.tensor_copy(vh[:, g % 2], nat[:, k]).then_inc(v_hi, 1)
                wait(v_hi, len(VSPL) * j + r + 1)
                pool.tensor_tensor(vl[:, g % 2], nat[:, k], vh[:, g % 2].bitcast(F32), ALU.subtract).then_inc(v_lo, 1)

            weights_low(0, 0)
            with pool.Fori(0, J) as j:
                for u in range(NU):
                    if PROJ[u - 1][1] == "v":
                        for g in (2, 3):
                            v_split(j, u - 1, g)
                    weights_low(NU * j + u + 1, (u + 1) % 2)
                    if PROJ[u][1] == "v":
                        for g in (0, 1):
                            v_split(j, u, g)

        @block.scalar
        def _(act):
            wait = Waiter(act, s.sem("passed_act"))
            act.sem_inc(ev, NAT)

            def weights_high(n, k, seen):
                wait(w_in[k], seen)
                wait(mm, NAT * n)
                act.activation(wh[:, k], wr[:, k], ACT.Copy).then_inc(w_hi, 1)

            weights_high(0, 0, 16)
            with act.Fori(0, J) as j:
                for u in range(NU):
                    n = NU * j + u
                    wait(qk_lo, done(SPLIT, SIZE, j, NAT * (u - 2) + NG))
                    wait(turned, done(TURN, SIZE, j, NAT * (u - 2) + NG))
                    wait(st_out[u % 2], 16 * (done([m // NAT for m in STO if m // NAT % 2 == u % 2], NU, j, u - 2)))
                    for g in range(NAT):
                        wait(mm, NAT * n + g + 1 + NAT)
                        act.activation(st[:, u % 2, g * GRP:g * GRP + width(g)], acc[g][:, 0:width(g)], ACT.Copy,
                                       scale=QK_SCALE if PROJ[u][1] == "q" else 1.0).then_inc(ev, 1)
                        if g == 1:
                            weights_high(n + 1, (u + 1) % 2, 16 * (NU // 2 * j + (u + 1) // 2 + 1))

        @block.vector
        def _(dve):
            wait = Waiter(dve, s.sem("passed_dve"))
            dve.sem_inc(qk_lo, len(SPLIT))
            dve.sem_inc(nat_ok, len(TURN))

            def split(j, u, g):
                pos = NAT * u + g
                r = nth(SPLIT, pos)
                wait(ev, NAT * (NU * j + u) + g + 1 + NAT)
                wait(qk_out[g % 2], 32 * (len(SPLIT) // 2 * j + r // 2))
                src = st[:, u % 2, g * GRP:(g + 1) * GRP]
                dve.tensor_copy(qh[:, g % 2], src).then_inc(qk_hi, 1)
                wait(qk_hi, len(SPLIT) * j + r + 1)
                dve.tensor_tensor(ql[:, g % 2], src, qh[:, g % 2].bitcast(F32), ALU.subtract).then_inc(qk_lo, 1)

            def rows(j, u, g):
                pos = NAT * u + g
                q = nth(TURN, pos)
                wait(turned, done(TURN, SIZE, j, pos))
                wait(nat_out[q % 2], 16 * (len(TURN) // 2 * j + q // 2))
                back = TURN[q - 2] if q >= 2 else TURN[q - 2] - SIZE
                wait(v_lo, done(VSPL, SIZE, j, back))
                if g < NG:
                    dve.tensor_copy(nat[:, q % 2], tb[q % 2][:, :].rearrange("p (b e) -> p b e", b=TPG)).then_inc(nat_ok, 1)
                else:
                    dve.tensor_copy(nat[0:NS, q % 2, 0], tb[q % 2][0:NS, 0:P]).then_inc(nat_ok, 1)

            with dve.Fori(0, J) as j:
                for u in range(NU):
                    if PROJ[u - 1][1] != "q":
                        for g in (2, 3, 4):
                            rows(j, u - 1, g)
                    for pair in ((0, 1), (2, 3)):
                        if PROJ[u][1] != "v":
                            for g in pair:
                                split(j, u, g)
                        if PROJ[u][1] != "q" and pair == (0, 1):
                            for g in pair:
                                rows(j, u, g)

        @block.tensor
        def _(pe):
            wait = Waiter(pe, s.sem("passed_pe"))
            pe.sem_inc(mm, NAT)
            pe.sem_inc(turned, len(TURN))
            pe.wait_ge(const_in, 16)

            def products(n, u, groups):
                k = u % 2
                for g in groups:
                    wait(ev, NAT * n + g + 1)
                for c in range(DC):
                    for weights, parts in ((wh, (hTh, hTl)), (wl, (hTh,))):
                        for g in groups:
                            cols = slice(g * GRP, g * GRP + width(g))
                            for part in parts:
                                start = c == 0 and weights is wh and part is hTh
                                stop = c == DC - 1 and weights is wl
                                m = pe.matmul(acc[g][:, 0:width(g)], weights[:, k, c], part[:, c, cols],
                                              start=start, stop=stop)
                            if stop:
                                m.then_inc(mm, 1)

            def turn(j, u, g):
                q = nth(TURN, NAT * u + g)
                wait(ev, NAT * (NU * j + u) + g + 1 + NAT)
                back = TURN[q - 2] if q >= 2 else TURN[q - 2] - SIZE
                wait(nat_ok, done(TURN, SIZE, j, back))
                if g < NG:
                    for b in range(TPG):
                        last = pe.transpose(tb[q % 2][:, b * P:(b + 1) * P],
                                            st[:, u % 2, (TPG * g + b) * P:(TPG * g + b + 1) * P], ident[:])
                else:
                    last = pe.transpose(tb[q % 2][0:NS, 0:P], st[:, u % 2, SEQ:TOK], ident[:])
                last.then_inc(turned, 1)

            with pe.Fori(0, J) as j:
                for u in range(NU):
                    n = NU * j + u
                    wait(w_lo, n + 1)
                    products(n, u, (0, 1))
                    if PROJ[u - 1][1] != "q":
                        for g in (2, 3, 4):
                            turn(j, u - 1, g)
                    products(n, u, (2, 3, 4))
                    if PROJ[u][1] != "q":
                        for g in (0, 1):
                            turn(j, u, g)
def attend_a(nc, t):
    with Stage(nc, "aa") as s:
        kk = s.sb("kk", [P, 2, 2, SEQ], F32R)
        vh = s.sb("vh", [P, 2, NT, P], F32R)
        vl = s.sb("vl", [P, 2, NT, P], F32R)
        qq = s.sb("qq", [P, 2, 2, 2, GRP], F32R)
        bias = s.sb("bias", [P, 2, SEQ])
        p1 = s.sb("p1", [P, 2, TPG, SEQ])
        p2 = s.sb("p2", [P, 2, SEQ])
        wth = s.sb("wth", [P, 2, GRP], F32R)
        wtl = s.sb("wtl", [P, 2, GRP], F32R)
        oT = s.sb("oT", [P, GRP])
        on = s.sb("on", [P, 2, TPG, P])
        mx = s.sb("mx", [P, 2, 2, 4])
        nm = s.sb("nm", [P, 2, 2])
        ll = s.sb("ll", [P, 2, 2])
        rl = s.sb("rl", [P, 2, TPG, 2])
        c2 = s.sb("c2", [P, 2])
        lam4 = s.sb("lam4", [P, 4, 64])
        lam2 = s.sb("lam2", [P, 2, 64])
        lame = s.sb("lame", [P, 5])
        nlam = s.sb("nlam", [P, 1])
        ident = s.sb("ident", [P, P])
        sc = [s.ps(f"sc{i}") for i in range(4)]
        tb = [s.ps(f"tb{i}") for i in range(2)]
        ob = [s.ps(f"ob{i}") for i in range(2)]
        const_in, lam_step, lam_out = s.sem("const_in"), s.sem("lam_step"), s.sem("lam_out")
        k_in = [s.sem(f"k_in{i}") for i in range(2)]
        v_in = [s.sem(f"v_in{i}") for i in range(2)]
        b_in = [s.sem(f"b_in{i}") for i in range(2)]
        q_in = [s.sem(f"q_in{i}") for i in range(2)]
        o_out = [s.sem(f"o_out{i}") for i in range(2)]
        (scored, biased, max_ok, exp_ok, rl_ok, c2_ok, w_ok, turned, high, low, pv, o_read, o_turned, o_ok) = (
            s.sem(n) for n in ("scored", "biased", "max_ok", "exp_ok", "rl_ok", "c2_ok", "w_ok", "turned",
                               "high", "low", "pv", "o_read", "o_turned", "o_ok"))
        p2_ok = s.sem("p2_ok")
        block = s.block()
        HP = A_HEADS // 2
        NB_, NGB = 2 * NT, 2 * NG
        chunk, step = {}, {}
        for B in range(NB_):
            for m in range(2):
                for kc in range(B % NT // TPG + 1):
                    chunk[B, m, kc] = len(chunk)
        for g in range(NGB):
            for kb in range(TPG * (g % NG) + TPG):
                step[g, kb] = len(step)
        NC_, NST = len(chunk), len(step)

        def wid(B, kc):
            i = B % NT
            return GRP if kc < i // TPG else (i % TPG + 1) * P

        def keys(B):
            return (B % NT + 1) * P

        def part_steps(g, b, half):
            n, slot = TPG * (g % NG) + TPG, 2 * (b - 1) + half
            return range(n * slot // 6, n * (slot + 1) // 6) if slot >= 0 else range(0)

        def first_block(g, kb):
            return max(0, kb - TPG * (g % NG))

        @block.sync
        def _(sp):
            wait = Waiter(sp, s.sem("passed_sp"))
            for i, name in enumerate(("lambda_q1", "lambda_q2", "lambda_k1", "lambda_k2")):
                sp.dma_start(lam4[:, i], t[name].partition_broadcast(P)).then_inc(const_in, 16)
            sp.dma_start(ident[:], t["c_ident"]).then_inc(const_in, 16)

            def load_k(h, par):
                for part in range(2):
                    src = t["kT"][part][ds(h, 1)][0].rearrange("(m e) x -> e m x", m=2)
                    sp.dma_start(kk[64 * part:64 * part + 64, par].bitcast(F32), src).then_inc(k_in[par], 16)
                sp.dma_start(bias[:, par], t["c_bias_a"][ds(h, 1)][0]).then_inc(b_in[par], 16)

            def load_v(h, par):
                for part, dst in enumerate((vh, vl)):
                    src = t["v_split"][0, part][:, ds(h * P, P)].rearrange("(b p) e -> p b e", p=P)
                    sp.dma_start(dst[:, par].bitcast(F32), src).then_inc(v_in[par], 16)

            def load_q(h, g):
                for half in range(2):
                    for part in range(2):
                        src = t["qT"][part][ds(h, 1)][0][:, (g % NG) * GRP:(g % NG + 1) * GRP]
                        sp.dma_start(qq[64 * half:64 * half + 64, g % 2, part].bitcast(F32),
                                     src.rearrange("(m e) x -> e m x", m=2)).then_inc(q_in[g % 2], 16)

            def send(hp, g):
                wait.apart(o_ok, NGB * hp + g + 1 + 2)
                h = 2 * hp + g // NG
                dst = t["oa"][(g % NG) * GRP:(g % NG + 1) * GRP, ds(h * P, P)]
                sp.dma_start(dst.rearrange("(b p) e -> p b e", p=P), on[:, g % 2]).then_inc(o_out[g % 2], 16)

            for par in range(2):
                load_k(par, par)
                if par == 0:
                    load_q(0, 0)
                    load_q(0, 1)
                load_v(par, par)
            with sp.Fori(0, HP) as hp:
                for g in range(NGB):
                    wait.apart(scored, NC_ * hp + chunk[TPG * g + 3, 1, g % NG] + 1)
                    nxt = g + 2
                    if nxt < NGB:
                        load_q(2 * hp + nxt // NG, nxt)
                    else:
                        load_q((2 * hp + 2) % A_HEADS, nxt - NGB)
                    if g >= 1:
                        send(hp, g - 1)
                    if g in (NG, ):
                        wait.apart(biased, NC_ * hp + chunk[TPG * NG - 1, 1, NG - 1] + 1 + 4)
                        load_k((2 * hp + 2) % A_HEADS, 0)
                    if g == NG + 1:
                        wait.apart(pv, NST * hp + step[NG - 1, NT - 1] + 1 + 2)
                        load_v((2 * hp + 2) % A_HEADS, 0)
                wait.apart(biased, NC_ * (hp + 1) + 4)
                load_k((2 * hp + 3) % A_HEADS, 1)
                send(hp, NGB - 1)
                wait.apart(pv, NST * (hp + 1) + 2)
                load_v((2 * hp + 3) % A_HEADS, 1)
            for k in range(2):
                sp.wait_ge(o_out[k], 16 * HP * NG)
                sp.wait_ge(q_in[k], 64 * (HP * NG + 1))
                sp.wait_ge(k_in[k], 32 * (HP + 1))
                sp.wait_ge(v_in[k], 32 * (HP + 1))
                sp.wait_ge(b_in[k], 16 * (HP + 1))
            sp.wait_ge(lam_step, 5)
            sp.dma_start(t["nlam"], nlam[:]).then_inc(lam_out, 16)
            sp.wait_ge(lam_out, 16)

        @block.tensor
        def _(pe):
            wait = Waiter(pe, s.sem("passed_pe"))
            pe.sem_inc(pv, 2)
            pe.wait_ge(const_in, 80)

            def scores(hp, B, m):
                g, par = B // TPG, B // NT
                if m == 0 and B % TPG == 0:
                    wait(q_in[g % 2], 64 * (NG * hp + g // 2 + 1))
                    if g % NG == 0:
                        wait(k_in[par], 32 * (hp + 1))
                q = slice((B % TPG) * P, (B % TPG + 1) * P)
                for kc in range(B % NT // TPG + 1):
                    c = chunk[B, m, kc]
                    w = wid(B, kc)
                    wait(biased, NC_ * hp + c + 1)
                    cols = slice(kc * GRP, kc * GRP + w)
                    for part in range(2):
                        mm = pe.matmul(sc[c % 4][:, 0:w], qq[:, g % 2, part, m, q], kk[:, par, m, cols],
                                       start=part == 0, stop=part == 1)
                    mm.then_inc(scored, 1)

            def turn(hp, g, kb):
                x = step[g, kb]
                if kb == 0:
                    wait(w_ok, NB_ * hp + TPG * (g + 1))
                wait(low, NST * hp + x + 1)
                for b in range(first_block(g, kb), TPG):
                    mm = pe.transpose(tb[x % 2][:, b * P:(b + 1) * P], p1[:, g % 2, b, kb * P:(kb + 1) * P], ident[:])
                mm.then_inc(turned, 1)

            def weigh(hp, g, kb):
                x, par = step[g, kb], g // NG
                last = kb == TPG * (g % NG) + TPG - 1
                if kb == 0:
                    wait(v_in[par], 32 * (hp + 1))
                    wait(o_ok, NGB * hp + g + 1)
                wait(low, NST * hp + x + 1 + 2)
                c = slice(first_block(g, kb) * P, GRP)
                for n, (v, w) in enumerate(((vh, wth), (vh, wtl), (vl, wth))):
                    mm = pe.matmul(ob[g % 2][:, c], v[:, par, kb], w[:, x % 2, c], start=kb == 0 and n == 0,
                                   stop=last and n == 2)
                mm.then_inc(pv, 1)

            def turn_back(hp, g):
                wait(o_read, NGB * hp + g + 1)
                for b in range(TPG):
                    mm = pe.transpose(ob[g % 2][:, b * P:(b + 1) * P], oT[:, b * P:(b + 1) * P], ident[:])
                mm.then_inc(o_turned, 1)

            def steps(hp, g, kbs):
                for kb in kbs:
                    turn(hp, g, kb)
                    if kb > 0:
                        weigh(hp, g, kb - 1)

            with pe.Fori(0, HP) as hp:
                for g in range(NGB):
                    for b in range(TPG):
                        for m in range(2):
                            scores(hp, TPG * g + b, m)
                            if g > 0:
                                steps(hp, g - 1, part_steps(g - 1, b, m))
                    if g > 0:
                        weigh(hp, g - 1, TPG * ((g - 1) % NG) + TPG - 1)
                        turn_back(hp, g - 1)
                g = NGB - 1
                steps(hp, g, range(NT))
                weigh(hp, g, NT - 1)
                turn_back(hp, g)

        @block.vector
        def _(dve):
            wait = Waiter(dve, s.sem("passed_dve"))
            dve.sem_inc(biased, 4)
            dve.sem_inc(low, 2)
            dve.sem_inc(o_ok, 2)
            dve.wait_ge(const_in, 80)
            dve.tensor_tensor(lam2[:], lam4[:, 0:2], lam4[:, 2:4], ALU.mult).then_inc(lam_step, 1)
            dve.wait_ge(lam_step, 1)
            dve.tensor_reduce(lame[:, 0:2], lam2[:], AX.X, ALU.add).then_inc(lam_step, 1)
            dve.wait_ge(lam_step, 3)
            dve.tensor_tensor(lame[:, 4:5], lame[:, 3:4], lame[:, 2:3], ALU.subtract).then_inc(lam_step, 1)
            dve.wait_ge(lam_step, 4)
            dve.tensor_scalar(nlam[:], lame[:, 4:5], -LAM_INIT, None, ALU.add).then_inc(lam_step, 1)
            dve.wait_ge(lam_step, 5)

            def add_bias(hp, B, m):
                i, par = B % NT, B // NT
                if m == 0:
                    if i == 0:
                        wait(b_in[par], 16 * (hp + 1))
                    g = B // TPG
                    if g >= 2:
                        wait(turned, NST * hp + step[g - 2, TPG * ((g - 2) % NG) + TPG - 1] + 1)
                    else:
                        wait(turned, NST * hp)
                    wait(max_ok, NB_ * hp + B)
                else:
                    wait(w_ok, NB_ * hp + max(B - 1, 0))
                for kc in range(i // TPG + 1):
                    c, w = chunk[B, m, kc], wid(B, kc)
                    wait.apart(scored, NC_ * hp + c + 1)
                    dst = p1[:, B // TPG % 2, B % TPG] if m == 0 else p2[:, B % 2]
                    x = kc * GRP + (NT - 1 - i) * P
                    dve.tensor_tensor_reduce(dst[:, kc * GRP:kc * GRP + w], sc[c % 4][:, 0:w], bias[:, par, x:x + w],
                                             1.0, -3.0e38, ALU.add, ALU.max,
                                             mx[:, B % 2, m, kc:kc + 1]).then_inc(biased, 1)

            def negate_max(hp, B):
                n = B % NT // TPG + 1
                wait(biased, NC_ * hp + chunk[B, 1, n - 1] + 1 + 4)
                wait(exp_ok, 2 * (NB_ * hp + B))
                dve.tensor_reduce(nm[:, B % 2], mx[:, B % 2, :, 0:n], AX.X, ALU.max, negate=True).then_inc(max_ok, 1)

            def factors(hp, B):
                g, b = B // TPG, B % TPG
                wait(exp_ok, 2 * (NB_ * hp + B + 1) + 4)
                dve.reciprocal(rl[:, g % 2, b], ll[:, B % 2]).then_inc(rl_ok, 1)
                wait(rl_ok, NB_ * hp + B + 1)
                wait(w_ok, NB_ * hp + max(B - 1, 0))
                dve.scalar_tensor_tensor(c2[:, B % 2:B % 2 + 1], ll[:, B % 2, 0:1], nlam[:], rl[:, g % 2, b, 1:2],
                                         ALU.mult, ALU.mult).then_inc(c2_ok, 1)

            def split_low(hp, g, kbs):
                for kb in kbs:
                    x = step[g, kb]
                    c = slice(first_block(g, kb) * P, GRP)
                    wait(high, NST * hp + x + 1)
                    dve.tensor_tensor(wtl[:, x % 2, c], tb[x % 2][:, c], wth[:, x % 2, c].bitcast(F32),
                                      ALU.subtract).then_inc(low, 1)

            def finish(hp, g):
                wait(o_turned, NGB * hp + g + 1)
                wait(o_out[g % 2], 16 * (NG * hp + g // 2))
                for b in range(TPG):
                    mm = dve.tensor_scalar(on[:, g % 2, b], ob[g % 2][:, b * P:(b + 1) * P], rl[:, g % 2, b, 0:1],
                                           None, ALU.mult)
                mm.then_inc(o_ok, 1)

            with dve.Fori(0, HP) as hp:
                for g in range(NGB):
                    for b in range(TPG):
                        B = TPG * g + b
                        for m in range(2):
                            add_bias(hp, B, m)
                            if m == 1:
                                negate_max(hp, B)
                            elif B > 0:
                                factors(hp, B - 1)
                            if g > 0:
                                split_low(hp, g - 1, part_steps(g - 1, b, m))
                    if g > 0:
                        finish(hp, g - 1)
                factors(hp, NB_ - 1)
                split_low(hp, NGB - 1, range(NT))
                finish(hp, NGB - 1)

        @block.gpsimd
        def _(pool):
            wait = Waiter(pool, s.sem("passed_pool"))
            with pool.Fori(0, HP) as hp:
                for B in range(NB_):
                    n = keys(B)
                    wait.apart(c2_ok, NB_ * hp + B + 1)
                    w, y = p1[:, B // TPG % 2, B % TPG, 0:n], p2[:, B % 2, 0:n]
                    pool.tensor_scalar(y, y, c2[:, B % 2:B % 2 + 1], None, ALU.mult).then_inc(p2_ok, 1)
                    wait(p2_ok, NB_ * hp + B + 1)
                    pool.tensor_tensor(w, w, y, ALU.add).then_inc(w_ok, 1)

        @block.scalar
        def _(act):
            wait = Waiter(act, s.sem("passed_act"))
            act.sem_inc(exp_ok, 4)
            act.wait_ge(lam_step, 2)
            act.activation(lame[:, 2:4], lame[:, 0:2], ACT.Exp).then_inc(lam_step, 1)

            def expo(hp, B, m):
                n = keys(B)
                wait(max_ok, NB_ * hp + B + 1)
                x = (p1[:, B // TPG % 2, B % TPG] if m == 0 else p2[:, B % 2])[:, 0:n]
                if m == 0:
                    wait(c2_ok, NB_ * hp + max(B - 1, 0))
                act.activation(x, x, ACT.Exp, bias=nm[:, B % 2, m:m + 1],
                               accum_out=ll[:, B % 2, m:m + 1]).then_inc(exp_ok, 1)

            def split_high(hp, g, kbs):
                for kb in kbs:
                    x = step[g, kb]
                    c = slice(first_block(g, kb) * P, GRP)
                    wait(pv, NST * hp + x + 1)
                    wait(turned, NST * hp + x + 1)
                    act.activation(wth[:, x % 2, c], tb[x % 2][:, c], ACT.Copy).then_inc(high, 1)

            def read_out(hp, g):
                wait(pv, NST * hp + step[g, TPG * (g % NG) + TPG - 1] + 1 + 2)
                wait(o_turned, NGB * hp + g)
                act.activation(oT[:], ob[g % 2][:], ACT.Copy).then_inc(o_read, 1)

            with act.Fori(0, HP) as hp:
                for g in range(NGB):
                    for b in range(TPG):
                        for m in range(2):
                            if m == 1:
                                expo(hp, TPG * g + b, 0)
                            elif TPG * g + b > 0:
                                expo(hp, TPG * g + b - 1, 1)
                            if g > 0:
                                split_high(hp, g - 1, part_steps(g - 1, b, m))
                    if g > 0:
                        read_out(hp, g - 1)
                expo(hp, NB_ - 1, 1)
                split_high(hp, NGB - 1, range(NT))
                read_out(hp, NGB - 1)
DILS = (1, 4, 16)
NPAT = len(DILS)


def token_rows(dram, pat):
    if pat == 0:
        return [(0, NT, dram.rearrange("(b a) e -> a b e", a=P))]
    if pat == 2:
        return [(0, NT, dram.rearrange("(a r) e -> a r e", r=NT))]
    return [(4 * j, 4, dram[512 * j:512 * (j + 1)].rearrange("(a r) e -> a r e", r=4)) for j in range(4)]


def attend_b(nc, t):
    with Stage(nc, "ab") as s:
        kk = s.sb("kk", [P, 2, SEQ], F32R)
        qq = s.sb("qq", [P, 2, 2, SEQ], F32R)
        vv = s.sb("vv", [P, NPAT, 2, NT, P], F32R)
        bias = s.sb("bias", [P, 2, NPAT, 2 * P])
        pr = s.sb("pr", [P, 4, GRP])
        wth = s.sb("wth", [P, 2, GRP], F32R)
        wtl = s.sb("wtl", [P, 2, GRP], F32R)
        on = s.sb("on", [P, NPAT, NT, P])
        mx = s.sb("mx", [P, 2, NPAT, NT])
        nm = s.sb("nm", [P, 2, NPAT, NT])
        ll = s.sb("ll", [P, 2, NPAT, NT])
        stats = s.sb("stats", [P, NPAT, NT, B_HEADS, 2])
        ident = s.sb("ident", [P, P])
        sc = [s.ps(f"sc{i}") for i in range(4)]
        tb = [s.ps(f"tb{i}") for i in range(2)]
        ob = [s.ps(f"ob{i}") for i in range(2)]
        const_in, stats_out = s.sem("const_in"), s.sem("stats_out")
        h_in = [s.sem(f"h_in{i}") for i in range(2)]
        v_in = [s.sem(f"v_in{i}") for i in range(NPAT)]
        o_out = [s.sem(f"o_out{i}") for i in range(NPAT)]
        scored, biased, max_ok, exp_ok, turned, high, low, pv, o_ok, stat_ok = (s.sem(n) for n in (
            "scored", "biased", "max_ok", "exp_ok", "turned", "high", "low", "pv", "o_ok", "stat_ok"))
        block = s.block()
        HSTEPS = [(p, list(range(n * i, n * i + n))) for p, n in ((0, 2), (1, 2), (2, 4)) for i in range(NT // n)]
        SH, S, PAIRS = len(HSTEPS), 2 * len(HSTEPS), B_HEADS // 2
        LAST_OF = [max(i for i, (p, _) in enumerate(HSTEPS) if p == pat) for pat in range(NPAT)]
        NOG = 12
        H_DMAS, NOUT = 2 + 4 + 1, [1, 4, 1]
        V_DMAS = [2 * n for n in NOUT]

        def step(x):
            par, i = divmod(x, SH)
            return (par,) + HSTEPS[i]

        def has_prev(p, b):
            return p == 0 and b > 0 or p == 1 and b >= 4

        def o_group(x):
            par, p, blocks = step(x)
            return 6 * par + 2 * p + blocks[0] // 8

        def tiles(p, blocks):
            out = []
            for n, b in enumerate(blocks):
                if p == 2:
                    out.append((n, b, b))
                    continue
                if has_prev(p, b):
                    out.append((2 * n, b - (1 if p == 0 else 4), b))
                out.append((2 * n + 1, b, b))
            return out

        def used(ap, p, blocks):
            if p == 0 and blocks[0] == 0:
                return ap[:, P:]
            if p == 1 and blocks[0] < 4:
                return ap.rearrange("p (n t x) -> p n t x", n=2, t=2)[:, :, 1]
            return ap

        def tokens(p, b, back):
            d = DILS[p]
            start = {0: P * b, 1: 512 * (b // 4) + b % 4, 2: b}[p]
            n = 2 * P if back else P
            start -= P * d if back else 0
            return slice(start, start + (n - 1) * d + 1, d)

        @block.sync
        def _(sp):
            wait = Waiter(sp, s.sem("passed_sp"))
            sp.dma_start(ident[:], t["c_ident"]).then_inc(const_in, 16)

            def load_head(pair, par):
                for part in range(2):
                    src = t["kT"][part][ds(4 + pair, 1)][0][64 * par:64 * par + 64]
                    sp.dma_start(kk[64 * part:64 * part + 64, par].bitcast(F32), src).then_inc(h_in[par], 16)
                    src = t["qT"][part][ds(4 + pair, 1)][0][64 * par:64 * par + 64]
                    for half in range(2):
                        sp.dma_start(qq[64 * half:64 * half + 64, par, part].bitcast(F32), src).then_inc(h_in[par], 16)
                sp.dma_start(bias[:, par], t["c_bias_b"][ds(2 * pair + par, 1)][0]
                             .rearrange("n p x -> p n x")).then_inc(h_in[par], 16)

            def load_v(pair, p):
                for part in range(2):
                    for b0, n, src in token_rows(t["v_split"][1, part][:, ds(pair * P, P)], p):
                        sp.dma_start(vv[:, p, part, b0:b0 + n].bitcast(F32), src).then_inc(v_in[p], 16)

            load_head(0, 0)
            for p in range(NPAT):
                load_v(0, p)
            load_head(0, 1)
            with sp.Fori(0, PAIRS) as i:
                nxt = (i + 1) % PAIRS
                wait.apart(biased, S * i + SH + 4)
                load_head(nxt, 0)
                for p in range(NPAT):
                    wait.apart(pv, S * i + SH + LAST_OF[p] + 1 + 2)
                    load_v(nxt, p)
                    if p == NPAT - 1:
                        load_head(nxt, 1)
                    wait.apart(o_ok, NOG * i + 6 + 2 * p + 2 + 2)
                    for b0, n, dst in token_rows(t["ob"][p][:, ds(i * P, P)], p):
                        sp.dma_start(dst, on[:, p, b0:b0 + n]).then_inc(o_out[p], 16)
            for k in range(2):
                sp.wait_ge(h_in[k], 16 * H_DMAS * (PAIRS + 1))
            for p in range(NPAT):
                sp.wait_ge(v_in[p], 16 * V_DMAS[p] * (PAIRS + 1))
                sp.wait_ge(o_out[p], 16 * NOUT[p] * PAIRS)
            sp.wait_ge(stat_ok, 2 * PAIRS)
            for p in range(NPAT):
                for b0, n, dst in token_rows(t["stats"][p], p):
                    sp.dma_start(dst, stats[:, p, b0:b0 + n].rearrange("p b h k -> p b (h k)")).then_inc(stats_out, 16)
            sp.wait_ge(stats_out, 16 * sum(NOUT))

        @block.tensor
        def _(pe):
            wait = Waiter(pe, s.sem("passed_pe"))
            pe.sem_inc(turned, 4)
            pe.sem_inc(pv, 2)
            pe.wait_ge(const_in, 16)

            def scores(i, x):
                par, p, blocks = step(x)
                if x % SH == 0:
                    wait(h_in[par], 16 * H_DMAS * (i + 1))
                wait(biased, S * i + x + 1)
                for n, b in enumerate(blocks):
                    back = has_prev(p, b)
                    col = n * P if p == 2 else 2 * n * P + (0 if back else P)
                    w = 2 * P if back else P
                    for part in range(2):
                        mm = pe.matmul(sc[x % 4][:, col:col + w], qq[:, par, part, tokens(p, b, False)],
                                       kk[:, par, tokens(p, b, back)], start=part == 0, stop=part == 1)
                mm.then_inc(scored, 1)

            def turn(i, x):
                par, p, blocks = step(x)
                wait(exp_ok, S * i + x + 1)
                wait(low, S * i + x + 1)
                for c, _, _ in tiles(p, blocks):
                    mm = pe.transpose(tb[x % 2][:, c * P:(c + 1) * P], pr[:, x % 4, c * P:(c + 1) * P], ident[:])
                mm.then_inc(turned, 1)

            def weigh(i, x):
                par, p, blocks = step(x)
                og = o_group(x)
                if x % SH == 0 or step(x - 1)[1] != p:
                    wait(v_in[p], 16 * V_DMAS[p] * (i + 1))
                if blocks[0] % 8 == 0:
                    wait(o_ok, NOG * i + og + 1)
                wait(low, S * i + x + 1 + 2)
                for b in blocks:
                    mine = [(c, v) for c, v, bb in tiles(p, blocks) if bb == b]
                    n = 0
                    for c, v in mine:
                        for w, part in ((wth, 0), (wth, 1), (wtl, 0)):
                            mm = pe.matmul(ob[og % 2][:, (b % 8) * 64:(b % 8 + 1) * 64], w[:, x % 2, c * P:(c + 1) * P],
                                           vv[:, p, part, v, 64 * par:64 * par + 64], start=n == 0,
                                           stop=n == 3 * len(mine) - 1)
                            n += 1
                mm.then_inc(pv, 1)

            with pe.Fori(0, PAIRS) as i:
                for x in range(S + 3):
                    if x < S:
                        scores(i, x)
                    if 2 <= x < S + 2:
                        turn(i, x - 2)
                    if x >= 3:
                        weigh(i, x - 3)

        @block.vector
        def _(dve):
            wait = Waiter(dve, s.sem("passed_dve"))
            dve.sem_inc(biased, 4)
            dve.sem_inc(low, 2)

            def add_bias(i, x):
                par, p, blocks = step(x)
                if x % SH == 0:
                    wait(h_in[par], 16 * H_DMAS * (i + 1))
                wait(turned, S * i + x + 1)
                wait.apart(scored, S * i + x + 1)
                for n, b in enumerate(blocks):
                    back = has_prev(p, b)
                    col = n * P if p == 2 else 2 * n * P + (0 if back else P)
                    w = 2 * P if back else P
                    mm = dve.tensor_tensor_reduce(pr[:, x % 4, col:col + w], sc[x % 4][:, col:col + w],
                                                  bias[:, par, p, 2 * P - w:], 1.0, -3.0e38, ALU.add, ALU.max,
                                                  mx[:, par, p, b:b + 1])
                mm.then_inc(biased, 1)
                wait(biased, S * i + x + 1 + 4)
                b0, n = blocks[0], len(blocks)
                dve.tensor_scalar(nm[:, par, p, b0:b0 + n], mx[:, par, p, b0:b0 + n], -1.0, None,
                                  ALU.mult).then_inc(max_ok, 1)

            def split_low(i, x):
                _, p, blocks = step(x)
                wait(high, S * i + x + 1)
                dve.tensor_tensor(used(wtl[:, x % 2], p, blocks), used(tb[x % 2][:], p, blocks),
                                  used(wth[:, x % 2].bitcast(F32), p, blocks), ALU.subtract).then_inc(low, 1)

            def keep_stats(i, par):
                wait.apart(exp_ok, S * i + SH * (par + 1))
                dve.tensor_copy(stats[:, :, :, ds(2 * i + par, 1), 0], mx[:, par])
                dve.tensor_copy(stats[:, :, :, ds(2 * i + par, 1), 1], ll[:, par]).then_inc(stat_ok, 1)

            with dve.Fori(0, PAIRS) as i:
                for x in range(S + 2):
                    if x < S:
                        add_bias(i, x)
                    if x >= 2:
                        split_low(i, x - 2)
                    if x == SH + 2:
                        keep_stats(i, 0)
                keep_stats(i, 1)

        @block.scalar
        def _(act):
            wait = Waiter(act, s.sem("passed_act"))
            act.sem_inc(o_ok, 2)

            def expo(i, x):
                par, p, blocks = step(x)
                if x % SH == 0:
                    wait(stat_ok, 2 * i + par if par == 0 else 2 * i)
                wait(max_ok, S * i + x + 1)
                for n, b in enumerate(blocks):
                    back = has_prev(p, b)
                    col = n * P if p == 2 else 2 * n * P + (0 if back else P)
                    w = 2 * P if back else P
                    y = pr[:, x % 4, col:col + w]
                    mm = act.activation(y, y, ACT.Exp, bias=nm[:, par, p, b:b + 1], accum_out=ll[:, par, p, b:b + 1])
                mm.then_inc(exp_ok, 1)

            def split_high(i, x):
                _, p, blocks = step(x)
                wait(pv, S * i + x + 1)
                wait(turned, S * i + x + 1 + 4)
                act.activation(used(wth[:, x % 2], p, blocks), used(tb[x % 2][:], p, blocks), ACT.Copy).then_inc(high, 1)

            def read_out(i, x):
                par, p, blocks = step(x)
                og, b0 = o_group(x), blocks[0] // 8 * 8
                wait(pv, S * i + x + 1 + 2)
                wait(o_out[p], 16 * NOUT[p] * i)
                act.activation(on[:, p, b0:b0 + 8, 64 * par:64 * par + 64],
                               ob[og % 2][:].rearrange("p (b e) -> p b e", b=8), ACT.Copy).then_inc(o_ok, 1)

            ends = {x for x in range(S) if x == S - 1 or o_group(x + 1) != o_group(x)}
            with act.Fori(0, PAIRS) as i:
                for x in range(S + 4):
                    if x - 4 in ends:
                        read_out(i, x - 4)
                    if 1 <= x < S + 1:
                        expo(i, x - 1)
                    if 2 <= x < S + 2:
                        split_high(i, x - 2)
W_OLD = 3
W_NEW = 4
QC = 8


def attend_sample(nc, t):
    with Stage(nc, "sa") as s:
        TILES = {"a": PAGES, "b": W_OLD + W_NEW}
        kc = {"a": s.sb("kca", [P, 2, TILES["a"], 512]), "b": s.sb("kcb", [P, 2, TILES["b"], 512])}
        vc = {"a": s.sb("vca", [P, 2, TILES["a"], 512]), "b": s.sb("vcb", [P, 1, TILES["b"], 512])}
        vn = {k: s.sb("vn" + k, [DEC_T, 2, 512]) for k in "ab"}
        kT = s.sb("kT", [P, 2, 512])
        qs = s.sb("qs", [P, 2, DC, NS])
        qd = s.sb("qd", [P, 2, 4, QC])
        kn = s.sb("kn", [P, 2, 4, DEC_T])
        bias = {k: s.sb("bias" + k, [P, TILES[k] + 1, 32]) for k in "ab"}
        count = s.sb("count", [P, TILES["b"] + 1, 32])
        sb_ = {k: s.sb("s" + k, [P, TILES[k] + 1, 32]) for k in "ab"}
        pb = {k: s.sb("p" + k, [P, TILES[k] + 1, 32]) for k in "ab"}
        mx, rs, li = (s.sb(n, [P, 32]) for n in ("mx", "rs", "li"))
        mrow = s.sb("mrow", [32, 1])
        dg = s.sb("dg", [32, 32])
        od = s.sb("od", [P, 4, QC])
        oT = s.sb("oT", [P, DC, NS])
        nlam = s.sb("nlam", [P, 1])
        ident = s.sb("ident", [P, P])
        ones = s.sb("ones", [P, P])
        rows = s.sb("rows", [NS, DC, P])
        ptab = s.sb("ptab", [1, DEC_B * PAGES], I32)
        tb = [s.ps(f"tb{i}") for i in range(2)]
        sc = [s.ps(f"sc{i}") for i in range(2)]
        scn, misc, den, ob = s.ps("scn"), s.ps("misc"), s.ps("den"), s.ps("ob")
        const_in, tab_in, zeroed = s.sem("const_in"), s.sem("tab_in"), s.sem("zeroed")
        k_in = {k: [s.sem(f"k_in{k}{i}") for i in range(2)] for k in "ab"}
        v_in = {k: [s.sem(f"v_in{k}{i}") for i in range(2)] for k in "ab"}
        kt_ok = [s.sem(f"kt_ok{i}") for i in range(2)]
        rows_out = s.sem("rows_out")
        (k_turned, k_used, q_ok, scored, s_read, max_part, max_turned, max_row, dg_ok, max_all, shifted, exp_ok,
         weighed, sum_ok, den_ok, li_ok, pv, o_div, o_ok, fin_t, fin_r) = (s.sem(n) for n in (
             "k_turned", "k_used", "q_ok", "scored", "s_read", "max_part", "max_turned", "max_row", "dg_ok",
             "max_all", "shifted", "exp_ok", "weighed", "sum_ok", "den_ok", "li_ok", "pv", "o_div", "o_ok",
             "fin_t", "fin_r"))
        block = s.block()
        N = DEC_B // 2
        PASSES = [("a", 0), ("b", 0), ("a", 1), ("b", 1)]
        NP_ = len(PASSES)
        tile = {}
        for x, (k, _) in enumerate(PASSES):
            for n in range(TILES[k]):
                tile[x, n] = len(tile)
        NTL = len(tile)
        K_DMAS = {"a": PAGES, "b": 5}
        V_DMAS = {"a": PAGES + 1, "b": 6}
        TURN_MAX, SPREAD_MAX, EXPO, SUMS = 1, 3, 4, 5

        def at(x):
            if x == NP_:
                return [None] * (SUMS + 1)
            return list(range(TILES[PASSES[x][0]]))

        @block.sync
        def _(sp):
            wait = Waiter(sp, s.sem("passed_sp"))
            sp.dma_start(ptab[:], t["page_table"]).then_inc(tab_in, 16)
            sp.dma_start(ident[:], t["c_ident"]).then_inc(const_in, 16)
            for i in range(2):
                sp.dma_start(qs[:, i], t["s_feat"][i].rearrange("c p n -> p c n")).then_inc(const_in, 16)
            for k in "ab":
                sp.dma_start(bias[k][:], t["c_bias_d" + k]).then_inc(const_in, 16)
            sp.dma_start(count[:], t["c_count"]).then_inc(const_in, 16)
            sp.dma_start(nlam[:], t["nlam"]).then_inc(const_in, 16)
            sp.wait_ge(tab_in, 16)

            def load_pages(cache, dst, seq, sem_):
                for n in range(PAGES):
                    page = sp.value_load(ptab[0:1, ds(seq * PAGES + n, 1)], min_val=0, max_val=t["n_phys"] - 1)
                    sp.dma_start(dst[:, n], cache[ds(page, 1)][0]).then_inc(sem_, 16)

            def load_window(cache, dst, seq, sem_):
                win = cache[ds(seq, 1)][0]
                old = win[0:PAST - 512].rearrange("(n g r) e -> r g n e", n=W_OLD, r=16)
                for r in range(4):
                    sp.dma_start(dst[32 * r:32 * r + 32, 0:W_OLD], old[r]).then_inc(sem_, 16)
                sp.dma_start(dst[:, W_OLD:], win[PAST - 512:].rearrange("(n p) e -> p n e", p=P)).then_inc(sem_, 16)

            def load_k(k, par, seq):
                (load_pages if k == "a" else load_window)(t["cache_k"][k], kc[k][:, par], seq, k_in[k][par])

            def load_v(k, par, seq):
                (load_pages if k == "a" else load_window)(t["cache_v"][k], vc[k][:, par % (2 if k == "a" else 1)],
                                                          seq, v_in[k][par])
                new = t["s_rows"][1 if k == "a" else 3][ds(seq * DEC_T, DEC_T)]
                sp.dma_start(vn[k][:, par], new).then_inc(v_in[k][par], 16)

            load_k("a", 0, 0)
            load_k("b", 0, 0)
            load_v("a", 0, 0)
            load_k("a", 1, 1)
            load_v("b", 0, 0)
            load_k("b", 1, 1)
            load_v("a", 1, 1)

            def refill(i, last):
                if not last:
                    wait.apart(scored, NP_ * i + 1)
                    load_k("a", 0, 2 * i + 2)
                    wait.apart(scored, NP_ * i + 2)
                    load_k("b", 0, 2 * i + 2)
                    wait.apart(pv, NP_ * i + 1)
                    load_v("a", 0, 2 * i + 2)
                wait.apart(pv, NP_ * i + 2)
                load_v("b", 1, 2 * i + 1)
                if not last:
                    wait.apart(scored, NP_ * i + 3)
                    load_k("a", 1, 2 * i + 3)
                    wait.apart(pv, NP_ * i + 3)
                    load_v("a", 1, 2 * i + 3)
                    wait.apart(scored, NP_ * i + 4)
                    load_k("b", 1, 2 * i + 3)
                    wait.apart(pv, NP_ * i + 4)
                    load_v("b", 0, 2 * i + 2)

            with sp.Fori(0, N - 1) as i:
                refill(i, False)
            refill(N - 1, True)
            sp.wait_ge(fin_r, 2)
            sp.dma_start(t["s_mix"].rearrange("n (c x) -> n c x", c=DC), rows[:]).then_inc(rows_out, 16)
            sp.wait_ge(rows_out, 16)

        @block.gpsimd
        def _(pool):
            pool.memset(ones[:], 1.0).then_inc(zeroed, 1)
            pool.memset(qd[:], 0.0).then_inc(zeroed, 1)
            for k in "ab":
                pool.memset(sb_[k][:, TILES[k]], MASKED).then_inc(zeroed, 1)

        @block.tensor
        def _(pe):
            wait = Waiter(pe, s.sem("passed_pe"))
            pe.sem_inc(k_used, 2)
            pe.wait_ge(const_in, 16 * 7)
            pe.wait_ge(zeroed, 4)

            def turn_k(i, x, n):
                k, par = PASSES[x]
                y = tile[x, n]
                if n == 0:
                    wait(k_in[k][par], 16 * K_DMAS[k] * (i + 1))
                wait(kt_ok[y % 2], NTL // 2 * i + y // 2)
                for j in range(4):
                    mm = pe.transpose(tb[y % 2][:, j * P:(j + 1) * P], kc[k][:, par, n, j * P:(j + 1) * P], ident[:])
                mm.then_inc(k_turned, 1)

            def score(i, x, n):
                k, par = PASSES[x]
                y = tile[x, n]
                if n == 0:
                    wait(q_ok, NP_ * i + x + 1)
                    wait(s_read, NP_ * i + x + 1)
                wait(kt_ok[y % 2], NTL // 2 * i + y // 2 + 1)
                for j in range(4):
                    mm = pe.matmul(sc[x % 2][:, 32 * n + QC * j:32 * n + QC * j + QC], kT[:, y % 2, j * P:(j + 1) * P],
                                   qd[:, x % 2, j], start=True, stop=True)
                mm.then_inc(k_used, 1)

            def score_new(i, x):
                wait(s_read, NP_ * i + x + 2)
                for j in range(4):
                    mm = pe.matmul(scn[0:DEC_T, QC * j:QC * j + QC], kn[:, x % 2, j], qd[:, x % 2, j],
                                   start=True, stop=True)
                mm.then_inc(scored, 1)

            def turn_max(i, x):
                wait(max_part, NP_ * i + x + 1)
                pe.transpose(misc[0:32, 0:P], mx[:], ident[:]).then_inc(max_turned, 1)

            def spread_max(i, x):
                wait(dg_ok, NP_ * i + x + 1)
                pe.matmul(misc[:, 0:32], ones[0:32, :], dg[:], start=True, stop=True).then_inc(max_all, 1)

            def sums(i, x):
                wait(sum_ok, NP_ * i + x + 1)
                pe.matmul(den[:, 0:32], ones[:], rs[:], start=True, stop=True).then_inc(den_ok, 1)

            def weigh(i, x):
                k, par = PASSES[x]
                wait(v_in[k][par], 16 * V_DMAS[k] * (i + 1))
                if x == 0:
                    wait(o_div, NP_ * i)
                else:
                    wait(o_div, NP_ * i + x)
                for j in range(4):
                    for n in range(TILES[k]):
                        pe.matmul(ob[:, QC * j:QC * j + QC], vc[k][:, par if k == "a" else 0, n, j * P:(j + 1) * P],
                                  pb[k][:, n, QC * j:QC * j + QC], start=n == 0, stop=False)
                    mm = pe.matmul(ob[:, QC * j:QC * j + QC], vn[k][:, par, j * P:(j + 1) * P],
                                   pb[k][0:DEC_T, TILES[k], QC * j:QC * j + QC], start=False, stop=True)
                mm.then_inc(pv, 1)

            with pe.Fori(0, N) as i:
                for x in range(NP_ + 1):
                    if x < NP_:
                        turn_k(i, x, 0)
                    for m, n in enumerate(at(x)):
                        if n is not None:
                            if n + 1 < len(at(x)):
                                turn_k(i, x, n + 1)
                            score(i, x, n)
                        if x > 0:
                            if m == TURN_MAX:
                                turn_max(i, x - 1)
                            if m == SPREAD_MAX:
                                spread_max(i, x - 1)
                            if m == SUMS:
                                sums(i, x - 1)
                    if x < NP_:
                        score_new(i, x)
                    if x > 0:
                        weigh(i, x - 1)
            pe.wait_ge(o_ok, DEC_B * 2)
            for half in range(2):
                for c in range(4):
                    mm = pe.transpose(tb[half][0:NS, c * P:(c + 1) * P], oT[:, 4 * half + c], ident[:])
                mm.then_inc(fin_t, 1)

        @block.vector
        def _(dve):
            wait = Waiter(dve, s.sem("passed_dve"))
            dve.sem_inc(s_read, 2)
            dve.wait_ge(const_in, 16 * 7)
            dve.wait_ge(zeroed, 4)

            def lay_queries(i, x):
                k, par = PASSES[x]
                f, tok = (0 if k == "a" else 4), ds((2 * i + par) * DEC_T, DEC_T)
                back = NP_ * i + x - 1
                if x >= 2:
                    wait.apart(scored, back)
                else:
                    wait.apart(scored, NP_ * i)
                for m in range(2):
                    dve.tensor_copy(qd[64 * m:64 * m + 64, x % 2, :, 4 * m:4 * m + 4], qs[64 * m:64 * m + 64, 0, f:f + 4, tok])
                dve.tensor_copy(kn[:, x % 2], qs[:, 1, f:f + 4, tok]).then_inc(q_ok, 1)

            def read_k(i, x, n):
                y = tile[x, n]
                if y % 2:
                    wait(k_used, NTL * i + y + 1)
                    wait(k_turned, NTL * i + y + 1)
                    dve.tensor_copy(kT[:, 1], tb[1][:]).then_inc(kt_ok[1], 1)

            def part_max(i, x):
                k = PASSES[x][0]
                T = TILES[k]
                wait(scored, NP_ * i + x + 1)
                dve.tensor_tensor(sb_[k][:, 0:T], sc[x % 2][:, 0:32 * T].rearrange("p (n c) -> p n c", c=32),
                                  bias[k][:, 0:T], ALU.add)
                dve.tensor_tensor(sb_[k][0:DEC_T, T], scn[0:DEC_T, 0:32], bias[k][0:DEC_T, T], ALU.add).then_inc(s_read, 1)
                wait(s_read, NP_ * i + x + 1 + 2)
                dve.tensor_reduce(mx[:], sb_[k][:].rearrange("p n c -> p c n"), AX.X, ALU.max).then_inc(max_part, 1)

            def row_max(i, x):
                wait(max_turned, NP_ * i + x + 1)
                dve.tensor_reduce(mrow[:], misc[0:32, 0:P], AX.X, ALU.max).then_inc(max_row, 1)
                wait(max_row, NP_ * i + x + 1)
                dve.tensor_scalar(dg[:], ident[0:32, 0:32], mrow[:], None, ALU.mult).then_inc(dg_ok, 1)

            def shift(i, x):
                k = PASSES[x][0]
                wait(max_all, NP_ * i + x + 1)
                dve.tensor_tensor(sb_[k][:], sb_[k][:],
                                  misc[:, 0:32].rearrange("p (o c) -> p o c", o=1).to_broadcast([P, TILES[k] + 1, 32]),
                                  ALU.subtract).then_inc(shifted, 1)

            def sum_tiles(i, x):
                k = PASSES[x][0]
                wait(exp_ok, NP_ * i + x + 1)
                if k == "b":
                    dve.tensor_tensor(pb[k][:], pb[k][:], count[:], ALU.mult).then_inc(weighed, 1)
                    wait(weighed, NP_ // 2 * i + x // 2 + 1)
                dve.tensor_reduce(rs[:], pb[k][:].rearrange("p n c -> p c n"), AX.X, ALU.add).then_inc(sum_ok, 1)

            def invert(i, x):
                wait(den_ok, NP_ * i + x + 1)
                dve.reciprocal(li[:], den[:, 0:32]).then_inc(li_ok, 1)

            def result(i, x):
                k, par = PASSES[x]
                tok = ds((2 * i + par) * DEC_T, DEC_T)
                wait(pv, NP_ * i + x + 1)
                wait(li_ok, NP_ * i + x + 1)
                dve.tensor_tensor(od[:], ob[:, 0:32].rearrange("p (j c) -> p j c", c=QC),
                                  li[:].rearrange("p (j c) -> p j c", c=QC), ALU.mult).then_inc(o_div, 1)
                wait(o_div, NP_ * i + x + 1)
                if k == "a":
                    dve.scalar_tensor_tensor(oT[:, 0:4, tok], od[:, :, 4:8], nlam[:], od[:, :, 0:4],
                                             ALU.mult, ALU.add).then_inc(o_ok, 1)
                else:
                    dve.tensor_copy(oT[0:64, 4:8, tok], od[0:64, :, 0:4])
                    dve.tensor_copy(oT[64:P, 4:8, tok], od[64:P, :, 4:8]).then_inc(o_ok, 1)

            with dve.Fori(0, N) as i:
                lay_queries(i, 0)
                for x in range(NP_ + 1):
                    if x > 0:
                        part_max(i, x - 1)
                    for m, n in enumerate(at(x)):
                        if n is not None:
                            read_k(i, x, n)
                        if x > 0:
                            if m == TURN_MAX:
                                row_max(i, x - 1)
                            if m == SPREAD_MAX:
                                shift(i, x - 1)
                            if m == SUMS:
                                sum_tiles(i, x - 1)
                                invert(i, x - 1)
                    if x + 1 < NP_:
                        lay_queries(i, x + 1)
                    if x > 0:
                        result(i, x - 1)
            for half in range(2):
                dve.wait_ge(fin_t, half + 1)
                dve.tensor_copy(rows[:, 4 * half:4 * half + 4],
                                tb[half][0:NS, :].rearrange("p (c x) -> p c x", c=4)).then_inc(fin_r, 1)

        @block.scalar
        def _(act):
            wait = Waiter(act, s.sem("passed_act"))

            def read_k(i, x, n):
                y = tile[x, n]
                if y % 2 == 0:
                    wait(k_used, NTL * i + y + 1)
                    wait(k_turned, NTL * i + y + 1)
                    act.activation(kT[:, 0], tb[0][:], ACT.Copy).then_inc(kt_ok[0], 1)

            def expo(i, x):
                k = PASSES[x][0]
                wait(shifted, NP_ * i + x + 1)
                act.activation(pb[k][:], sb_[k][:], ACT.Exp).then_inc(exp_ok, 1)

            with act.Fori(0, N) as i:
                for x in range(NP_ + 1):
                    for m, n in enumerate(at(x)):
                        if n is not None:
                            read_k(i, x, n)
                        if x > 0 and m == EXPO:
                            expo(i, x - 1)
def mix(nc, t):
    with Stage(nc, "mx") as s:
        wr = s.sb("wr", [P, 2, D])
        wh = s.sb("wh", [P, DC, D], F32R)
        wl = s.sb("wl", [P, DC, D], F32R)
        st = s.sb("st", [P, NPAT, NT, 2 * B_HEADS])
        wg = s.sb("wg", [P, NPAT, NT, B_HEADS])
        wt = s.sb("wt", [P, NPAT, NT, B_HEADS])
        mm_ = s.sb("mm", [P, NT, B_HEADS])
        dn = s.sb("dn", [P, NT, B_HEADS])
        ob = s.sb("ob", [P, 2, NPAT, 512])
        cm = s.sb("cm", [P, 2, D])
        sq = s.sb("sq", [P, D])
        ss = s.sb("ss", [P, 2, 12])
        sd = s.sb("sd", [P, 2, 12])
        rs = s.sb("rs", [P, 2, 12])
        gmix = s.sb("gmix", [P, D])
        gpost = s.sb("gpost", [P, D])
        gffn = s.sb("gffn", [P, D])
        mTh = s.sb("mTh", [P, 2, DC, P], F32R)
        mTl = s.sb("mTl", [P, 2, DC, P], F32R)
        xt = s.sb("xt", [P, 2, D])
        zn = s.sb("zn", [P, D])
        x1 = s.sb("x1", [P, 2, D])
        h2 = s.sb("h2", [P, 2, D])
        hh = s.sb("hh", [P, 2, DC, P], F32R)
        hl = s.sb("hl", [P, 2, DC, P], F32R)
        zs = s.sb("zs", [P, 2, 2])
        z1 = s.sb("z1", [P, 8])
        eps = s.sb("eps", [P, 1])
        ident = s.sb("ident", [P, P])
        t1 = [s.ps(f"t1{i}") for i in range(2)]
        t2 = [s.ps(f"t2{i}") for i in range(2)]
        zb = [[s.ps(f"z{k}{h}") for h in range(2)] for k in range(2)]
        const_in, st_in, w_hi, w_lo, prep = (s.sem(n) for n in ("const_in", "st_in", "w_hi", "w_lo", "prep"))
        w_in = [s.sem(f"w_in{i}") for i in range(2)]
        mix_in = [s.sem(f"mix_in{i}") for i in range(2)]
        x_in = [s.sem(f"x_in{i}") for i in range(2)]
        x1_out = [s.sem(f"x1_out{i}") for i in range(2)]
        h_out = [s.sem(f"h_out{i}") for i in range(2)]
        (b_part, b_rest, b_sum, squared, ss_ok, sd_ok, rs_ok, scaled, mixed, turned, high, low, mul, z_sq, z_ss, z_sd,
         z_rs, z_ok, x1_ok, x_sq, x_sd, x_rs, h_ok, turned2, high2, low2) = (s.sem(n) for n in (
             "b_part", "b_rest", "b_sum", "squared", "ss_ok", "sd_ok", "rs_ok", "scaled", "mixed", "turned", "high",
             "low", "mul", "z_sq", "z_ss", "z_sd", "z_rs", "z_ok", "x1_ok", "x_sq", "x_sd", "x_rs", "h_ok",
             "turned2", "high2", "low2"))
        b_part2 = s.sem("b_part2")
        block = s.block()
        LASTT = NT

        def pipeline(eng, slot):
            for n in (-1, 0, 1):
                slot(n, n % 2)
            with eng.Fori(1, NT // 2 - 1) as i:
                for k in range(2):
                    slot(2 * i + k, k)
            for n in range(NT - 2, LASTT + 3):
                slot(n, n % 2)

        def some(n):
            return not isinstance(n, int) or 0 <= n <= LASTT

        def rows_of(n):
            return NS if isinstance(n, int) and n == LASTT else P

        @block.sync
        def _(sp):
            wait = Waiter(sp, s.sem("passed_sp"))
            for p in range(NPAT):
                sp.dma_start(st[:, p], t["stats"][p].rearrange("(b p) c -> p b c", p=P)).then_inc(st_in, 16)
            sp.dma_start(ident[:], t["c_ident"]).then_inc(const_in, 16)
            for h in range(A_HEADS):
                sp.dma_start(gmix[:, h * P:(h + 1) * P], t["subln_a"].partition_broadcast(P)).then_inc(const_in, 16)
            for h in range(B_HEADS):
                sp.dma_start(gmix[:, 512 + 64 * h:512 + 64 * h + 64],
                             t["norm_b_out"].partition_broadcast(P)).then_inc(const_in, 16)
            sp.dma_start(gpost[:], t["norm_mix_post"].partition_broadcast(P)).then_inc(const_in, 16)
            sp.dma_start(gffn[:], t["norm_ffn_pre"].partition_broadcast(P)).then_inc(const_in, 16)

            def load_mix(n, k):
                if isinstance(n, int) and n == LASTT:
                    sp.dma_start(cm[0:NS, k], t["s_mix"]).then_inc(mix_in[k], 16)
                    return
                rows = ds(n * P, P)
                sp.dma_start(cm[:, k, 0:512], t["oa"][rows, :]).then_inc(mix_in[k], 16)
                for p in range(NPAT):
                    sp.dma_start(ob[:, k, p], t["ob"][p][rows, :]).then_inc(mix_in[k], 16)

            def load_x(n, k):
                if isinstance(n, int) and n == LASTT:
                    sp.dma_start(xt[0:NS, k], t["x_sample"]).then_inc(x_in[k], 16)
                else:
                    sp.dma_start(xt[:, k], t["x_prompt"][ds(n * P, P), :]).then_inc(x_in[k], 16)

            load_mix(0, 0)
            for c in range(2):
                sp.dma_start(wr[:, c], t["w_out"][c * P:(c + 1) * P, :]).then_inc(w_in[c], 16)
            load_mix(1, 1)
            load_x(0, 0)
            load_x(1, 1)
            for c in range(2, DC):
                sp.wait_ge(w_lo, c - 1)
                sp.dma_start(wr[:, c % 2], t["w_out"][c * P:(c + 1) * P, :]).then_inc(w_in[c % 2], 16)

            def slot(n, k):
                if some(n) and (not isinstance(n, int) or n + 2 <= LASTT):
                    wait.apart(turned, 2 * n + 2)
                    load_mix(n + 2, k)
                m, km = n - 1, 1 - k
                if some(m):
                    wait.apart(x1_ok, m + 1)
                    r = rows_of(m)
                    at = slice(SEQ, TOK) if r == NS else ds(m * P, P)
                    sp.dma_start(t["x1"][at, :], x1[0:r, km]).then_inc(x1_out[km], 16)
                    if not isinstance(m, int) or m + 2 <= LASTT:
                        load_x(m + 2, km)
                m = n - 2
                if some(m):
                    wait.apart(low2, 2 * m + 2 + 2)
                    r = rows_of(m)
                    at = slice(SEQ, TOK) if r == NS else ds(m * P, P)
                    for part, src in enumerate((hh, hl)):
                        sp.dma_start(t["h2T"][part][:, :, at], src[:, k, :, 0:r].bitcast(F32)).then_inc(h_out[k], 16)

            pipeline(sp, slot)
            for k in range(2):
                sp.wait_ge(x1_out[k], 16 * (9 - k))
                sp.wait_ge(h_out[k], 32 * (9 - k))

        def seen(n, k, each):
            if isinstance(n, int):
                return each * ((n - k) // 2 + 1)
            return each // 2 * (n - k) + each

        @block.gpsimd
        def _(pool):
            wait = Waiter(pool, s.sem("passed_pool"))
            for c in range(DC):
                pool.wait_ge(w_hi, c + 1)
                pool.tensor_tensor(wl[:, c], wr[:, c % 2], wh[:, c].bitcast(F32), ALU.subtract).then_inc(w_lo, 1)
            pool.wait_ge(prep, 9)

            def slot(n, k):
                m, km = n + 1, 1 - k
                if some(m):
                    r = rows_of(m)
                    if r == P:
                        wait(mix_in[km], seen(m, km, 64))
                        for p in (1, 2):
                            o = ob[:, km, p].rearrange("p (h e) -> p h e", h=B_HEADS)
                            last = pool.tensor_tensor(o, o, wg[:, p, ds(m, 1), :].rearrange("p o h -> p (o h)")
                                                      .rearrange("p (h o) -> p h o", o=1).to_broadcast([P, B_HEADS, 64]),
                                                      ALU.mult)
                        last.then_inc(b_part, 1)
                        wait(b_part, m + 1)
                        pool.tensor_tensor(ob[:, km, 1], ob[:, km, 1], ob[:, km, 2], ALU.add).then_inc(b_rest, 1)
                    wait(scaled, m + 1)
                    pool.tensor_tensor(cm[0:r, km], cm[0:r, km], gmix[0:r], ALU.mult).then_inc(mixed, 1)
                m = n - 1
                if some(m):
                    r = rows_of(m)
                    wait(z_ok, m + 1)
                    wait(x_in[km], seen(m, km, 16))
                    if not isinstance(m, int) or m >= 2:
                        wait(x1_out[km], seen(m - 2, km, 16))
                    pool.tensor_tensor(x1[0:r, km], zn[0:r], xt[0:r, km], ALU.add).then_inc(x1_ok, 1)

            pipeline(pool, slot)

        @block.scalar
        def _(act):
            wait = Waiter(act, s.sem("passed_act"))
            act.wait_ge(prep, 4)
            act.activation(wt[:], wt[:], ACT.Exp).then_inc(prep, 1)
            for c in range(DC):
                act.wait_ge(w_in[c % 2], 16 * (c // 2 + 1))
                act.activation(wh[:, c], wr[:, c % 2], ACT.Copy).then_inc(w_hi, 1)

            def slot(n, k):
                if some(n):
                    r = rows_of(n)
                    if not isinstance(n, int) or n >= 2:
                        wait(mul, n - 1)
                    for half in range(2):
                        wait(turned, 2 * n + half + 1)
                        act.activation(mTh[:, k, 4 * half:4 * half + 4, 0:r],
                                       t1[half][:].rearrange("p (c x) -> p c x", c=4)[:, :, 0:r],
                                       ACT.Copy).then_inc(high, 1)
                m, km = n + 1, 1 - k
                if some(m):
                    r = rows_of(m)
                    wait(b_sum, m + 1)
                    if r == NS:
                        wait(mix_in[km], 64 * 8 + 16)
                    act.activation(sq[0:r], cm[0:r, km], ACT.Square).then_inc(squared, 1)
                    wait(ss_ok, m + 1)
                    act.activation(sd[0:r, km, 0:4], ss[0:r, km, 0:4], ACT.Sqrt, scale=1.0 / P, bias=eps[0:r])
                    act.activation(sd[0:r, km, 4:12], ss[0:r, km, 4:12], ACT.Sqrt, scale=1.0 / 64,
                                   bias=eps[0:r]).then_inc(sd_ok, 1)
                m = n - 1
                if some(m):
                    r = rows_of(m)
                    wait(mul, m + 1)
                    for half in range(2):
                        last = act.activation(sq[0:r, 512 * half:512 * half + 512], zb[km][half][0:r, :], ACT.Square,
                                              accum_out=zs[0:r, km, half:half + 1])
                    last.then_inc(z_sq, 1)
                    wait(z_ss, m + 1)
                    act.activation(z1[0:r, 1:2], z1[0:r, 0:1], ACT.Sqrt, scale=1.0 / D, bias=eps[0:r]).then_inc(z_sd, 1)
                    wait(x1_ok, m + 1)
                    act.activation(sq[0:r], x1[0:r, km], ACT.Square, accum_out=z1[0:r, 3:4]).then_inc(x_sq, 1)
                    wait(x_sq, m + 1)
                    act.activation(z1[0:r, 4:5], z1[0:r, 3:4], ACT.Sqrt, scale=1.0 / D, bias=eps[0:r]).then_inc(x_sd, 1)
                m = n - 2
                if some(m):
                    r = rows_of(m)
                    if not isinstance(m, int) or m >= 2:
                        wait(h_out[k], seen(m - 2, k, 32))
                    for half in range(2):
                        wait(turned2, 2 * m + half + 1)
                        act.activation(hh[:, k, 4 * half:4 * half + 4, 0:r],
                                       t2[half][:].rearrange("p (c x) -> p c x", c=4)[:, :, 0:r],
                                       ACT.Copy).then_inc(high2, 1)

            pipeline(act, slot)

        @block.vector
        def _(dve):
            wait = Waiter(dve, s.sem("passed_dve"))
            dve.sem_inc(low, 2)
            dve.sem_inc(low2, 2)
            dve.memset(eps[:], EPS).then_inc(prep, 1)
            st5 = st[:].rearrange("p n b (h k) -> p n b h k", k=2)
            m_, l_ = st5[:, :, :, :, 0], st5[:, :, :, :, 1]
            dve.wait_ge(st_in, 16 * NPAT)
            dve.tensor_tensor(mm_[:], m_[:, 0], m_[:, 1], ALU.max).then_inc(prep, 1)
            dve.wait_ge(prep, 2)
            dve.tensor_tensor(mm_[:], mm_[:], m_[:, 2], ALU.max).then_inc(prep, 1)
            dve.wait_ge(prep, 3)
            for p in range(NPAT):
                last = dve.tensor_tensor(wt[:, p], m_[:, p], mm_[:], ALU.subtract)
            last.then_inc(prep, 1)
            dve.wait_ge(prep, 5)
            for p in range(NPAT):
                last = dve.tensor_tensor(wg[:, p], wt[:, p], l_[:, p], ALU.mult)
            last.then_inc(prep, 1)
            dve.wait_ge(prep, 6)
            dve.tensor_reduce(dn[:], wg[:].rearrange("p n b h -> p b h n"), AX.X, ALU.add).then_inc(prep, 1)
            dve.wait_ge(prep, 7)
            dve.reciprocal(dn[:], dn[:]).then_inc(prep, 1)
            dve.wait_ge(prep, 8)
            for p in range(NPAT):
                last = dve.tensor_tensor(wg[:, p], wt[:, p], dn[:], ALU.mult)
            dve.wait_ge(const_in, 16 * (1 + A_HEADS + B_HEADS + 2))
            dve.tensor_scalar(gmix[:, 0:512], gmix[:, 0:512], 1.0 - LAM_INIT, None, ALU.mult).then_inc(prep, 1)
            dve.wait_ge(prep, 9)

            def slot(n, k):
                if some(n):
                    r = rows_of(n)
                    for half in range(2):
                        wait(high, 2 * n + half + 1)
                        dve.tensor_tensor(mTl[:, k, 4 * half:4 * half + 4, 0:r],
                                          t1[half][:].rearrange("p (c x) -> p c x", c=4)[:, :, 0:r],
                                          mTh[:, k, 4 * half:4 * half + 4, 0:r].bitcast(F32),
                                          ALU.subtract).then_inc(low, 1)
                m, km = n + 1, 1 - k
                if some(m):
                    r = rows_of(m)
                    if r == P:
                        wait(mix_in[km], seen(m, km, 64))
                        o = ob[:, km, 0].rearrange("p (h e) -> p h e", h=B_HEADS)
                        w = wg[:, 0, ds(m, 1), :].rearrange("p o h -> p (o h)").rearrange("p (h o) -> p h o", o=1)
                        dve.tensor_tensor(o, o, w.to_broadcast([P, B_HEADS, 64]), ALU.mult).then_inc(b_part2, 1)
                        wait(b_part2, m + 1)
                        wait(b_rest, m + 1)
                        dve.tensor_tensor(cm[:, km, 512:D], ob[:, km, 0], ob[:, km, 1], ALU.add).then_inc(b_sum, 1)
                    else:
                        dve.sem_inc(b_sum, 1)
                    wait(squared, m + 1)
                    dve.tensor_reduce(ss[0:r, km, 0:4], sq[0:r, 0:512].rearrange("p (h e) -> p h e", h=A_HEADS), AX.X, ALU.add)
                    dve.tensor_reduce(ss[0:r, km, 4:12], sq[0:r, 512:D].rearrange("p (h e) -> p h e", h=B_HEADS), AX.X,
                                      ALU.add).then_inc(ss_ok, 1)
                    wait(sd_ok, m + 1)
                    dve.reciprocal(rs[0:r, km], sd[0:r, km]).then_inc(rs_ok, 1)
                    wait(rs_ok, m + 1)
                    for c0, c1, heads, r0 in ((0, 512, A_HEADS, 0), (512, D, B_HEADS, 4)):
                        e = (c1 - c0) // heads
                        y = cm[0:r, km, c0:c1].rearrange("p (h e) -> p h e", h=heads)
                        last = dve.tensor_tensor(y, y, rs[0:r, km, r0:r0 + heads].rearrange("p (h o) -> p h o", o=1)
                                                 .to_broadcast([r, heads, e]), ALU.mult)
                    last.then_inc(scaled, 1)
                m = n - 1
                if some(m):
                    r = rows_of(m)
                    wait(z_sq, m + 1)
                    dve.tensor_tensor(z1[0:r, 0:1], zs[0:r, km, 0:1], zs[0:r, km, 1:2], ALU.add).then_inc(z_ss, 1)
                    wait(z_sd, m + 1)
                    dve.reciprocal(z1[0:r, 2:3], z1[0:r, 1:2]).then_inc(z_rs, 1)
                    wait(z_rs, m + 1)
                    if not isinstance(m, int) or m >= 1:
                        wait(x1_ok, m)
                    for half in range(2):
                        c = slice(512 * half, 512 * half + 512)
                        last = dve.scalar_tensor_tensor(zn[0:r, c], zb[km][half][0:r, :], z1[0:r, 2:3], gpost[0:r, c],
                                                        ALU.mult, ALU.mult)
                    last.then_inc(z_ok, 1)
                    wait(x_sd, m + 1)
                    dve.reciprocal(z1[0:r, 5:6], z1[0:r, 4:5]).then_inc(x_rs, 1)
                    wait(x_rs, m + 1)
                    if not isinstance(m, int) or m >= 2:
                        wait(turned2, 2 * m - 2)
                    dve.scalar_tensor_tensor(h2[0:r, km], x1[0:r, km], z1[0:r, 5:6], gffn[0:r],
                                             ALU.mult, ALU.mult).then_inc(h_ok, 1)
                m = n - 2
                if some(m):
                    r = rows_of(m)
                    for half in range(2):
                        wait(high2, 2 * m + half + 1)
                        dve.tensor_tensor(hl[:, k, 4 * half:4 * half + 4, 0:r],
                                          t2[half][:].rearrange("p (c x) -> p c x", c=4)[:, :, 0:r],
                                          hh[:, k, 4 * half:4 * half + 4, 0:r].bitcast(F32),
                                          ALU.subtract).then_inc(low2, 1)

            pipeline(dve, slot)

        @block.tensor
        def _(pe):
            wait = Waiter(pe, s.sem("passed_pe"))
            pe.wait_ge(const_in, 16 * (1 + A_HEADS + B_HEADS + 2))

            def turn(src, k, dst, r, done_, low_, n):
                for half in range(2):
                    wait(low_, 2 * n + half + 1)
                    for c in range(4):
                        cc = 4 * half + c
                        last = pe.transpose(dst[half][:, c * P:c * P + r], src[0:r, k, cc * P:(cc + 1) * P],
                                            ident[0:r, 0:r])
                    last.then_inc(done_, 1)

            def slot(n, k):
                km = 1 - k
                if some(n):
                    wait(mixed, n + 1)
                    turn(cm, k, t1, rows_of(n), turned, low, n)
                m = n - 1
                if some(m):
                    r = rows_of(m)
                    wait(low, 2 * m + 2 + 2)
                    if isinstance(m, int) and m == 0:
                        wait(w_lo, DC)
                    if not isinstance(m, int) or m >= 2:
                        wait(z_ok, m - 1)
                    for c in range(DC):
                        for x, (a, b) in enumerate(((mTh, wh), (mTh, wl), (mTl, wh))):
                            for half in range(2):
                                last = pe.matmul(zb[km][half][0:r, :], a[:, km, c, 0:r], b[:, c, 512 * half:512 * half + 512],
                                                 start=c == 0 and x == 0, stop=c == DC - 1 and x == 2)
                    last.then_inc(mul, 1)
                m = n - 2
                if some(m):
                    wait(h_ok, m + 1)
                    turn(h2, k, t2, rows_of(m), turned2, low2, m)

            pipeline(pe, slot)
TAPS = 3
HALF_F = FT // 2


def ffn(nc, t):
    with Stage(nc, "ff") as s:
        hh = s.sb("hh", [P, 2, DC, GRP], F32R)
        hs = s.sb("hs", [P, 2, DC, NS], F32R)
        wr = s.sb("wr", [P, 2, HALF_F, P])
        wh = s.sb("wh", [P, 2, HALF_F, P], F32R)
        wl = s.sb("wl", [P, 2, HALF_F, P], F32R)
        ah = s.sb("ah", [P, FT, GRP], F32R)
        al = s.sb("al", [P, FT, GRP], F32R)
        sh = s.sb("sh", [P, FT, NS], F32R)
        sl = s.sb("sl", [P, FT, NS], F32R)
        gb = s.sb("gb", [P, 2, GRP + 2])
        gs = s.sb("gs", [P, 2, DEC_B, DEC_T + 2])
        ca = s.sb("ca", [P, GRP])
        cb = s.sb("cb", [P, GRP])
        sa = s.sb("sa", [P, 2, NS])
        sb2 = s.sb("sb2", [P, 2, NS])
        carry = s.sb("carry", [P, FT, 2])
        tail = s.sb("tail", [P, FT, DEC_B, 2])
        cw = s.sb("cw", [P, TAPS + 1, FT])
        yT = s.sb("yT", [P, GRP])
        yTs = s.sb("yTs", [P, NS])
        yn = s.sb("yn", [P, TPG, D])
        ys = s.sb("ys", [NS, D])
        xt = s.sb("xt", [P, D])
        gain = s.sb("gain", [P, D])
        junk = s.sb("junk", [P, 512])
        s4 = s.sb("s4", [P, 5, 8])
        eps = s.sb("eps", [P, 1])
        ident = s.sb("ident", [P, P])
        gp = [s.ps(f"g{i}") for i in range(2)]
        up = [s.ps(f"u{i}") for i in range(2)]
        dp = [s.ps(f"d{i}") for i in range(2)]
        tp = [s.ps(f"t{i}") for i in range(2)]
        const_in, copied, prep, pre_t, pre_r = (s.sem(n) for n in ("const_in", "copied", "prep", "pre_t", "pre_r"))
        w_in = [s.sem(f"w_in{i}") for i in range(2)]
        h_in, hs_in = s.sem("h_in"), s.sem("hs_in")
        x_in = s.sem("x_in")
        y_out, last_out = s.sem("y_out"), s.sem("last_out")
        (w_hi, w_lo, mm, g_read, conv1, conv2, conv_ok, gelu_ok, a_ok, a_hi, a_lo, d_read, y_turned, y_ok, y_sq, y_sum,
         y_sd, y_rs, y_norm, y_add, gs_read, cs1, cs2, convs_ok, gelus_ok, as_ok, as_hi, as_lo, ds_read, fin_t, fin_r) = (
            s.sem(n) for n in (
                "w_hi", "w_lo", "mm", "g_read", "conv1", "conv2", "conv_ok", "gelu_ok", "a_ok", "a_hi", "a_lo",
                "d_read", "y_turned", "y_ok", "y_sq", "y_sum", "y_sd", "y_rs", "y_norm", "y_add", "gs_read", "cs1",
                "cs2", "convs_ok", "gelus_ok", "as_ok", "as_hi", "as_lo", "ds_read", "fin_t", "fin_r"))
        carried, carried_s, y_half = s.sem("carried"), s.sem("carried_s"), s.sem("y_half")
        block = s.block()
        UNITS = 2 * FT + 2 * DC
        wg_view = t["w_gate"].rearrange("(c p) f -> p c f", p=P)
        wu_view = t["w_up"].rearrange("(c p) f -> p c f", p=P)
        wd_view = t["w_down"].rearrange("(c p) f -> p c f", p=P)

        def chunks(u):
            return DC if u < 2 * FT else HALF_F

        def groups(eng, f_tile, d_tile, end):
            def group(g, last):
                with eng.Fori(0, HALF_F - 1) as i:
                    for k in range(2):
                        f_tile(g, 2 * i + k, k, DC, last)
                f_tile(g, FT - 2, 0, DC, last)
                f_tile(g, FT - 1, 1, HALF_F, last)
                with eng.Fori(0, DC // 2 - 1) as i:
                    for k in range(2):
                        d_tile(g, 2 * i + k, k, HALF_F, last)
                d_tile(g, DC - 2, 0, HALF_F, last)
                d_tile(g, DC - 1, 1, 0 if last else DC, last)
                end(g, last)

            with eng.Fori(0, NG - 1) as g:
                group(g, False)
            group(NG - 1, True)

        @block.sync
        def _(sp):
            wait = Waiter(sp, s.sem("passed_sp"))
            sp.sem_inc(w_lo, 2)
            sp.dma_start(ident[:], t["c_ident"]).then_inc(const_in, 16)
            sp.dma_start(junk[0:TAPS * FT, 0:P], t["w_conv"].rearrange("j (f p) -> (j f) p", p=P)).then_inc(const_in, 16)
            sp.dma_start(junk[TAPS * FT:(TAPS + 1) * FT, 0:P], t["b_conv"].rearrange("(f p) -> f p", p=P)).then_inc(const_in, 16)
            sp.dma_start(gain[:], t["norm_ffn_post"].partition_broadcast(P)).then_inc(const_in, 16)
            sp.dma_start(yn[0:2 * DEC_B].rearrange("p a d -> p (a d)")[:, 0:D_FF], t["state_conv"]).then_inc(const_in, 16)
            for part in range(2):
                sp.dma_start(hs[:, part].bitcast(F32), t["h2T"][part][:, :, SEQ:TOK]).then_inc(hs_in, 16)

            def load_w(n, k, src):
                wait.apart(w_lo, n + 1)
                sp.dma_start(wr[:, k, 0:src.shape[1]], src).then_inc(w_in[k], 16)

            def f_tile(g, f, k, after, last):
                n = UNITS * g + 2 * f
                load_w(n, 0, wg_view[:, :, ds(f * P, P)])
                load_w(n + 1, 1, wu_view[:, :, ds(f * P, P)])

            def d_tile(g, d, k, after, last):
                n = UNITS * g + 2 * FT + 2 * d
                for half in range(2):
                    load_w(n + half, half, wd_view[:, half * HALF_F:(half + 1) * HALF_F, ds(d * P, P)])

            def end(g, last):
                if not last:
                    wait.apart(mm, UNITS * g + 2 * FT)
                    for part in range(2):
                        sp.dma_start(hh[:, part].bitcast(F32), t["h2T"][part][:, :, ds((g + 1) * GRP, GRP)]).then_inc(h_in, 16)

            for part in range(2):
                sp.dma_start(hh[:, part].bitcast(F32), t["h2T"][part][:, :, 0:GRP]).then_inc(h_in, 16)
            groups(sp, f_tile, d_tile, end)
            sp.wait_ge(fin_r, (FT + 3) // 4)
            flat = yn[:].rearrange("p a d -> p (a d)")
            sp.dma_start(t["conv_prompt"], flat[0:2, 0:D_FF]).then_inc(last_out, 16)
            sp.dma_start(t["conv_sample"], flat[32:32 + 2 * DEC_B, 0:D_FF]).then_inc(last_out, 16)
            sp.wait_ge(last_out, 32)

        @block.gpsimd
        def _(pool):
            wait = Waiter(pool, s.sem("passed_pool"))
            pool.memset(carry[:], 0.0).then_inc(prep, 1)
            for kind in range(2):
                for b in range(DEC_B):
                    pool.dma_start(t["win_out"][kind][b][0:PAST - DEC_T], t["win_cache"][kind][b][DEC_T:]).then_inc(copied, 16)
                    pool.dma_start(t["win_out"][kind][b][PAST - DEC_T:],
                                   t["s_rows"][2 + kind][DEC_T * b:DEC_T * (b + 1)]).then_inc(copied, 16)
                pool.dma_start(t["a_out"][kind], t["s_rows"][kind]).then_inc(copied, 16)

            def weights_low(n, k, size):
                if size:
                    wait(w_hi, n + 1)
                    pool.tensor_tensor(wl[:, k, 0:size], wr[:, k, 0:size], wh[:, k, 0:size].bitcast(F32),
                                       ALU.subtract).then_inc(w_lo, 1)

            weights_low(0, 0, DC)

            def f_tile(g, f, k, after, last):
                n = UNITS * g + 2 * f
                weights_low(n + 1, 1, DC)
                weights_low(n + 2, 0, after)

            def d_tile(g, d, k, after, last):
                n = UNITS * g + 2 * FT + 2 * d
                weights_low(n + 1, 1, HALF_F)
                weights_low(n + 2, 0, after)

            def end(g, last):
                for b in range(TPG + last):
                    r = P if b < TPG else NS
                    y = yn[:, b] if b < TPG else ys[:]
                    n = TPG * g + b
                    at = ds(n * P, P) if b < TPG else slice(SEQ, TOK)
                    pool.dma_start(xt[0:r], t["x1"][at, :]).then_inc(x_in, 16)
                    wait(y_norm, n + 1)
                    wait(x_in, 16 * (n + 1))
                    pool.tensor_tensor(y, y, xt[0:r], ALU.add).then_inc(y_add, 1)
                    wait.apart(y_add, n + 1)
                    dst = t["y_prompt"][at, :] if b < TPG else t["y_sample"]
                    pool.dma_start(dst, y).then_inc(y_out, 16)

            groups(pool, f_tile, d_tile, end)
            pool.wait_ge(y_out, 16 * (NT + 1))
            pool.wait_ge(copied, 16 * (4 * DEC_B + 2))

        @block.tensor
        def _(pe):
            wait = Waiter(pe, s.sem("passed_pe"))
            pe.sem_inc(mm, 1)
            pe.wait_ge(const_in, 16 * 5)
            pe.transpose(tp[0][:, 0:(TAPS + 1) * FT], junk[0:(TAPS + 1) * FT, 0:P],
                         ident[0:(TAPS + 1) * FT, 0:(TAPS + 1) * FT]).then_inc(pre_t, 1)
            old = yn[0:2 * DEC_B].rearrange("p a d -> p (a d)")
            for f in range(FT):
                m = pe.transpose(tp[1][:, f * 16:f * 16 + 16], old[:, f * P:(f + 1) * P], ident[0:16, 0:16])
            m.then_inc(pre_t, 1)

            def products(n, k, dst, c0, size, src, dst_s, src_s, first, stop_, last):
                for c in range(size):
                    for x, (w, part) in enumerate(((wh, 0), (wh, 1), (wl, 0))):
                        a, b = first and c == 0 and x == 0, stop_ and c == size - 1 and x == 2
                        m = pe.matmul(dst[:], w[:, k, c], src[part][:, c0 + c], start=a, stop=b)
                        if last:
                            m = pe.matmul(dst_s[:, 0:NS], w[:, k, c], src_s[part][:, c0 + c], start=a, stop=b)
                m.then_inc(mm, 1)

            def f_tile(g, f, k, after, last):
                n = UNITS * g + 2 * f
                if not isinstance(f, int) or f == 0:
                    wait(h_in, 32 * (g + 1))
                if last:
                    wait(hs_in, 32)
                wait(w_lo, n + 1 + 2)
                wait(g_read, FT * g + f + 1)
                if last:
                    wait(gs_read, f + 1)
                    wait(y_ok, DC * g + 2)
                products(n, 0, gp[k], 0, DC, (hh[:, 0], hh[:, 1]), tp[0], (hs[:, 0], hs[:, 1]), True, True, last)
                wait(w_lo, n + 2 + 2)
                wait(a_ok, FT * g + f + 1)
                if last:
                    wait(as_ok, f + 1)
                products(n + 1, 1, up[k], 0, DC, (hh[:, 0], hh[:, 1]), tp[1], (hs[:, 0], hs[:, 1]), True, True, last)

            def d_tile(g, d, k, after, last):
                n = UNITS * g + 2 * FT + 2 * d
                wait(a_lo, FT * (g + 1))
                wait(d_read, DC * g + d + 1)
                if last:
                    wait(as_lo, FT)
                    wait(g_read, FT * (g + 1) + 2)
                    wait(ds_read, d + 1)
                for half in range(2):
                    wait(w_lo, n + half + 1 + 2)
                    products(n + half, half, dp[k], half * HALF_F, HALF_F, (ah, al), gp[k], (sh, sl), half == 0,
                             half == 1, last)
                wait(d_read, DC * g + d + 1 + 2)
                wait(y_ok, DC * g + d + 1)
                for b in range(TPG):
                    m = pe.transpose(tp[k][:, b * P:(b + 1) * P], yT[:, b * P:(b + 1) * P], ident[:])
                if last:
                    wait(ds_read, d + 1 + 2)
                    m = pe.transpose(up[k][0:NS, 0:P], yTs[:], ident[:])
                m.then_inc(y_turned, 1)

            groups(pe, f_tile, d_tile, lambda g, last: None)
            pe.wait_ge(y_ok, DC * NG + 2)
            pe.wait_ge(g_read, 2 + FT * NG)
            for f in range(FT):
                if f % 4 == 0 and f >= 8:
                    pe.wait_ge(fin_r, f // 4 - 1)
                bank = (gp, up)[f // 4 % 2][0]
                pe.transpose(bank[0:2, (f % 4) * P:(f % 4 + 1) * P], carry[:, f], ident[:])
                m = pe.transpose((gp, up)[f // 4 % 2][1][0:2 * DEC_B, (f % 4) * P:(f % 4 + 1) * P],
                                 tail[:, f].rearrange("p b j -> p (b j)"), ident[:])
                if f % 4 == 3 or f == FT - 1:
                    m.then_inc(fin_t, 1)

        @block.scalar
        def _(act):
            wait = Waiter(act, s.sem("passed_act"))
            act.sem_inc(g_read, 2)
            act.sem_inc(d_read, 2)
            act.sem_inc(gs_read, 1)
            act.sem_inc(ds_read, 2)

            def weights_high(n, k, size, seen):
                if size:
                    wait(w_in[k], seen)
                    wait(mm, n)
                    act.activation(wh[:, k, 0:size], wr[:, k, 0:size], ACT.Copy).then_inc(w_hi, 1)

            weights_high(0, 0, DC, 16)

            def f_tile(g, f, k, after, last):
                n, q = UNITS * g + 2 * f, FT * g + f
                pairs = UNITS // 2 * g + f
                weights_high(n + 1, 1, DC, 16 * (pairs + 1))
                wait(mm, n + 1 + 1)
                wait(conv_ok, q)
                act.activation(gb[:, k, 2:], gp[k][:], ACT.Copy).then_inc(g_read, 1)
                if last:
                    wait(convs_ok, f)
                    act.activation(gs[:, k, :, 2:], tp[0][:, 0:NS].rearrange("p (b j) -> p b j", b=DEC_B),
                                   ACT.Copy).then_inc(gs_read, 1)
                weights_high(n + 2, 0, after, 16 * (pairs + 2))
                wait(conv_ok, q + 1 + 1)
                act.activation(ca[:], ca[:], ACT.Gelu_apprx_tanh).then_inc(gelu_ok, 1)
                if last:
                    wait(convs_ok, f + 1 + 1)
                    act.activation(sa[:, k], sa[:, k], ACT.Gelu_apprx_tanh).then_inc(gelus_ok, 1)

            def d_tile(g, d, k, after, last):
                n, q = UNITS * g + 2 * FT + 2 * d, DC * g + d
                pairs = UNITS // 2 * g + FT + d
                weights_high(n + 1, 1, HALF_F, 16 * (pairs + 1))
                weights_high(n + 2, 0, after, 16 * (pairs + 2))
                wait(mm, n + 2 + 1)
                wait(y_turned, q)
                act.activation(yT[:], dp[k][:], ACT.Copy).then_inc(d_read, 1)
                if last:
                    act.activation(yTs[:], gp[k][:, 0:NS], ACT.Copy).then_inc(ds_read, 1)

            def end(g, last):
                wait(y_ok, DC * (g + 1) + 2)
                for b in range(TPG + last):
                    r = P if b < TPG else NS
                    y = yn[:, b] if b < TPG else ys[:]
                    n = TPG * g + b
                    if b > 0:
                        wait(y_sq, n)
                    else:
                        wait(y_norm, TPG * g)
                    for half in range(2):
                        if half:
                            wait(y_half, n + 1)
                        m = act.activation(junk[0:r], y[:, 512 * half:512 * half + 512], ACT.Square,
                                           accum_out=s4[0:r, b, half:half + 1])
                        m.then_inc(y_sq if half else y_half, 1)
                for b in range(TPG + last):
                    r = P if b < TPG else NS
                    n = TPG * g + b
                    wait(y_sum, n + 1)
                    act.activation(s4[0:r, b, 3:4], s4[0:r, b, 2:3], ACT.Sqrt, scale=1.0 / D, bias=eps[0:r]).then_inc(y_sd, 1)

            groups(act, f_tile, d_tile, end)

        @block.vector
        def _(dve):
            wait = Waiter(dve, s.sem("passed_dve"))
            dve.memset(eps[:], EPS)
            dve.sem_inc(conv_ok, 1)
            dve.sem_inc(convs_ok, 1)
            dve.sem_inc(a_ok, 2)
            dve.sem_inc(as_ok, 1)
            dve.sem_inc(y_ok, 2)
            dve.wait_ge(prep, 1)
            dve.wait_ge(pre_t, 1)
            dve.tensor_copy(cw[:], tp[0][:, 0:(TAPS + 1) * FT].rearrange("p (j f) -> p j f", f=FT)).then_inc(pre_r, 1)
            dve.wait_ge(pre_t, 2)
            dve.tensor_copy(tail[:], tp[1][:, 0:FT * 16].rearrange("p (f b j) -> p f b j", f=FT, b=DEC_B)).then_inc(pre_r, 1)
            dve.wait_ge(pre_r, 2)

            def tap(j, f):
                return cw[:, j, ds(f, 1)]

            def convolve(src, a, b, f, first, second, done_, q, w, c0):
                dve.tensor_scalar(a, src(0), tap(0, f), tap(TAPS, f), ALU.mult, ALU.add).then_inc(first, 1)
                wait(first, q + 1)
                dve.scalar_tensor_tensor(b, src(1), tap(1, f), a, ALU.mult, ALU.add).then_inc(second, 1)
                wait(second, q + 1)
                dve.scalar_tensor_tensor(a, src(2), tap(2, f), b, ALU.mult, ALU.add).then_inc(done_, 1)

            def f_tile(g, f, k, after, last):
                q = FT * g + f
                dve.tensor_copy(gb[:, k, 0:2], carry[:, ds(f, 1), :].rearrange("p o j -> p (o j)")).then_inc(carried, 1)
                wait(g_read, q + 1 + 2)
                wait(carried, 2 * q + 1)
                convolve(lambda j: gb[:, k, j:j + GRP], ca[:], cb[:], f, conv1, conv2, conv_ok, q, GRP, 0)
                dve.tensor_copy(carry[:, ds(f, 1), :].rearrange("p o j -> p (o j)"), gb[:, k, GRP:]).then_inc(carried, 1)
                if last:
                    shape = lambda x: x[:, k].rearrange("p (b j) -> p b j", b=DEC_B)
                    dve.tensor_copy(gs[:, k, :, 0:2], tail[:, ds(f, 1)].rearrange("p o b j -> p (o b) j")).then_inc(carried_s, 1)
                    wait(gs_read, f + 1 + 1)
                    wait(carried_s, 2 * f + 1)
                    convolve(lambda j: gs[:, k, :, j:j + DEC_T], shape(sa), shape(sb2), f, cs1, cs2, convs_ok, f, NS, 0)
                    dve.tensor_copy(tail[:, ds(f, 1)].rearrange("p o b j -> p (o b) j"), gs[:, k, :, DEC_T:]).then_inc(carried_s, 1)
                wait(mm, UNITS * g + 2 * f + 2 + 1)
                wait(gelu_ok, q + 1)
                dve.tensor_tensor(cb[:], ca[:], up[k][:], ALU.mult).then_inc(a_ok, 1)
                wait.apart(a_ok, q + 1 + 2)
                hi = ah[:, ds(f, 1), :].rearrange("p o x -> p (o x)")
                dve.tensor_copy(hi, cb[:]).then_inc(a_hi, 1)
                wait(a_hi, q + 1)
                dve.tensor_tensor(al[:, ds(f, 1), :].rearrange("p o x -> p (o x)"), cb[:], hi.bitcast(F32),
                                  ALU.subtract).then_inc(a_lo, 1)
                if last:
                    wait(gelus_ok, f + 1)
                    dve.tensor_tensor(sb2[:, k], sa[:, k], tp[1][:, 0:NS], ALU.mult).then_inc(as_ok, 1)
                    wait.apart(as_ok, f + 1 + 1)
                    hi = sh[:, ds(f, 1), :].rearrange("p o x -> p (o x)")
                    dve.tensor_copy(hi, sb2[:, k]).then_inc(as_hi, 1)
                    wait(as_hi, f + 1)
                    dve.tensor_tensor(sl[:, ds(f, 1), :].rearrange("p o x -> p (o x)"), sb2[:, k], hi.bitcast(F32),
                                      ALU.subtract).then_inc(as_lo, 1)

            def d_tile(g, d, k, after, last):
                q = DC * g + d
                wait(y_out, 64 * g)
                wait.apart(y_turned, q + 1)
                if last:
                    dve.tensor_copy(ys[:, ds(d * P, P)], up[k][0:NS, 0:P])
                dve.tensor_copy(yn[:, :, ds(d * P, P)], tp[k][:].rearrange("p (b x) -> p b x", b=TPG)).then_inc(y_ok, 1)

            def end(g, last):
                for b in range(TPG + last):
                    r = P if b < TPG else NS
                    n = TPG * g + b
                    wait(y_sq, n + 1)
                    dve.tensor_tensor(s4[0:r, b, 2:3], s4[0:r, b, 0:1], s4[0:r, b, 1:2], ALU.add).then_inc(y_sum, 1)
                for b in range(TPG + last):
                    r = P if b < TPG else NS
                    y = yn[:, b] if b < TPG else ys[:]
                    n = TPG * g + b
                    wait(y_sd, n + 1)
                    dve.reciprocal(s4[0:r, b, 4:5], s4[0:r, b, 3:4]).then_inc(y_rs, 1)
                    wait(y_rs, n + 1)
                    dve.scalar_tensor_tensor(y, y, s4[0:r, b, 4:5], gain[0:r], ALU.mult, ALU.mult).then_inc(y_norm, 1)

            groups(dve, f_tile, d_tile, end)
            for n in range((FT + 3) // 4):
                dve.wait_ge(fin_t, n + 1)
                w = min(4, FT - 4 * n) * P
                src = (gp, up)[n % 2]
                if n == 0:
                    dve.wait_ge(y_out, 16 * NT + 16)
                flat = yn[:].rearrange("p a d -> p (a d)")
                dve.tensor_copy(flat[0:2, 512 * n:512 * n + w], src[0][0:2, 0:w])
                dve.tensor_copy(flat[32:32 + 2 * DEC_B, 512 * n:512 * n + w], src[1][0:2 * DEC_B, 0:w]).then_inc(fin_r, 1)
def program(nc, a, out):
    (y_prompt, y_sample, a_k_prompt, a_v_prompt, a_k_sample, a_v_sample, win_k_prompt, win_v_prompt,
     win_k_sample, win_v_sample, conv_prompt, conv_sample) = out

    def rows(x):
        return x[0].rearrange("n s h e -> (n s) (h e)")

    def by_sequence(x):
        return x[0].rearrange("n s h e -> n s (h e)")

    def scratch(name, shape):
        return nc.dram_tensor(f"scratch_{name}", shape, F32).ap()

    t = {name: a[name][0] for name in (
        "norm_mix_pre", "w_in", "lambda_q1", "lambda_k1", "lambda_q2", "lambda_k2", "subln_a", "norm_b_out", "w_out",
        "norm_mix_post", "norm_ffn_pre", "w_gate", "w_up", "w_conv", "b_conv", "w_down", "norm_ffn_post", "x_prompt")}
    t |= {name: x for name, x in a.items() if name.startswith("c_")}
    t["x_sample"] = a["x_sample"].rearrange("s t d -> (s t) d")
    t["page_table"] = a["page_table"].rearrange("(o s) n -> o (s n)", o=1)
    t["n_phys"] = a["cache_a_k"].shape[1]
    t["cache_k"] = {"a": by_sequence(a["cache_a_k"]), "b": by_sequence(a["cache_win_k"])}
    t["cache_v"] = {"a": by_sequence(a["cache_a_v"]), "b": by_sequence(a["cache_win_v"])}
    t["win_cache"] = [t["cache_k"]["b"], t["cache_v"]["b"]]
    t["state_conv"] = a["state_conv"][0].rearrange("s j f -> (s j) f")
    t["kv_out"] = [rows(a_k_prompt), rows(a_v_prompt), rows(win_k_prompt), rows(win_v_prompt)]
    t["a_out"] = [rows(a_k_sample), rows(a_v_sample)]
    t["win_out"] = [by_sequence(win_k_sample), by_sequence(win_v_sample)]
    t["y_prompt"], t["y_sample"] = y_prompt[0], y_sample.rearrange("s t d -> (s t) d")
    t["conv_prompt"], t["conv_sample"] = conv_prompt[0, 0], conv_sample[0].rearrange("s j f -> (s j) f")
    t["qT"] = scratch("qT", [2, 8, P, SEQ])
    t["kT"] = scratch("kT", [2, 8, P, SEQ])
    t["v_split"] = scratch("v_split", [2, 2, SEQ, 512])
    t["s_feat"] = scratch("s_feat", [2, 8, P, NS])
    t["s_rows"] = scratch("s_rows", [4, NS, 512])
    t["oa"] = scratch("oa", [SEQ, 512])
    t["ob"] = scratch("ob", [NPAT, SEQ, 512])
    t["stats"] = scratch("stats", [NPAT, SEQ, 2 * B_HEADS])
    t["nlam"] = scratch("nlam", [P, 1])
    t["s_mix"] = scratch("s_mix", [NS, D])
    t["x1"] = scratch("x1", [TOK, D])
    t["h2T"] = scratch("h2T", [2, P, DC, TOK])
    stage_norm_project(nc, t)
    attend_a(nc, t)
    attend_b(nc, t)
    attend_sample(nc, t)
    mix(nc, t)
    ffn(nc, t)


def constants():
    import numpy as np

    f32 = np.float32
    slope_a = 2.0 ** (-8.0 * (np.arange(A_HEADS) + 1) / A_HEADS)
    slope_b = 2.0 ** (-8.0 * (np.arange(B_HEADS) + 1) / B_HEADS)

    def bias(slope, dist, ok):
        return np.where(ok, -slope * dist, MASKED).astype(f32)

    p = np.arange(P)
    dist = p[:, None] - (np.arange(SEQ)[None] - (SEQ - P))
    c = {"c_ident": np.eye(P, dtype=f32), "c_bias_a": np.stack([bias(s, dist, dist >= 0) for s in slope_a])}
    steps = p[:, None] + P - np.arange(2 * P)[None]
    ok = (steps >= 0) & (steps <= P)
    c["c_bias_b"] = np.stack([np.stack([bias(s, d * steps, ok) for d in DILS]) for s in slope_b])
    col = np.arange(32)
    j, m, tok = col // QC, col % QC // DEC_T, col % DEC_T
    new = PAST + p[:, None]
    paged = np.concatenate([P * np.arange(PAGES)[None] + p[:, None], new], 1)
    old = 16 * (32 * np.arange(W_OLD)[None] + (p % 32)[:, None]) + (p // 32)[:, None]
    recent = PAST - 512 + P * np.arange(W_NEW)[None] + p[:, None]
    window = np.concatenate([old, recent, new], 1)
    back = lambda pos: PAST + tok[None, None] - pos[:, :, None]
    real = lambda pos: (pos < PAST + DEC_T)[:, :, None]
    c["c_bias_da"] = bias(slope_a[j], back(paged), (back(paged) >= 0) & real(paged))
    d = back(window)
    count = sum(((d >= 0) & (d <= P * dil) & (d % dil == 0)).astype(int) for dil in DILS) * real(window)
    c["c_bias_db"] = bias(slope_b[2 * j + m], d, count > 0)
    c["c_count"] = count.astype(f32)
    return c


_INS = ["x_prompt", "x_sample", "cache_a_k", "cache_a_v", "page_table", "cache_win_k", "cache_win_v", "state_conv",
        "norm_mix_pre", "w_in", "lambda_q1", "lambda_k1", "lambda_q2", "lambda_k2", "subln_a", "norm_b_out", "w_out",
        "norm_mix_post", "norm_ffn_pre", "w_gate", "w_up", "w_conv", "b_conv", "w_down", "norm_ffn_post"]
_OUTS = [(1, SEQ, D), (DEC_B, DEC_T, D), (1, 1, SEQ, A_HEADS, P), (1, 1, SEQ, A_HEADS, P),
         (1, DEC_B, DEC_T, A_HEADS, P), (1, DEC_B, DEC_T, A_HEADS, P), (1, 1, SEQ, B_HEADS, 64),
         (1, 1, SEQ, B_HEADS, 64), (1, DEC_B, PAST, B_HEADS, 64), (1, DEC_B, PAST, B_HEADS, 64),
         (1, 1, 2, D_FF), (1, DEC_B, 2, D_FF)]


def kernel(**inputs):
    import numpy as _np
    import concourse.bacc as _bacc
    from concourse.bass_utils import run_bass_kernel_spmd as _run

    nc = _bacc.Bacc("TRN2", target_bir_lowering=False, num_devices=1)
    arrays, args = {}, {}
    given = {name: _np.ascontiguousarray(inputs[name]) for name in _INS} | constants()
    for name, x in given.items():
        arrays[f"in_{name}"] = x
        args[name] = nc.dram_tensor(f"in_{name}", x.shape, mybir.dt.from_np(x.dtype), kind="ExternalInput").ap()
    outs = [nc.dram_tensor(f"out_{i}", shape, F32, kind="ExternalOutput").ap() for i, shape in enumerate(_OUTS)]
    program(nc, args, outs)
    r = _run(nc, [arrays], core_ids=[0])
    return tuple(r.results[0][f"out_{i}"] for i in range(len(_OUTS)))
```

```python
import concourse.bass as bass
from concourse import mybir
from contextlib import ExitStack

F32 = mybir.dt.float32
F32R = mybir.dt.float32r
I32 = mybir.dt.int32
ALU = mybir.AluOpType
ACT = mybir.ActivationFunctionType
AX = mybir.AxisListType

P = 128
D = 1024
DC = D // P
SEQ = 2048
NT = SEQ // P
DEC_B, DEC_T = 8, 4
NS = DEC_B * DEC_T
TOK = SEQ + NS
GRP = 512
NG = SEQ // GRP
TPG = GRP // P
A_HEADS, B_HEADS = 4, 8
PAST = 2048
PAGES = PAST // P
D_FF = 2816
FT = D_FF // P
EPS = 1e-6
QK_SCALE = 0.125
MASKED = -1.0e30
LAM_INIT = 0.8 - 0.6
ds = bass.ds


class Stage:

    def __init__(self, nc, name):
        self.nc, self.name, self.stack, self.sems = nc, name, ExitStack(), []
        self.credits, self.soft = {}, []

    def __enter__(self):
        self.stack.__enter__()
        return self

    def __exit__(self, *a):
        self.stack.__exit__(*a)
        self.nc.clear_and_free_semaphores(self.sems)
        self.nc.all_engine_barrier()

    def sb(self, name, shape, dt=F32):
        return self.stack.enter_context(self.nc.sbuf_tensor(f"{self.name}_{name}", shape, dt))

    def ps(self, name):
        return self.stack.enter_context(self.nc.psum_tensor(f"{self.name}_{name}", [P, 512], F32))

    def sem(self, name):
        self.sems.append(self.nc.alloc_semaphore(name=f"{self.name}_{name}"))
        return self.sems[-1]

    def soft_sem(self, name):
        self.soft.append(self.sem(name))
        return self.soft[-1]

    def credit(self, sem, n):
        self.credits[self.sems.index(sem)] = n

    def block(self):
        engines = (self.nc.vector, self.nc.gpsimd, self.nc.scalar, self.nc.tensor, self.nc.sync)
        for i, sem in enumerate(self.sems):
            if sem not in self.soft:
                engines[i % len(engines)].sem_inc(sem, 1 + self.credits.get(i, 0))
        self.nc.all_engine_barrier()
        return self.stack.enter_context(self.nc.Block())


def raised(value):
    value = value + 1
    assert (value if isinstance(value, int) else value.min_val) > 0
    return value


def done(marks, size, i, pos):
    back, p = divmod(pos, size)
    return len(marks) * (i + back + 1) + sum(m <= p for m in marks)


PROJ = [(4, "k", 0), (8, "v", 1), (0, "q", None), (16, "k", 2), (20, "v", 3), (12, "q", None)]
NU = len(PROJ)
NAT = 5


def stage_norm_project(nc, t):
    with Stage(nc, "hT") as outer:
        hTh = outer.sb("h", [P, DC, TOK], F32R)
        hTl = outer.sb("l", [P, DC, TOK], F32R)
        norm_transpose(nc, t, hTh, hTl)
        project(nc, t, hTh, hTl)


def norm_transpose(nc, t, hTh, hTl):
    with Stage(nc, "nt") as s:
        xt = s.sb("x", [P, 2, D])
        hn = s.sb("hn", [P, 2, D])
        junk = s.sb("junk", [P, D])
        gain = s.sb("gain", [P, D])
        ident = s.sb("ident", [P, P])
        ss = s.sb("ss", [P, 2])
        eps = s.sb("eps", [P, 1])
        vr = s.sb("vr", [P, 2])
        rs = s.sb("rs", [P, 2])
        pt = [s.ps(f"t{i}") for i in range(4)]
        const_in, x_in = s.sem("const_in"), [s.sem("x_in0"), s.sem("x_in1")]
        sq, var, rstd, normed, turned, hi, lo = (s.sem(n) for n in ("sq", "var", "rstd", "normed", "turned", "hi", "lo"))
        s.credit(turned, 2)
        block = s.block()
        LAST = NT // 2

        @block.sync
        def _(sp):
            passed = s.sem("passed_sp")
            sp.dma_start(gain[:], t["norm_mix_pre"].partition_broadcast(P)).then_inc(const_in, 16)
            sp.dma_start(ident[:], t["c_ident"]).then_inc(const_in, 16)
            for k in range(2):
                sp.dma_start(xt[:, k], t["x_prompt"][k * P:(k + 1) * P]).then_inc(x_in[k], 16)
            with sp.Fori(0, LAST - 1) as i:
                for k in range(2):
                    sp.wait_ge(normed, raised(2 * i + k + 1))
                    sp.sem_inc(passed, 1)
                    sp.dma_start(xt[:, k], t["x_prompt"][ds((2 * i + 2 + k) * P, P)]).then_inc(x_in[k], 16)
            sp.wait_ge(normed, raised(NT - 1))
            sp.dma_start(xt[0:NS, 0], t["x_sample"]).then_inc(x_in[0], 16)

        @block.scalar
        def _(act):
            passed = s.sem("passed_act")
            act.wait_ge(const_in, raised(33))

            def square(k, n, n_in, rows=P):
                act.wait_ge(x_in[k], raised(n_in))
                if not (isinstance(n, int) and n == 0):
                    act.wait_ge(normed, raised(n))
                act.activation(junk[0:rows], xt[0:rows, k], ACT.Square,
                               accum_out=ss[0:rows, k:k + 1]).then_inc(sq, 1)
                act.wait_ge(sq, raised(n + 1))
                act.activation(vr[0:rows, k:k + 1], ss[0:rows, k:k + 1], ACT.Sqrt, scale=1.0 / D,
                               bias=eps[0:rows, :]).then_inc(var, 1)

            def high(half, n, cols, w):
                act.wait_ge(turned, raised(2 * n + half + 3))
                act.sem_inc(passed, 1)
                src = pt[half][:, :].rearrange("p (c x) -> p c x", c=4)[:, :, 0:w]
                act.activation(hTh[:, 4 * half:4 * half + 4, cols], src, ACT.Copy).then_inc(hi, 1)

            with act.Fori(0, LAST) as i:
                for k in range(2):
                    square(k, 2 * i + k, 16 * i + 16)
                    for half in range(2):
                        high(half, 2 * i + k, ds((2 * i + k) * P, P), P)
            square(0, NT, 16 * LAST + 16, NS)
            for half in range(2):
                high(half, NT, slice(SEQ, TOK), NS)

        @block.vector
        def _(dve):
            dve.memset(eps[:], EPS).then_inc(const_in, 1)
            dve.wait_ge(const_in, raised(33))

            def norm(k, n, rows=P):
                dve.wait_ge(var, raised(n + 1))
                dve.reciprocal(rs[0:rows, k:k + 1], vr[0:rows, k:k + 1]).then_inc(rstd, 1)
                dve.wait_ge(rstd, raised(n + 1))
                dve.wait_ge(turned, raised(2 * n))
                dve.scalar_tensor_tensor(hn[0:rows, k], xt[0:rows, k], rs[0:rows, k:k + 1], gain[0:rows, :],
                                         ALU.mult, ALU.mult).then_inc(normed, 1)

            def low(half, n, cols, w):
                dve.wait_ge(hi, raised(2 * n + half + 1))
                src = pt[half][:, :].rearrange("p (c x) -> p c x", c=4)[:, :, 0:w]
                dve.tensor_tensor(hTl[:, 4 * half:4 * half + 4, cols], src,
                                  hTh[:, 4 * half:4 * half + 4, cols].bitcast(F32), ALU.subtract).then_inc(lo, 1)

            with dve.Fori(0, LAST) as i:
                for k in range(2):
                    norm(k, 2 * i + k)
                    for half in range(2):
                        low(half, 2 * i + k, ds((2 * i + k) * P, P), P)
            norm(0, NT, NS)
            for half in range(2):
                low(half, NT, slice(SEQ, TOK), NS)

        @block.tensor
        def _(pe):
            pe.wait_ge(const_in, raised(32))

            def turn(k, n, rows=P):
                pe.wait_ge(normed, raised(n + 1))
                for half in range(2):
                    if not isinstance(n, int) or n >= 1:
                        pe.wait_ge(lo, raised(2 * n + half - 1))
                    for c in range(4):
                        cc = 4 * half + c
                        last = pe.transpose(pt[half][:, c * P:c * P + rows], hn[0:rows, k, cc * P:(cc + 1) * P],
                                            ident[0:rows, 0:rows])
                    last.then_inc(turned, 1)

            turn(0, 0)
            turn(1, 1)
            with pe.Fori(1, LAST) as i:
                for k in range(2):
                    turn(k, 2 * i + k)
            turn(0, NT, NS)


def project(nc, t, hTh, hTl):
    with Stage(nc, "pj") as s:
        wr = s.sb("wr", [P, 2, DC, P])
        wh = s.sb("wh", [P, 2, DC, P], F32R)
        wl = s.sb("wl", [P, 2, DC, P], F32R)
        st = s.sb("st", [P, 2, TOK])
        qh = s.sb("qh", [P, 2, GRP], F32R)
        ql = s.sb("ql", [P, 2, GRP], F32R)
        nat = s.sb("nat", [P, 2, TPG, P])
        vh = s.sb("vh", [P, 2, TPG, P], F32R)
        vl = s.sb("vl", [P, 2, TPG, P], F32R)
        ident = s.sb("ident", [P, P])
        acc = [s.ps(f"acc{i}") for i in range(NAT)]
        tb = [s.ps(f"tb{i}") for i in range(2)]
        const_in = s.sem("const_in")
        w_in = [s.sem("w_in0"), s.sem("w_in1")]
        w_hi, w_lo, mm, ev, qk_hi, qk_lo, turned, nat_ok, v_hi, v_lo = (s.sem(n) for n in (
            "w_hi", "w_lo", "mm", "ev", "qk_hi", "qk_lo", "turned", "nat_ok", "v_hi", "v_lo"))
        st_out = [s.sem("st_out0"), s.sem("st_out1")]
        qk_out = [s.sem("qk_out0"), s.sem("qk_out1")]
        nat_out = [s.sem("nat_out0"), s.sem("nat_out1")]
        v_out = [s.sem("v_out0"), s.sem("v_out1")]
        J = 4
        SIZE = NAT * NU
        ALL = list(range(SIZE))
        SPLIT = [NAT * u + g for u in range(NU) if PROJ[u][1] != "v" for g in range(NG)]
        TURN = [NAT * u + g for u in range(NU) if PROJ[u][1] != "q" for g in range(NAT)]
        VSPL = [NAT * u + g for u in range(NU) if PROJ[u][1] == "v" for g in range(NG)]
        STO = [NAT * u for u in range(NU) if PROJ[u][1] != "v"]
        for k in range(2):
            s.credit(st_out[k], 16 * len(STO) // 2)
        s.credit(v_lo, len(VSPL))
        s.credit(ev, NAT)
        s.credit(qk_lo, len(SPLIT))
        s.credit(nat_ok, len(TURN))
        s.credit(mm, NAT)
        s.credit(turned, len(TURN))
        block = s.block()

        def nth(marks, pos):
            return marks.index(pos)

        w_view = t["w_in"].rearrange("(c p) f -> p c f", p=P)
        first = {"q": t["qT"], "k": t["kT"]}

        def width(g):
            return GRP if g < NG else NS

        @block.sync
        def _(sp):
            passed = s.sem("passed_sp")
            sp.dma_start(ident[:], t["c_ident"]).then_inc(const_in, 16)
            for u in range(2):
                sp.dma_start(wr[:, u], w_view[:, :, PROJ[u][0] * P:(PROJ[u][0] + 1) * P]).then_inc(w_in[u], 16)

            def rows_out(j, u, g):
                kind, which = PROJ[u][1:]
                pos = NAT * u + g
                sp.wait_ge(nat_ok, raised(done(TURN, SIZE, j, pos)))
                sp.sem_inc(passed, 1)
                k, cols = nth(TURN, pos) % 2, ds(j * P, P)
                if g == NG:
                    sp.dma_start(t["s_rows"][which][:, cols], nat[0:NS, k, 0]).then_inc(nat_out[k], 16)
                    return
                rows = slice(g * GRP, (g + 1) * GRP)
                sp.dma_start(t["kv_out"][which][rows, cols].rearrange("(b p) e -> p b e", p=P),
                             nat[:, k]).then_inc(nat_out[k], 16)
                if kind == "v":
                    sp.wait_ge(v_lo, raised(done(VSPL, SIZE, j, pos)))
                    sp.sem_inc(passed, 1)
                    for part, src in enumerate((vh, vl)):
                        sp.dma_start(t["v_split"][which // 2, part][rows, cols].rearrange("(b p) e -> p b e", p=P),
                                     src[:, g % 2].bitcast(F32)).then_inc(v_out[g % 2], 16)

            def split_out(j, u, g):
                kind = PROJ[u][1]
                sp.wait_ge(qk_lo, raised(done(SPLIT, SIZE, j, NAT * u + g)))
                sp.sem_inc(passed, 1)
                for part, src in enumerate((qh, ql)):
                    sp.dma_start(first[kind][part][ds(4 * (u // 3) + j, 1)][0][:, g * GRP:(g + 1) * GRP],
                                 src[:, g % 2].bitcast(F32)).then_inc(qk_out[g % 2], 16)

            with sp.Fori(0, J) as j:
                for u in range(NU):
                    kind, before = PROJ[u][1], PROJ[u - 1][1]
                    sp.wait_ge(w_lo, raised(NU * j + u + 1))
                    sp.sem_inc(passed, 1)
                    ahead = (PROJ[u + 2][0] + j) if u + 2 < NU else (PROJ[u + 2 - NU][0] + 1 + j)
                    sp.dma_start(wr[:, u % 2], w_view[:, :, ds(ahead * P, P)]).then_inc(w_in[u % 2], 16)
                    if before != "q":
                        for g in (2, 3, 4):
                            rows_out(j, u - 1, g)
                    for pair in ((0, 1), (2, 3)):
                        if kind != "v":
                            for g in pair:
                                split_out(j, u, g)
                        if kind != "q" and pair == (0, 1):
                            for g in pair:
                                rows_out(j, u, g)
                    if kind != "v":
                        sp.wait_ge(ev, raised(NAT * (NU * j + u) + NG + 1 + NAT))
                        sp.sem_inc(passed, 1)
                        sp.dma_start(t["s_feat"][0 if kind == "q" else 1][ds(4 * (u // 3) + j, 1)][0],
                                     st[:, u % 2, SEQ:TOK]).then_inc(st_out[u % 2], 16)
            for k in range(2):
                sp.wait_ge(w_in[k], raised(16 * (J * NU // 2 + 1)))
                sp.wait_ge(qk_out[k], raised(32 * J * len(SPLIT) // 2))
                sp.wait_ge(nat_out[k], raised(16 * J * len(TURN) // 2))
                sp.wait_ge(v_out[k], raised(32 * J * len(VSPL) // 2))
                sp.wait_ge(st_out[k], raised(16 * (J + 1) * len(STO) // 2))

        @block.gpsimd
        def _(pool):
            passed = s.sem("passed_pool")

            def weights_low(n, k):
                pool.wait_ge(w_hi, raised(n + 1))
                pool.tensor_tensor(wl[:, k], wr[:, k], wh[:, k].bitcast(F32), ALU.subtract).then_inc(w_lo, 1)

            def v_split(j, u, g):
                pos = NAT * u + g
                r = nth(VSPL, pos)
                pool.wait_ge(nat_ok, raised(done(TURN, SIZE, j, pos)))
                pool.wait_ge(v_out[g % 2], raised(32 * (len(VSPL) // 2 * j + r // 2)))
                pool.sem_inc(passed, 1)
                k = nth(TURN, pos) % 2
                pool.tensor_copy(vh[:, g % 2], nat[:, k]).then_inc(v_hi, 1)
                pool.wait_ge(v_hi, raised(len(VSPL) * j + r + 1))
                pool.tensor_tensor(vl[:, g % 2], nat[:, k], vh[:, g % 2].bitcast(F32), ALU.subtract).then_inc(v_lo, 1)

            weights_low(0, 0)
            with pool.Fori(0, J) as j:
                for u in range(NU):
                    if PROJ[u - 1][1] == "v":
                        for g in (2, 3):
                            v_split(j, u - 1, g)
                    weights_low(NU * j + u + 1, (u + 1) % 2)
                    if PROJ[u][1] == "v":
                        for g in (0, 1):
                            v_split(j, u, g)

        @block.scalar
        def _(act):

            def weights_high(n, k, seen):
                act.wait_ge(w_in[k], raised(seen))
                act.wait_ge(mm, raised(NAT * n))
                act.activation(wh[:, k], wr[:, k], ACT.Copy).then_inc(w_hi, 1)

            weights_high(0, 0, 16)
            with act.Fori(0, J) as j:
                for u in range(NU):
                    n = NU * j + u
                    act.wait_ge(qk_lo, raised(done(SPLIT, SIZE, j, NAT * (u - 2) + NG)))
                    act.wait_ge(turned, raised(done(TURN, SIZE, j, NAT * (u - 2) + NG)))
                    act.wait_ge(st_out[u % 2], raised(16 * (done([m // NAT for m in STO if m // NAT % 2 == u % 2], NU, j, u - 2))))
                    for g in range(NAT):
                        act.wait_ge(mm, raised(NAT * n + g + 1 + NAT))
                        act.activation(st[:, u % 2, g * GRP:g * GRP + width(g)], acc[g][:, 0:width(g)], ACT.Copy,
                                       scale=QK_SCALE if PROJ[u][1] == "q" else 1.0).then_inc(ev, 1)
                        if g == 1:
                            weights_high(n + 1, (u + 1) % 2, 16 * (NU // 2 * j + (u + 1) // 2 + 1))

        @block.vector
        def _(dve):

            def split(j, u, g):
                pos = NAT * u + g
                r = nth(SPLIT, pos)
                dve.wait_ge(ev, raised(NAT * (NU * j + u) + g + 1 + NAT))
                dve.wait_ge(qk_out[g % 2], raised(32 * (len(SPLIT) // 2 * j + r // 2)))
                src = st[:, u % 2, g * GRP:(g + 1) * GRP]
                dve.tensor_copy(qh[:, g % 2], src).then_inc(qk_hi, 1)
                dve.wait_ge(qk_hi, raised(len(SPLIT) * j + r + 1))
                dve.tensor_tensor(ql[:, g % 2], src, qh[:, g % 2].bitcast(F32), ALU.subtract).then_inc(qk_lo, 1)

            def rows(j, u, g):
                pos = NAT * u + g
                q = nth(TURN, pos)
                dve.wait_ge(turned, raised(done(TURN, SIZE, j, pos)))
                dve.wait_ge(nat_out[q % 2], raised(16 * (len(TURN) // 2 * j + q // 2)))
                back = TURN[q - 2] if q >= 2 else TURN[q - 2] - SIZE
                dve.wait_ge(v_lo, raised(done(VSPL, SIZE, j, back)))
                if g < NG:
                    dve.tensor_copy(nat[:, q % 2], tb[q % 2][:, :].rearrange("p (b e) -> p b e", b=TPG)).then_inc(nat_ok, 1)
                else:
                    dve.tensor_copy(nat[0:NS, q % 2, 0], tb[q % 2][0:NS, 0:P]).then_inc(nat_ok, 1)

            with dve.Fori(0, J) as j:
                for u in range(NU):
                    if PROJ[u - 1][1] != "q":
                        for g in (2, 3, 4):
                            rows(j, u - 1, g)
                    for pair in ((0, 1), (2, 3)):
                        if PROJ[u][1] != "v":
                            for g in pair:
                                split(j, u, g)
                        if PROJ[u][1] != "q" and pair == (0, 1):
                            for g in pair:
                                rows(j, u, g)

        @block.tensor
        def _(pe):
            pe.wait_ge(const_in, raised(16))

            def products(n, u, groups):
                k = u % 2
                for g in groups:
                    pe.wait_ge(ev, raised(NAT * n + g + 1))
                for c in range(DC):
                    for weights, parts in ((wh, (hTh, hTl)), (wl, (hTh,))):
                        for g in groups:
                            cols = slice(g * GRP, g * GRP + width(g))
                            for part in parts:
                                start = c == 0 and weights is wh and part is hTh
                                stop = c == DC - 1 and weights is wl
                                m = pe.matmul(acc[g][:, 0:width(g)], weights[:, k, c], part[:, c, cols],
                                              start=start, stop=stop)
                            if stop:
                                m.then_inc(mm, 1)

            def turn(j, u, g):
                q = nth(TURN, NAT * u + g)
                pe.wait_ge(ev, raised(NAT * (NU * j + u) + g + 1 + NAT))
                back = TURN[q - 2] if q >= 2 else TURN[q - 2] - SIZE
                pe.wait_ge(nat_ok, raised(done(TURN, SIZE, j, back)))
                if g < NG:
                    for b in range(TPG):
                        last = pe.transpose(tb[q % 2][:, b * P:(b + 1) * P],
                                            st[:, u % 2, (TPG * g + b) * P:(TPG * g + b + 1) * P], ident[:])
                else:
                    last = pe.transpose(tb[q % 2][0:NS, 0:P], st[:, u % 2, SEQ:TOK], ident[:])
                last.then_inc(turned, 1)

            with pe.Fori(0, J) as j:
                for u in range(NU):
                    n = NU * j + u
                    pe.wait_ge(w_lo, raised(n + 1))
                    products(n, u, (0, 1))
                    if PROJ[u - 1][1] != "q":
                        for g in (2, 3, 4):
                            turn(j, u - 1, g)
                    products(n, u, (2, 3, 4))
                    if PROJ[u][1] != "q":
                        for g in (0, 1):
                            turn(j, u, g)
def attend_a(nc, t):
    with Stage(nc, "aa") as s:
        kk = s.sb("kk", [P, 2, 2, SEQ], F32R)
        vh = s.sb("vh", [P, 2, NT, P], F32R)
        vl = s.sb("vl", [P, 2, NT, P], F32R)
        qq = s.sb("qq", [P, 2, 2, 2, GRP], F32R)
        bias = s.sb("bias", [P, 2, SEQ])
        p1 = s.sb("p1", [P, 2, TPG, SEQ])
        p2 = s.sb("p2", [P, 3, SEQ])
        wth = s.sb("wth", [P, 2, GRP], F32R)
        wtl = s.sb("wtl", [P, 2, GRP], F32R)
        oT = s.sb("oT", [P, GRP])
        on = s.sb("on", [P, 2, TPG, P])
        mx = s.sb("mx", [P, 2, 2, 4])
        nm = s.sb("nm", [P, 2, 2])
        ll = s.sb("ll", [P, 2, 2])
        rl = s.sb("rl", [P, 2, TPG, 2])
        c2 = s.sb("c2", [P, 2])
        lam4 = s.sb("lam4", [P, 4, 64])
        lam2 = s.sb("lam2", [P, 2, 64])
        lame = s.sb("lame", [P, 5])
        nlam = s.sb("nlam", [P, 1])
        ident = s.sb("ident", [P, P])
        sc = [s.ps(f"sc{i}") for i in range(4)]
        tb = [s.ps(f"tb{i}") for i in range(2)]
        ob = [s.ps(f"ob{i}") for i in range(2)]
        const_in, lam_step, lam_out = s.sem("const_in"), s.sem("lam_step"), s.sem("lam_out")
        k_in = [s.sem(f"k_in{i}") for i in range(2)]
        v_in = [s.sem(f"v_in{i}") for i in range(2)]
        b_in = [s.sem(f"b_in{i}") for i in range(2)]
        q_in = [s.sem(f"q_in{i}") for i in range(2)]
        o_out = [s.sem(f"o_out{i}") for i in range(2)]
        (scored, biased, max_ok, exp_ok, rl_ok, c2_ok, w_ok, turned, high, low, pv, o_read, o_turned, o_ok) = (
            s.sem(n) for n in ("scored", "biased", "max_ok", "exp_ok", "rl_ok", "c2_ok", "w_ok", "turned",
                               "high", "low", "pv", "o_read", "o_turned", "o_ok"))
        p2_ok, rolled = s.sem("p2_ok"), s.sem("rolled")
        s.credit(pv, 2)
        s.credit(biased, 4)
        s.credit(low, 2)
        s.credit(o_ok, 2)
        s.credit(exp_ok, 4)
        block = s.block()
        HP = A_HEADS // 2
        NB_, NGB = 2 * NT, 2 * NG
        chunk, step = {}, {}
        for B in range(NB_):
            for m in range(2):
                for kc in range(B % NT // TPG + 1):
                    chunk[B, m, kc] = len(chunk)
        for g in range(NGB):
            for kb in range(TPG * (g % NG) + TPG):
                step[g, kb] = len(step)
        NC_, NST = len(chunk), len(step)

        def wid(B, kc):
            i = B % NT
            return GRP if kc < i // TPG else (i % TPG + 1) * P

        def keys(B):
            return (B % NT + 1) * P

        def part_steps(g, b, half):
            n, slot = TPG * (g % NG) + TPG, 2 * (b - 1) + half
            return range(n * slot // 6, n * (slot + 1) // 6) if slot >= 0 else range(0)

        def first_block(g, kb):
            return max(0, kb - TPG * (g % NG))

        @block.sync
        def _(sp):
            passed = s.sem("passed_sp")
            for i, name in enumerate(("lambda_q1", "lambda_q2", "lambda_k1", "lambda_k2")):
                sp.dma_start(lam4[:, i], t[name].partition_broadcast(P)).then_inc(const_in, 16)
            sp.dma_start(ident[:], t["c_ident"]).then_inc(const_in, 16)

            def load_k(h, par):
                for part in range(2):
                    src = t["kT"][part][ds(h, 1)][0].rearrange("(m e) x -> e m x", m=2)
                    sp.dma_start(kk[64 * part:64 * part + 64, par].bitcast(F32), src).then_inc(k_in[par], 16)
                sp.dma_start(bias[:, par], t["c_bias_a"][ds(h, 1)][0]).then_inc(b_in[par], 16)

            def load_v(h, par):
                for part, dst in enumerate((vh, vl)):
                    src = t["v_split"][0, part][:, ds(h * P, P)].rearrange("(b p) e -> p b e", p=P)
                    sp.dma_start(dst[:, par].bitcast(F32), src).then_inc(v_in[par], 16)

            def load_q(h, g):
                for half in range(2):
                    for part in range(2):
                        src = t["qT"][part][ds(h, 1)][0][:, (g % NG) * GRP:(g % NG + 1) * GRP]
                        sp.dma_start(qq[64 * half:64 * half + 64, g % 2, part].bitcast(F32),
                                     src.rearrange("(m e) x -> e m x", m=2)).then_inc(q_in[g % 2], 16)

            def send(hp, g):
                sp.wait_ge(o_ok, raised(NGB * hp + g + 1 + 2))
                sp.sem_inc(passed, 1)
                h = 2 * hp + g // NG
                dst = t["oa"][(g % NG) * GRP:(g % NG + 1) * GRP, ds(h * P, P)]
                sp.dma_start(dst.rearrange("(b p) e -> p b e", p=P), on[:, g % 2]).then_inc(o_out[g % 2], 16)

            def roll_window(kind, b):
                old, new = t["win_cache"][kind][ds(b, 1)][0], t["win_out"][kind][ds(b, 1)][0]
                sp.dma_start(new[0:PAST - DEC_T], old[DEC_T:]).then_inc(rolled, 16)
                sp.dma_start(new[PAST - DEC_T:], t["s_rows"][2 + kind][ds(b * DEC_T, DEC_T)]).then_inc(rolled, 16)

            for kind in range(2):
                sp.dma_start(t["a_out"][kind], t["s_rows"][kind]).then_inc(rolled, 16)
            for par in range(2):
                load_k(par, par)
                if par == 0:
                    load_q(0, 0)
                    load_q(0, 1)
                load_v(par, par)
            with sp.Fori(0, HP) as hp:
                for g in range(NGB):
                    sp.wait_ge(scored, raised(NC_ * hp + chunk[TPG * g + 3, 1, g % NG] + 1))
                    sp.sem_inc(passed, 1)
                    roll_window(g % 2, DEC_B // HP * hp + g // 2)
                    nxt = g + 2
                    if nxt < NGB:
                        load_q(2 * hp + nxt // NG, nxt)
                    else:
                        load_q((2 * hp + 2) % A_HEADS, nxt - NGB)
                    if g >= 1:
                        send(hp, g - 1)
                    if g in (NG, ):
                        sp.wait_ge(biased, raised(NC_ * hp + chunk[TPG * NG - 1, 1, NG - 1] + 1 + 4))
                        sp.sem_inc(passed, 1)
                        load_k((2 * hp + 2) % A_HEADS, 0)
                    if g == NG + 1:
                        sp.wait_ge(pv, raised(NST * hp + step[NG - 1, NT - 1] + 1 + 2))
                        sp.sem_inc(passed, 1)
                        load_v((2 * hp + 2) % A_HEADS, 0)
                sp.wait_ge(biased, raised(NC_ * (hp + 1) + 4))
                sp.sem_inc(passed, 1)
                load_k((2 * hp + 3) % A_HEADS, 1)
                send(hp, NGB - 1)
                sp.wait_ge(pv, raised(NST * (hp + 1) + 2))
                sp.sem_inc(passed, 1)
                load_v((2 * hp + 3) % A_HEADS, 1)
            for k in range(2):
                sp.wait_ge(o_out[k], raised(16 * HP * NG))
                sp.wait_ge(q_in[k], raised(64 * (HP * NG + 1)))
                sp.wait_ge(k_in[k], raised(32 * (HP + 1)))
                sp.wait_ge(v_in[k], raised(32 * (HP + 1)))
                sp.wait_ge(b_in[k], raised(16 * (HP + 1)))
            sp.wait_ge(rolled, raised(16 * (4 * DEC_B + 2)))
            sp.wait_ge(lam_step, raised(5))
            sp.dma_start(t["nlam"], nlam[:]).then_inc(lam_out, 16)
            sp.wait_ge(lam_out, raised(16))

        @block.tensor
        def _(pe):
            pe.wait_ge(const_in, raised(80))

            def scores(hp, B, m):
                g, par = B // TPG, B // NT
                if m == 0 and B % TPG == 0:
                    pe.wait_ge(q_in[g % 2], raised(64 * (NG * hp + g // 2 + 1)))
                    if g % NG == 0:
                        pe.wait_ge(k_in[par], raised(32 * (hp + 1)))
                q = slice((B % TPG) * P, (B % TPG + 1) * P)
                for kc in range(B % NT // TPG + 1):
                    c = chunk[B, m, kc]
                    w = wid(B, kc)
                    pe.wait_ge(biased, raised(NC_ * hp + c + 1))
                    cols = slice(kc * GRP, kc * GRP + w)
                    for part in range(2):
                        mm = pe.matmul(sc[c % 4][:, 0:w], qq[:, g % 2, part, m, q], kk[:, par, m, cols],
                                       start=part == 0, stop=part == 1)
                    mm.then_inc(scored, 1)

            def turn(hp, g, kb):
                x = step[g, kb]
                if kb == 0:
                    pe.wait_ge(w_ok, raised(NB_ * hp + TPG * (g + 1)))
                pe.wait_ge(low, raised(NST * hp + x + 1))
                for b in range(first_block(g, kb), TPG):
                    mm = pe.transpose(tb[x % 2][:, b * P:(b + 1) * P], p1[:, g % 2, b, kb * P:(kb + 1) * P], ident[:])
                mm.then_inc(turned, 1)

            def weigh(hp, g, kb):
                x, par = step[g, kb], g // NG
                last = kb == TPG * (g % NG) + TPG - 1
                if kb == 0:
                    pe.wait_ge(v_in[par], raised(32 * (hp + 1)))
                    pe.wait_ge(o_ok, raised(NGB * hp + g + 1))
                pe.wait_ge(low, raised(NST * hp + x + 1 + 2))
                c = slice(first_block(g, kb) * P, GRP)
                for n, (v, w) in enumerate(((vh, wth), (vh, wtl), (vl, wth))):
                    mm = pe.matmul(ob[g % 2][:, c], v[:, par, kb], w[:, x % 2, c], start=kb == 0 and n == 0,
                                   stop=last and n == 2)
                mm.then_inc(pv, 1)

            def turn_back(hp, g):
                pe.wait_ge(o_read, raised(NGB * hp + g + 1))
                for b in range(TPG):
                    mm = pe.transpose(ob[g % 2][:, b * P:(b + 1) * P], oT[:, b * P:(b + 1) * P], ident[:])
                mm.then_inc(o_turned, 1)

            def steps(hp, g, kbs):
                for kb in kbs:
                    turn(hp, g, kb)
                    if kb > 0:
                        weigh(hp, g, kb - 1)

            with pe.Fori(0, HP) as hp:
                for g in range(NGB):
                    for b in range(TPG):
                        for m in range(2):
                            scores(hp, TPG * g + b, m)
                            if g > 0:
                                steps(hp, g - 1, part_steps(g - 1, b, m))
                    if g > 0:
                        weigh(hp, g - 1, TPG * ((g - 1) % NG) + TPG - 1)
                        turn_back(hp, g - 1)
                g = NGB - 1
                steps(hp, g, range(NT))
                weigh(hp, g, NT - 1)
                turn_back(hp, g)

        @block.vector
        def _(dve):
            passed = s.sem("passed_dve")
            dve.wait_ge(const_in, raised(80))
            dve.tensor_tensor(lam2[:], lam4[:, 0:2], lam4[:, 2:4], ALU.mult).then_inc(lam_step, 1)
            dve.wait_ge(lam_step, raised(1))
            dve.tensor_reduce(lame[:, 0:2], lam2[:], AX.X, ALU.add).then_inc(lam_step, 1)
            dve.wait_ge(lam_step, raised(3))
            dve.tensor_tensor(lame[:, 4:5], lame[:, 3:4], lame[:, 2:3], ALU.subtract).then_inc(lam_step, 1)
            dve.wait_ge(lam_step, raised(4))
            dve.tensor_scalar(nlam[:], lame[:, 4:5], -LAM_INIT, None, ALU.add).then_inc(lam_step, 1)
            dve.wait_ge(lam_step, raised(5))

            def add_bias(hp, B, m):
                i, par = B % NT, B // NT
                if m == 0:
                    if i == 0:
                        dve.wait_ge(b_in[par], raised(16 * (hp + 1)))
                    g = B // TPG
                    if g >= 2:
                        dve.wait_ge(turned, raised(NST * hp + step[g - 2, TPG * ((g - 2) % NG) + TPG - 1] + 1))
                    else:
                        dve.wait_ge(turned, raised(NST * hp))
                    dve.wait_ge(max_ok, raised(NB_ * hp + B))
                else:
                    dve.wait_ge(w_ok, raised(NB_ * hp + max(B - 2, 0)))
                for kc in range(i // TPG + 1):
                    c, w = chunk[B, m, kc], wid(B, kc)
                    dve.wait_ge(scored, raised(NC_ * hp + c + 1))
                    dve.sem_inc(passed, 1)
                    dst = p1[:, B // TPG % 2, B % TPG] if m == 0 else p2[:, B % 3]
                    x = kc * GRP + (NT - 1 - i) * P
                    dve.tensor_tensor_reduce(dst[:, kc * GRP:kc * GRP + w], sc[c % 4][:, 0:w], bias[:, par, x:x + w],
                                             1.0, -3.0e38, ALU.add, ALU.max,
                                             mx[:, B % 2, m, kc:kc + 1]).then_inc(biased, 1)

            def negate_max(hp, B):
                n = B % NT // TPG + 1
                dve.wait_ge(biased, raised(NC_ * hp + chunk[B, 1, n - 1] + 1 + 4))
                dve.wait_ge(exp_ok, raised(2 * (NB_ * hp + B)))
                dve.tensor_reduce(nm[:, B % 2], mx[:, B % 2, :, 0:n], AX.X, ALU.max, negate=True).then_inc(max_ok, 1)

            def factors(hp, B):
                g, b = B // TPG, B % TPG
                dve.wait_ge(exp_ok, raised(2 * (NB_ * hp + B + 1) + 4))
                dve.reciprocal(rl[:, g % 2, b], ll[:, B % 2]).then_inc(rl_ok, 1)
                dve.wait_ge(rl_ok, raised(NB_ * hp + B + 1))
                dve.wait_ge(w_ok, raised(NB_ * hp + max(B - 1, 0)))
                dve.scalar_tensor_tensor(c2[:, B % 2:B % 2 + 1], ll[:, B % 2, 0:1], nlam[:], rl[:, g % 2, b, 1:2],
                                         ALU.mult, ALU.mult).then_inc(c2_ok, 1)

            def split_low(hp, g, kbs):
                for kb in kbs:
                    x = step[g, kb]
                    c = slice(first_block(g, kb) * P, GRP)
                    dve.wait_ge(high, raised(NST * hp + x + 1))
                    dve.tensor_tensor(wtl[:, x % 2, c], tb[x % 2][:, c], wth[:, x % 2, c].bitcast(F32),
                                      ALU.subtract).then_inc(low, 1)

            def finish(hp, g):
                dve.wait_ge(o_turned, raised(NGB * hp + g + 1))
                dve.wait_ge(o_out[g % 2], raised(16 * (NG * hp + g // 2)))
                for b in range(TPG):
                    mm = dve.tensor_scalar(on[:, g % 2, b], ob[g % 2][:, b * P:(b + 1) * P], rl[:, g % 2, b, 0:1],
                                           None, ALU.mult)
                mm.then_inc(o_ok, 1)

            with dve.Fori(0, HP) as hp:
                for g in range(NGB):
                    for b in range(TPG):
                        B = TPG * g + b
                        for m in range(2):
                            add_bias(hp, B, m)
                            if m == 1:
                                negate_max(hp, B)
                            if g > 0:
                                split_low(hp, g - 1, part_steps(g - 1, b, m))
                            if m == 0 and B > 0:
                                factors(hp, B - 1)
                    if g > 0:
                        finish(hp, g - 1)
                factors(hp, NB_ - 1)
                split_low(hp, NGB - 1, range(NT))
                finish(hp, NGB - 1)

        @block.gpsimd
        def _(pool):
            with pool.Fori(0, HP) as hp:
                for B in range(NB_):
                    n = keys(B)
                    w, y = p1[:, B // TPG % 2, B % TPG, 0:n], p2[:, B % 3, 0:n]
                    pool.wait_ge(p2_ok, raised(NB_ * hp + B + 1))
                    pool.tensor_tensor(w, w, y, ALU.add).then_inc(w_ok, 1)

        @block.scalar
        def _(act):
            act.wait_ge(lam_step, raised(2))
            act.activation(lame[:, 2:4], lame[:, 0:2], ACT.Exp).then_inc(lam_step, 1)

            def expo(hp, B, m):
                n = keys(B)
                act.wait_ge(max_ok, raised(NB_ * hp + B + 1))
                x = (p1[:, B // TPG % 2, B % TPG] if m == 0 else p2[:, B % 3])[:, 0:n]
                if m == 0:
                    act.wait_ge(c2_ok, raised(NB_ * hp + max(B - 1, 0)))
                act.activation(x, x, ACT.Exp, bias=nm[:, B % 2, m:m + 1],
                               accum_out=ll[:, B % 2, m:m + 1]).then_inc(exp_ok, 1)

            def scale(hp, B):
                y = p2[:, B % 3, 0:keys(B)]
                act.wait_ge(c2_ok, raised(NB_ * hp + B + 1))
                act.activation(y, y, ACT.Copy, scale=c2[:, B % 2:B % 2 + 1]).then_inc(p2_ok, 1)

            def split_high(hp, g, kbs):
                for kb in kbs:
                    x = step[g, kb]
                    c = slice(first_block(g, kb) * P, GRP)
                    act.wait_ge(pv, raised(NST * hp + x + 1))
                    act.wait_ge(turned, raised(NST * hp + x + 1))
                    act.activation(wth[:, x % 2, c], tb[x % 2][:, c], ACT.Copy).then_inc(high, 1)

            def read_out(hp, g):
                act.wait_ge(pv, raised(NST * hp + step[g, TPG * (g % NG) + TPG - 1] + 1 + 2))
                act.wait_ge(o_turned, raised(NGB * hp + g))
                act.activation(oT[:], ob[g % 2][:], ACT.Copy).then_inc(o_read, 1)

            with act.Fori(0, HP) as hp:
                for g in range(NGB):
                    for b in range(TPG):
                        for m in range(2):
                            if m == 1:
                                expo(hp, TPG * g + b, 0)
                            elif TPG * g + b > 0:
                                expo(hp, TPG * g + b - 1, 1)
                            if g > 0:
                                split_high(hp, g - 1, part_steps(g - 1, b, m))
                            if m == 0 and TPG * g + b > 0:
                                scale(hp, TPG * g + b - 1)
                    if g > 0:
                        read_out(hp, g - 1)
                expo(hp, NB_ - 1, 1)
                scale(hp, NB_ - 1)
                split_high(hp, NGB - 1, range(NT))
                read_out(hp, NGB - 1)
DILS = (1, 4, 16)
NPAT = len(DILS)


def token_rows(dram, pat):
    if pat == 0:
        return [(0, NT, dram.rearrange("(b a) e -> a b e", a=P))]
    if pat == 2:
        return [(0, NT, dram.rearrange("(a r) e -> a r e", r=NT))]
    return [(4 * j, 4, dram[512 * j:512 * (j + 1)].rearrange("(a r) e -> a r e", r=4)) for j in range(4)]


def attend_b(nc, t):
    with Stage(nc, "ab") as s:
        kk = s.sb("kk", [P, 2, SEQ], F32R)
        qq = s.sb("qq", [P, 2, 2, SEQ], F32R)
        vv = s.sb("vv", [P, NPAT, 2, NT, P], F32R)
        bias = s.sb("bias", [P, 2, NPAT, 2 * P])
        pr = s.sb("pr", [P, 4, GRP])
        wth = s.sb("wth", [P, 2, GRP], F32R)
        wtl = s.sb("wtl", [P, 2, GRP], F32R)
        on = s.sb("on", [P, NPAT, NT, P])
        mx = s.sb("mx", [P, 2, NPAT, NT])
        nm = s.sb("nm", [P, 2, NPAT, NT])
        ll = s.sb("ll", [P, 2, NPAT, NT])
        stats = s.sb("stats", [P, NPAT, NT, B_HEADS, 2])
        ident = s.sb("ident", [P, P])
        sc = [s.ps(f"sc{i}") for i in range(4)]
        tb = [s.ps(f"tb{i}") for i in range(2)]
        ob = [s.ps(f"ob{i}") for i in range(2)]
        const_in, stats_out = s.sem("const_in"), s.sem("stats_out")
        h_in = [s.sem(f"h_in{i}") for i in range(2)]
        v_in = [s.sem(f"v_in{i}") for i in range(NPAT)]
        o_out = [s.sem(f"o_out{i}") for i in range(NPAT)]
        scored, biased, max_ok, exp_ok, turned, high, low, pv, o_ok, stat_ok = (s.sem(n) for n in (
            "scored", "biased", "max_ok", "exp_ok", "turned", "high", "low", "pv", "o_ok", "stat_ok"))
        s.credit(turned, 4)
        s.credit(pv, 2)
        s.credit(biased, 4)
        s.credit(low, 2)
        s.credit(o_ok, 2)
        block = s.block()
        HSTEPS = [(p, list(range(n * i, n * i + n))) for p, n in ((0, 2), (1, 2), (2, 4)) for i in range(NT // n)]
        SH, S, PAIRS = len(HSTEPS), 2 * len(HSTEPS), B_HEADS // 2
        LAST_OF = [max(i for i, (p, _) in enumerate(HSTEPS) if p == pat) for pat in range(NPAT)]
        NOG = 12
        H_DMAS, NOUT = 2 + 4 + 1, [1, 4, 1]
        V_DMAS = [2 * n for n in NOUT]

        def step(x):
            par, i = divmod(x, SH)
            return (par,) + HSTEPS[i]

        def has_prev(p, b):
            return p == 0 and b > 0 or p == 1 and b >= 4

        def o_group(x):
            par, p, blocks = step(x)
            return 6 * par + 2 * p + blocks[0] // 8

        def tiles(p, blocks):
            out = []
            for n, b in enumerate(blocks):
                if p == 2:
                    out.append((n, b, b))
                    continue
                if has_prev(p, b):
                    out.append((2 * n, b - (1 if p == 0 else 4), b))
                out.append((2 * n + 1, b, b))
            return out

        def used(ap, p, blocks):
            if p == 0 and blocks[0] == 0:
                return ap[:, P:]
            if p == 1 and blocks[0] < 4:
                return ap.rearrange("p (n t x) -> p n t x", n=2, t=2)[:, :, 1]
            return ap

        def tokens(p, b, back):
            d = DILS[p]
            start = {0: P * b, 1: 512 * (b // 4) + b % 4, 2: b}[p]
            n = 2 * P if back else P
            start -= P * d if back else 0
            return slice(start, start + (n - 1) * d + 1, d)

        @block.sync
        def _(sp):
            passed = s.sem("passed_sp")
            sp.dma_start(ident[:], t["c_ident"]).then_inc(const_in, 16)

            def load_head(pair, par):
                for part in range(2):
                    src = t["kT"][part][ds(4 + pair, 1)][0][64 * par:64 * par + 64]
                    sp.dma_start(kk[64 * part:64 * part + 64, par].bitcast(F32), src).then_inc(h_in[par], 16)
                    src = t["qT"][part][ds(4 + pair, 1)][0][64 * par:64 * par + 64]
                    for half in range(2):
                        sp.dma_start(qq[64 * half:64 * half + 64, par, part].bitcast(F32), src).then_inc(h_in[par], 16)
                sp.dma_start(bias[:, par], t["c_bias_b"][ds(2 * pair + par, 1)][0]
                             .rearrange("n p x -> p n x")).then_inc(h_in[par], 16)

            def load_v(pair, p):
                for part in range(2):
                    for b0, n, src in token_rows(t["v_split"][1, part][:, ds(pair * P, P)], p):
                        sp.dma_start(vv[:, p, part, b0:b0 + n].bitcast(F32), src).then_inc(v_in[p], 16)

            load_head(0, 0)
            for p in range(NPAT):
                load_v(0, p)
            load_head(0, 1)
            with sp.Fori(0, PAIRS) as i:
                nxt = (i + 1) % PAIRS
                sp.wait_ge(biased, raised(S * i + SH + 4))
                sp.sem_inc(passed, 1)
                load_head(nxt, 0)
                for p in range(NPAT):
                    sp.wait_ge(pv, raised(S * i + SH + LAST_OF[p] + 1 + 2))
                    sp.sem_inc(passed, 1)
                    load_v(nxt, p)
                    if p == NPAT - 1:
                        load_head(nxt, 1)
                    sp.wait_ge(o_ok, raised(NOG * i + 6 + 2 * p + 2 + 2))
                    sp.sem_inc(passed, 1)
                    for b0, n, dst in token_rows(t["ob"][p][:, ds(i * P, P)], p):
                        sp.dma_start(dst, on[:, p, b0:b0 + n]).then_inc(o_out[p], 16)
            for k in range(2):
                sp.wait_ge(h_in[k], raised(16 * H_DMAS * (PAIRS + 1)))
            for p in range(NPAT):
                sp.wait_ge(v_in[p], raised(16 * V_DMAS[p] * (PAIRS + 1)))
                sp.wait_ge(o_out[p], raised(16 * NOUT[p] * PAIRS))
            sp.wait_ge(stat_ok, raised(2 * PAIRS))
            for p in range(NPAT):
                for b0, n, dst in token_rows(t["stats"][p], p):
                    sp.dma_start(dst, stats[:, p, b0:b0 + n].rearrange("p b h k -> p b (h k)")).then_inc(stats_out, 16)
            sp.wait_ge(stats_out, raised(16 * sum(NOUT)))

        @block.tensor
        def _(pe):
            pe.wait_ge(const_in, raised(16))

            def scores(i, x):
                par, p, blocks = step(x)
                if x % SH == 0:
                    pe.wait_ge(h_in[par], raised(16 * H_DMAS * (i + 1)))
                pe.wait_ge(biased, raised(S * i + x + 1))
                for n, b in enumerate(blocks):
                    back = has_prev(p, b)
                    col = n * P if p == 2 else 2 * n * P + (0 if back else P)
                    w = 2 * P if back else P
                    for part in range(2):
                        mm = pe.matmul(sc[x % 4][:, col:col + w], qq[:, par, part, tokens(p, b, False)],
                                       kk[:, par, tokens(p, b, back)], start=part == 0, stop=part == 1)
                mm.then_inc(scored, 1)

            def turn(i, x):
                par, p, blocks = step(x)
                pe.wait_ge(exp_ok, raised(S * i + x + 1))
                pe.wait_ge(low, raised(S * i + x + 1))
                for c, _, _ in tiles(p, blocks):
                    mm = pe.transpose(tb[x % 2][:, c * P:(c + 1) * P], pr[:, x % 4, c * P:(c + 1) * P], ident[:])
                mm.then_inc(turned, 1)

            def weigh(i, x):
                par, p, blocks = step(x)
                og = o_group(x)
                if x % SH == 0 or step(x - 1)[1] != p:
                    pe.wait_ge(v_in[p], raised(16 * V_DMAS[p] * (i + 1)))
                if blocks[0] % 8 == 0:
                    pe.wait_ge(o_ok, raised(NOG * i + og + 1))
                pe.wait_ge(low, raised(S * i + x + 1 + 2))
                for b in blocks:
                    mine = [(c, v) for c, v, bb in tiles(p, blocks) if bb == b]
                    n = 0
                    for c, v in mine:
                        for w, part in ((wth, 0), (wth, 1), (wtl, 0)):
                            mm = pe.matmul(ob[og % 2][:, (b % 8) * 64:(b % 8 + 1) * 64], w[:, x % 2, c * P:(c + 1) * P],
                                           vv[:, p, part, v, 64 * par:64 * par + 64], start=n == 0,
                                           stop=n == 3 * len(mine) - 1)
                            n += 1
                mm.then_inc(pv, 1)

            with pe.Fori(0, PAIRS) as i:
                for x in range(S + 3):
                    if x < S:
                        scores(i, x)
                    if 2 <= x < S + 2:
                        turn(i, x - 2)
                    if x >= 3:
                        weigh(i, x - 3)

        @block.vector
        def _(dve):
            passed = s.sem("passed_dve")

            def add_bias(i, x):
                par, p, blocks = step(x)
                if x % SH == 0:
                    dve.wait_ge(h_in[par], raised(16 * H_DMAS * (i + 1)))
                dve.wait_ge(turned, raised(S * i + x + 1))
                dve.wait_ge(scored, raised(S * i + x + 1))
                dve.sem_inc(passed, 1)
                for n, b in enumerate(blocks):
                    back = has_prev(p, b)
                    col = n * P if p == 2 else 2 * n * P + (0 if back else P)
                    w = 2 * P if back else P
                    mm = dve.tensor_tensor_reduce(pr[:, x % 4, col:col + w], sc[x % 4][:, col:col + w],
                                                  bias[:, par, p, 2 * P - w:], 1.0, -3.0e38, ALU.add, ALU.max,
                                                  mx[:, par, p, b:b + 1])
                mm.then_inc(biased, 1)
                dve.wait_ge(biased, raised(S * i + x + 1 + 4))
                b0, n = blocks[0], len(blocks)
                dve.tensor_scalar(nm[:, par, p, b0:b0 + n], mx[:, par, p, b0:b0 + n], -1.0, None,
                                  ALU.mult).then_inc(max_ok, 1)

            def split_low(i, x):
                _, p, blocks = step(x)
                dve.wait_ge(high, raised(S * i + x + 1))
                dve.tensor_tensor(used(wtl[:, x % 2], p, blocks), used(tb[x % 2][:], p, blocks),
                                  used(wth[:, x % 2].bitcast(F32), p, blocks), ALU.subtract).then_inc(low, 1)

            def keep_stats(i, par):
                dve.wait_ge(exp_ok, raised(S * i + SH * (par + 1)))
                dve.sem_inc(passed, 1)
                dve.tensor_copy(stats[:, :, :, ds(2 * i + par, 1), 0], mx[:, par])
                dve.tensor_copy(stats[:, :, :, ds(2 * i + par, 1), 1], ll[:, par]).then_inc(stat_ok, 1)

            with dve.Fori(0, PAIRS) as i:
                for x in range(S + 2):
                    if x < S:
                        add_bias(i, x)
                    if x >= 2:
                        split_low(i, x - 2)
                    if x == SH + 2:
                        keep_stats(i, 0)
                keep_stats(i, 1)

        @block.scalar
        def _(act):

            def expo(i, x):
                par, p, blocks = step(x)
                if x % SH == 0:
                    act.wait_ge(stat_ok, raised(2 * i + par if par == 0 else 2 * i))
                act.wait_ge(max_ok, raised(S * i + x + 1))
                for n, b in enumerate(blocks):
                    back = has_prev(p, b)
                    col = n * P if p == 2 else 2 * n * P + (0 if back else P)
                    w = 2 * P if back else P
                    y = pr[:, x % 4, col:col + w]
                    mm = act.activation(y, y, ACT.Exp, bias=nm[:, par, p, b:b + 1], accum_out=ll[:, par, p, b:b + 1])
                mm.then_inc(exp_ok, 1)

            def split_high(i, x):
                _, p, blocks = step(x)
                act.wait_ge(pv, raised(S * i + x + 1))
                act.wait_ge(turned, raised(S * i + x + 1 + 4))
                act.activation(used(wth[:, x % 2], p, blocks), used(tb[x % 2][:], p, blocks), ACT.Copy).then_inc(high, 1)

            def read_out(i, x):
                par, p, blocks = step(x)
                og, b0 = o_group(x), blocks[0] // 8 * 8
                act.wait_ge(pv, raised(S * i + x + 1 + 2))
                act.wait_ge(o_out[p], raised(16 * NOUT[p] * i))
                act.activation(on[:, p, b0:b0 + 8, 64 * par:64 * par + 64],
                               ob[og % 2][:].rearrange("p (b e) -> p b e", b=8), ACT.Copy).then_inc(o_ok, 1)

            ends = {x for x in range(S) if x == S - 1 or o_group(x + 1) != o_group(x)}
            with act.Fori(0, PAIRS) as i:
                for x in range(S + 4):
                    if x - 4 in ends:
                        read_out(i, x - 4)
                    if 1 <= x < S + 1:
                        expo(i, x - 1)
                    if 2 <= x < S + 2:
                        split_high(i, x - 2)
W_OLD = 3
W_NEW = 4
QC = 8


def attend_sample(nc, t):
    with Stage(nc, "sa") as s:
        TILES = {"a": PAGES, "b": W_OLD + W_NEW}
        kc = {"a": s.sb("kca", [P, 2, TILES["a"], 512]), "b": s.sb("kcb", [P, 2, TILES["b"], 512])}
        vc = {"a": s.sb("vca", [P, 2, TILES["a"], 512]), "b": s.sb("vcb", [P, 1, TILES["b"], 512])}
        vn = {k: s.sb("vn" + k, [DEC_T, 2, 512]) for k in "ab"}
        kT = s.sb("kT", [P, 2, 512])
        qs = s.sb("qs", [P, 2, DC, NS])
        qd = s.sb("qd", [P, 2, 4, QC])
        kn = s.sb("kn", [P, 2, 4, DEC_T])
        bias = {k: s.sb("bias" + k, [P, TILES[k] + 1, 32]) for k in "ab"}
        count = s.sb("count", [P, TILES["b"] + 1, 32])
        sb_ = {k: s.sb("s" + k, [P, TILES[k] + 1, 32]) for k in "ab"}
        pb = {k: s.sb("p" + k, [P, TILES[k] + 1, 32]) for k in "ab"}
        mx, rs, li = (s.sb(n, [P, 32]) for n in ("mx", "rs", "li"))
        mrow = s.sb("mrow", [32, 1])
        dg = s.sb("dg", [32, 32])
        od = s.sb("od", [P, 4, QC])
        oT = s.sb("oT", [P, DC, NS])
        nlam = s.sb("nlam", [P, 1])
        ident = s.sb("ident", [P, P])
        ones = s.sb("ones", [P, P])
        rows = s.sb("rows", [NS, DC, P])
        ptab = s.sb("ptab", [1, DEC_B * PAGES], I32)
        tb = [s.ps(f"tb{i}") for i in range(2)]
        sc = [s.ps(f"sc{i}") for i in range(2)]
        scn, misc, den, ob = s.ps("scn"), s.ps("misc"), s.ps("den"), s.ps("ob")
        const_in, tab_in, zeroed = s.sem("const_in"), s.sem("tab_in"), s.sem("zeroed")
        k_in = {k: [s.sem(f"k_in{k}{i}") for i in range(2)] for k in "ab"}
        v_in = {k: [s.soft_sem(f"v_in{k}{i}") for i in range(2)] for k in "ab"}
        kt_ok = [s.sem(f"kt_ok{i}") for i in range(2)]
        rows_out = s.sem("rows_out")
        (k_turned, k_used, q_ok, scored, s_read, max_part, max_turned, max_row, dg_ok, max_all, shifted, exp_ok,
         weighed, sum_ok, den_ok, li_ok, pv, o_div, o_ok, fin_t, fin_r) = (s.sem(n) for n in (
             "k_turned", "k_used", "q_ok", "scored", "s_read", "max_part", "max_turned", "max_row", "dg_ok",
             "max_all", "shifted", "exp_ok", "weighed", "sum_ok", "den_ok", "li_ok", "pv", "o_div", "o_ok",
             "fin_t", "fin_r"))
        s.credit(k_used, 2)
        s.credit(s_read, 2)
        block = s.block()
        N = DEC_B // 2
        PASSES = [("a", 0), ("b", 0), ("a", 1), ("b", 1)]
        NP_ = len(PASSES)
        tile = {}
        for x, (k, _) in enumerate(PASSES):
            for n in range(TILES[k]):
                tile[x, n] = len(tile)
        NTL = len(tile)
        K_DMAS = {"a": PAGES, "b": 5}
        V_DMAS = {"a": PAGES + 1, "b": 6}
        TURN_MAX, SPREAD_MAX, EXPO, SUMS = 1, 3, 4, 5

        def at(x):
            if x == NP_:
                return [None] * (SUMS + 1)
            return list(range(TILES[PASSES[x][0]]))

        def load_pages(eng, cache, dst, seq, sem_):
            for n in range(PAGES):
                page = eng.value_load(ptab[0:1, ds(seq * PAGES + n, 1)], min_val=0, max_val=t["n_phys"] - 1)
                eng.dma_start(dst[:, n], cache[ds(page, 1)][0]).then_inc(sem_, 16)

        @block.sync
        def _(sp):
            passed = s.sem("passed_sp")
            sp.dma_start(ptab[:], t["page_table"]).then_inc(tab_in, 16)
            sp.dma_start(ident[:], t["c_ident"]).then_inc(const_in, 16)
            for i in range(2):
                sp.dma_start(qs[:, i], t["s_feat"][i].rearrange("c p n -> p c n")).then_inc(const_in, 16)
            for k in "ab":
                sp.dma_start(bias[k][:], t["c_bias_d" + k]).then_inc(const_in, 16)
            sp.dma_start(count[:], t["c_count"]).then_inc(const_in, 16)
            sp.dma_start(nlam[:], t["nlam"]).then_inc(const_in, 16)
            sp.wait_ge(tab_in, raised(16))

            def load_window(cache, dst, seq, sem_):
                win = cache[ds(seq, 1)][0]
                old = win[0:PAST - 512].rearrange("(n g r) e -> r g n e", n=W_OLD, r=16)
                for r in range(4):
                    sp.dma_start(dst[32 * r:32 * r + 32, 0:W_OLD], old[r]).then_inc(sem_, 16)
                sp.dma_start(dst[:, W_OLD:], win[PAST - 512:].rearrange("(n p) e -> p n e", p=P)).then_inc(sem_, 16)

            def load_k(k, par, seq):
                if k == "a":
                    load_pages(sp, t["cache_k"][k], kc[k][:, par], seq, k_in[k][par])
                else:
                    load_window(t["cache_k"][k], kc[k][:, par], seq, k_in[k][par])

            def load_v(par, seq):
                load_window(t["cache_v"]["b"], vc["b"][:, 0], seq, v_in["b"][par])
                sp.dma_start(vn["b"][:, par], t["s_rows"][3][ds(seq * DEC_T, DEC_T)]).then_inc(v_in["b"][par], 16)

            load_k("a", 0, 0)
            load_k("b", 0, 0)
            load_v(0, 0)
            load_k("a", 1, 1)
            load_k("b", 1, 1)

            def refill(i, last):
                if not last:
                    sp.wait_ge(scored, raised(NP_ * i + 1))
                    sp.sem_inc(passed, 1)
                    load_k("a", 0, 2 * i + 2)
                    sp.wait_ge(scored, raised(NP_ * i + 2))
                    sp.sem_inc(passed, 1)
                    load_k("b", 0, 2 * i + 2)
                sp.wait_ge(pv, raised(NP_ * i + 2))
                sp.sem_inc(passed, 1)
                load_v(1, 2 * i + 1)
                if not last:
                    sp.wait_ge(scored, raised(NP_ * i + 3))
                    sp.sem_inc(passed, 1)
                    load_k("a", 1, 2 * i + 3)
                    sp.wait_ge(scored, raised(NP_ * i + 4))
                    sp.sem_inc(passed, 1)
                    load_k("b", 1, 2 * i + 3)
                    sp.wait_ge(pv, raised(NP_ * i + 4))
                    sp.sem_inc(passed, 1)
                    load_v(0, 2 * i + 2)

            with sp.Fori(0, N - 1) as i:
                refill(i, False)
            refill(N - 1, True)
            sp.wait_ge(fin_r, raised(2))
            sp.dma_start(t["s_mix"].rearrange("n (c x) -> n c x", c=DC), rows[:]).then_inc(rows_out, 16)
            sp.wait_ge(rows_out, raised(16))

        @block.gpsimd
        def _(pool):
            passed = s.sem("passed_pool")
            pool.memset(ones[:], 1.0).then_inc(zeroed, 1)
            pool.memset(qd[:], 0.0).then_inc(zeroed, 1)
            for k in "ab":
                pool.memset(sb_[k][:, TILES[k]], MASKED).then_inc(zeroed, 1)

            pool.wait_ge(tab_in, raised(16))

            def load_v(par, seq):
                load_pages(pool, t["cache_v"]["a"], vc["a"][:, par], seq, v_in["a"][par])
                pool.dma_start(vn["a"][:, par], t["s_rows"][1][ds(seq * DEC_T, DEC_T)]).then_inc(v_in["a"][par], 16)

            for par in range(2):
                load_v(par, par)
            with pool.Fori(0, N - 1) as i:
                for par in range(2):
                    pool.wait_ge(pv, raised(NP_ * i + 2 * par + 1))
                    pool.sem_inc(passed, 1)
                    load_v(par, 2 * i + 2 + par)

        @block.tensor
        def _(pe):
            pe.wait_ge(const_in, raised(16 * 7))
            pe.wait_ge(zeroed, raised(4))

            def turn_k(i, x, n):
                k, par = PASSES[x]
                y = tile[x, n]
                if n == 0:
                    pe.wait_ge(k_in[k][par], raised(16 * K_DMAS[k] * (i + 1)))
                pe.wait_ge(kt_ok[y % 2], raised(NTL // 2 * i + y // 2))
                for j in range(4):
                    mm = pe.transpose(tb[y % 2][:, j * P:(j + 1) * P], kc[k][:, par, n, j * P:(j + 1) * P], ident[:])
                mm.then_inc(k_turned, 1)

            def score(i, x, n):
                k, par = PASSES[x]
                y = tile[x, n]
                if n == 0:
                    pe.wait_ge(q_ok, raised(NP_ * i + x + 1))
                    pe.wait_ge(s_read, raised(NP_ * i + x + 1))
                pe.wait_ge(kt_ok[y % 2], raised(NTL // 2 * i + y // 2 + 1))
                for j in range(4):
                    mm = pe.matmul(sc[x % 2][:, 32 * n + QC * j:32 * n + QC * j + QC], kT[:, y % 2, j * P:(j + 1) * P],
                                   qd[:, x % 2, j], start=True, stop=True)
                mm.then_inc(k_used, 1)

            def score_new(i, x):
                pe.wait_ge(s_read, raised(NP_ * i + x + 2))
                for j in range(4):
                    mm = pe.matmul(scn[0:DEC_T, QC * j:QC * j + QC], kn[:, x % 2, j], qd[:, x % 2, j],
                                   start=True, stop=True)
                mm.then_inc(scored, 1)

            def turn_max(i, x):
                pe.wait_ge(max_part, raised(NP_ * i + x + 1))
                pe.transpose(misc[0:32, 0:P], mx[:], ident[:]).then_inc(max_turned, 1)

            def spread_max(i, x):
                pe.wait_ge(dg_ok, raised(NP_ * i + x + 1))
                pe.matmul(misc[:, 0:32], ones[0:32, :], dg[:], start=True, stop=True).then_inc(max_all, 1)

            def sums(i, x):
                pe.wait_ge(sum_ok, raised(NP_ * i + x + 1))
                pe.matmul(den[:, 0:32], ones[:], rs[:], start=True, stop=True).then_inc(den_ok, 1)

            def weigh(i, x):
                k, par = PASSES[x]
                pe.wait_ge(v_in[k][par], 16 * V_DMAS[k] * (i + 1))
                if x == 0:
                    pe.wait_ge(o_div, raised(NP_ * i))
                else:
                    pe.wait_ge(o_div, raised(NP_ * i + x))
                for j in range(4):
                    for n in range(TILES[k]):
                        pe.matmul(ob[:, QC * j:QC * j + QC], vc[k][:, par if k == "a" else 0, n, j * P:(j + 1) * P],
                                  pb[k][:, n, QC * j:QC * j + QC], start=n == 0, stop=False)
                    mm = pe.matmul(ob[:, QC * j:QC * j + QC], vn[k][:, par, j * P:(j + 1) * P],
                                   pb[k][0:DEC_T, TILES[k], QC * j:QC * j + QC], start=False, stop=True)
                mm.then_inc(pv, 1)

            with pe.Fori(0, N) as i:
                for x in range(NP_ + 1):
                    if x < NP_:
                        turn_k(i, x, 0)
                    for m, n in enumerate(at(x)):
                        if n is not None:
                            if n + 1 < len(at(x)):
                                turn_k(i, x, n + 1)
                            score(i, x, n)
                        if x > 0:
                            if m == TURN_MAX:
                                turn_max(i, x - 1)
                            if m == SPREAD_MAX:
                                spread_max(i, x - 1)
                            if m == SUMS:
                                sums(i, x - 1)
                    if x < NP_:
                        score_new(i, x)
                    if x > 0:
                        weigh(i, x - 1)
            pe.wait_ge(o_ok, raised(DEC_B * 2))
            for half in range(2):
                for c in range(4):
                    mm = pe.transpose(tb[half][0:NS, c * P:(c + 1) * P], oT[:, 4 * half + c], ident[:])
                mm.then_inc(fin_t, 1)

        @block.vector
        def _(dve):
            passed = s.sem("passed_dve")
            dve.wait_ge(const_in, raised(16 * 7))
            dve.wait_ge(zeroed, raised(4))

            def lay_queries(i, x):
                k, par = PASSES[x]
                f, tok = (0 if k == "a" else 4), ds((2 * i + par) * DEC_T, DEC_T)
                back = NP_ * i + x - 1
                if x >= 2:
                    dve.wait_ge(scored, raised(back))
                    dve.sem_inc(passed, 1)
                else:
                    dve.wait_ge(scored, raised(NP_ * i))
                    dve.sem_inc(passed, 1)
                for m in range(2):
                    dve.tensor_copy(qd[64 * m:64 * m + 64, x % 2, :, 4 * m:4 * m + 4], qs[64 * m:64 * m + 64, 0, f:f + 4, tok])
                dve.tensor_copy(kn[:, x % 2], qs[:, 1, f:f + 4, tok]).then_inc(q_ok, 1)

            def read_k(i, x, n):
                y = tile[x, n]
                if y % 2:
                    dve.wait_ge(k_used, raised(NTL * i + y + 1))
                    dve.wait_ge(k_turned, raised(NTL * i + y + 1))
                    dve.tensor_copy(kT[:, 1], tb[1][:]).then_inc(kt_ok[1], 1)

            def part_max(i, x):
                k = PASSES[x][0]
                T = TILES[k]
                dve.wait_ge(scored, raised(NP_ * i + x + 1))
                dve.tensor_tensor(sb_[k][:, 0:T], sc[x % 2][:, 0:32 * T].rearrange("p (n c) -> p n c", c=32),
                                  bias[k][:, 0:T], ALU.add)
                dve.tensor_tensor(sb_[k][0:DEC_T, T], scn[0:DEC_T, 0:32], bias[k][0:DEC_T, T], ALU.add).then_inc(s_read, 1)
                dve.wait_ge(s_read, raised(NP_ * i + x + 1 + 2))
                dve.tensor_reduce(mx[:], sb_[k][:].rearrange("p n c -> p c n"), AX.X, ALU.max).then_inc(max_part, 1)

            def row_max(i, x):
                dve.wait_ge(max_turned, raised(NP_ * i + x + 1))
                dve.tensor_reduce(mrow[:], misc[0:32, 0:P], AX.X, ALU.max).then_inc(max_row, 1)
                dve.wait_ge(max_row, raised(NP_ * i + x + 1))
                dve.tensor_scalar(dg[:], ident[0:32, 0:32], mrow[:], None, ALU.mult).then_inc(dg_ok, 1)

            def shift(i, x):
                k = PASSES[x][0]
                dve.wait_ge(max_all, raised(NP_ * i + x + 1))
                dve.tensor_tensor(sb_[k][:], sb_[k][:],
                                  misc[:, 0:32].rearrange("p (o c) -> p o c", o=1).to_broadcast([P, TILES[k] + 1, 32]),
                                  ALU.subtract).then_inc(shifted, 1)

            def sum_tiles(i, x):
                k = PASSES[x][0]
                dve.wait_ge(exp_ok, raised(NP_ * i + x + 1))
                if k == "b":
                    dve.tensor_tensor(pb[k][:], pb[k][:], count[:], ALU.mult).then_inc(weighed, 1)
                    dve.wait_ge(weighed, raised(NP_ // 2 * i + x // 2 + 1))
                dve.tensor_reduce(rs[:], pb[k][:].rearrange("p n c -> p c n"), AX.X, ALU.add).then_inc(sum_ok, 1)

            def invert(i, x):
                dve.wait_ge(den_ok, raised(NP_ * i + x + 1))
                dve.reciprocal(li[:], den[:, 0:32]).then_inc(li_ok, 1)

            def result(i, x):
                k, par = PASSES[x]
                tok = ds((2 * i + par) * DEC_T, DEC_T)
                dve.wait_ge(pv, raised(NP_ * i + x + 1))
                dve.wait_ge(li_ok, raised(NP_ * i + x + 1))
                dve.tensor_tensor(od[:], ob[:, 0:32].rearrange("p (j c) -> p j c", c=QC),
                                  li[:].rearrange("p (j c) -> p j c", c=QC), ALU.mult).then_inc(o_div, 1)
                dve.wait_ge(o_div, raised(NP_ * i + x + 1))
                if k == "a":
                    dve.scalar_tensor_tensor(oT[:, 0:4, tok], od[:, :, 4:8], nlam[:], od[:, :, 0:4],
                                             ALU.mult, ALU.add).then_inc(o_ok, 1)
                else:
                    dve.tensor_copy(oT[0:64, 4:8, tok], od[0:64, :, 0:4])
                    dve.tensor_copy(oT[64:P, 4:8, tok], od[64:P, :, 4:8]).then_inc(o_ok, 1)

            with dve.Fori(0, N) as i:
                lay_queries(i, 0)
                for x in range(NP_ + 1):
                    if x > 0:
                        part_max(i, x - 1)
                    for m, n in enumerate(at(x)):
                        if n is not None:
                            read_k(i, x, n)
                        if x > 0:
                            if m == TURN_MAX:
                                row_max(i, x - 1)
                            if m == SPREAD_MAX:
                                shift(i, x - 1)
                            if m == SUMS:
                                sum_tiles(i, x - 1)
                                invert(i, x - 1)
                    if x + 1 < NP_:
                        lay_queries(i, x + 1)
                    if x > 0:
                        result(i, x - 1)
            for half in range(2):
                dve.wait_ge(fin_t, raised(half + 1))
                dve.tensor_copy(rows[:, 4 * half:4 * half + 4],
                                tb[half][0:NS, :].rearrange("p (c x) -> p c x", c=4)).then_inc(fin_r, 1)

        @block.scalar
        def _(act):

            def read_k(i, x, n):
                y = tile[x, n]
                if y % 2 == 0:
                    act.wait_ge(k_used, raised(NTL * i + y + 1))
                    act.wait_ge(k_turned, raised(NTL * i + y + 1))
                    act.activation(kT[:, 0], tb[0][:], ACT.Copy).then_inc(kt_ok[0], 1)

            def expo(i, x):
                k = PASSES[x][0]
                act.wait_ge(shifted, raised(NP_ * i + x + 1))
                act.activation(pb[k][:], sb_[k][:], ACT.Exp).then_inc(exp_ok, 1)

            with act.Fori(0, N) as i:
                for x in range(NP_ + 1):
                    for m, n in enumerate(at(x)):
                        if n is not None:
                            read_k(i, x, n)
                        if x > 0 and m == EXPO:
                            expo(i, x - 1)
def mix(nc, t):
    with Stage(nc, "mx") as s:
        wr = s.sb("wr", [P, 2, D])
        wh = s.sb("wh", [P, DC, D], F32R)
        wl = s.sb("wl", [P, DC, D], F32R)
        st = s.sb("st", [P, NPAT, NT, 2 * B_HEADS])
        wg = s.sb("wg", [P, NPAT, NT, B_HEADS])
        wt = s.sb("wt", [P, NPAT, NT, B_HEADS])
        mm_ = s.sb("mm", [P, NT, B_HEADS])
        dn = s.sb("dn", [P, NT, B_HEADS])
        ob = s.sb("ob", [P, 2, NPAT, 512])
        cm = s.sb("cm", [P, 2, D])
        sq = s.sb("sq", [P, D])
        ss = s.sb("ss", [P, 2, 12])
        sd = s.sb("sd", [P, 2, 12])
        rs = s.sb("rs", [P, 2, 12])
        gmix = s.sb("gmix", [P, D])
        gpost = s.sb("gpost", [P, D])
        gffn = s.sb("gffn", [P, D])
        mTh = s.sb("mTh", [P, 2, DC, P], F32R)
        mTl = s.sb("mTl", [P, 2, DC, P], F32R)
        xt = s.sb("xt", [P, 2, D])
        zn = s.sb("zn", [P, D])
        x1 = s.sb("x1", [P, 2, D])
        h2 = s.sb("h2", [P, 2, D])
        hh = s.sb("hh", [P, 2, DC, P], F32R)
        hl = s.sb("hl", [P, 2, DC, P], F32R)
        zs = s.sb("zs", [P, 2, 2])
        z1 = s.sb("z1", [P, 8])
        eps = s.sb("eps", [P, 1])
        ident = s.sb("ident", [P, P])
        t1 = [s.ps(f"t1{i}") for i in range(2)]
        t2 = [s.ps(f"t2{i}") for i in range(2)]
        zb = [[s.ps(f"z{k}{h}") for h in range(2)] for k in range(2)]
        const_in, st_in, w_hi, w_lo, prep = (s.sem(n) for n in ("const_in", "st_in", "w_hi", "w_lo", "prep"))
        w_in = [s.sem(f"w_in{i}") for i in range(2)]
        mix_in = [s.sem(f"mix_in{i}") for i in range(2)]
        x_in = [s.sem(f"x_in{i}") for i in range(2)]
        x1_out = [s.sem(f"x1_out{i}") for i in range(2)]
        h_out = [s.sem(f"h_out{i}") for i in range(2)]
        (b_part, b_rest, b_sum, squared, ss_ok, sd_ok, rs_ok, scaled, mixed, turned, high, low, mul, z_sq, z_ss, z_sd,
         z_rs, z_ok, x1_ok, x_sq, x_sd, x_rs, h_ok, turned2, high2, low2) = (s.sem(n) for n in (
             "b_part", "b_rest", "b_sum", "squared", "ss_ok", "sd_ok", "rs_ok", "scaled", "mixed", "turned", "high",
             "low", "mul", "z_sq", "z_ss", "z_sd", "z_rs", "z_ok", "x1_ok", "x_sq", "x_sd", "x_rs", "h_ok",
             "turned2", "high2", "low2"))
        b_part2 = s.sem("b_part2")
        s.credit(low, 2)
        s.credit(low2, 2)
        block = s.block()
        LASTT = NT

        def pipeline(eng, slot):
            for n in (-1, 0, 1):
                slot(n, n % 2)
            with eng.Fori(1, NT // 2 - 1) as i:
                for k in range(2):
                    slot(2 * i + k, k)
            for n in range(NT - 2, LASTT + 3):
                slot(n, n % 2)

        def some(n):
            return not isinstance(n, int) or 0 <= n <= LASTT

        def rows_of(n):
            return NS if isinstance(n, int) and n == LASTT else P

        @block.sync
        def _(sp):
            passed = s.sem("passed_sp")
            for p in range(NPAT):
                sp.dma_start(st[:, p], t["stats"][p].rearrange("(b p) c -> p b c", p=P)).then_inc(st_in, 16)
            sp.dma_start(ident[:], t["c_ident"]).then_inc(const_in, 16)
            for h in range(A_HEADS):
                sp.dma_start(gmix[:, h * P:(h + 1) * P], t["subln_a"].partition_broadcast(P)).then_inc(const_in, 16)
            for h in range(B_HEADS):
                sp.dma_start(gmix[:, 512 + 64 * h:512 + 64 * h + 64],
                             t["norm_b_out"].partition_broadcast(P)).then_inc(const_in, 16)
            sp.dma_start(gpost[:], t["norm_mix_post"].partition_broadcast(P)).then_inc(const_in, 16)
            sp.dma_start(gffn[:], t["norm_ffn_pre"].partition_broadcast(P)).then_inc(const_in, 16)

            def load_mix(n, k):
                if isinstance(n, int) and n == LASTT:
                    sp.dma_start(cm[0:NS, k], t["s_mix"]).then_inc(mix_in[k], 16)
                    return
                rows = ds(n * P, P)
                sp.dma_start(cm[:, k, 0:512], t["oa"][rows, :]).then_inc(mix_in[k], 16)
                for p in range(NPAT):
                    sp.dma_start(ob[:, k, p], t["ob"][p][rows, :]).then_inc(mix_in[k], 16)

            def load_x(n, k):
                if isinstance(n, int) and n == LASTT:
                    sp.dma_start(xt[0:NS, k], t["x_sample"]).then_inc(x_in[k], 16)
                else:
                    sp.dma_start(xt[:, k], t["x_prompt"][ds(n * P, P), :]).then_inc(x_in[k], 16)

            load_mix(0, 0)
            for c in range(2):
                sp.dma_start(wr[:, c], t["w_out"][c * P:(c + 1) * P, :]).then_inc(w_in[c], 16)
            load_mix(1, 1)
            load_x(0, 0)
            load_x(1, 1)
            for c in range(2, DC):
                sp.wait_ge(w_lo, raised(c - 1))
                sp.dma_start(wr[:, c % 2], t["w_out"][c * P:(c + 1) * P, :]).then_inc(w_in[c % 2], 16)

            def slot(n, k):
                if some(n) and (not isinstance(n, int) or n + 2 <= LASTT):
                    sp.wait_ge(turned, raised(2 * n + 2))
                    sp.sem_inc(passed, 1)
                    load_mix(n + 2, k)
                m, km = n - 1, 1 - k
                if some(m):
                    sp.wait_ge(x1_ok, raised(m + 1))
                    sp.sem_inc(passed, 1)
                    r = rows_of(m)
                    at = slice(SEQ, TOK) if r == NS else ds(m * P, P)
                    sp.dma_start(t["x1"][at, :], x1[0:r, km]).then_inc(x1_out[km], 16)
                    if not isinstance(m, int) or m + 2 <= LASTT:
                        load_x(m + 2, km)
                m = n - 2
                if some(m):
                    sp.wait_ge(low2, raised(2 * m + 2 + 2))
                    sp.sem_inc(passed, 1)
                    r = rows_of(m)
                    at = slice(SEQ, TOK) if r == NS else ds(m * P, P)
                    for part, src in enumerate((hh, hl)):
                        sp.dma_start(t["h2T"][part][:, :, at], src[:, k, :, 0:r].bitcast(F32)).then_inc(h_out[k], 16)

            pipeline(sp, slot)
            for k in range(2):
                sp.wait_ge(x1_out[k], raised(16 * (9 - k)))
                sp.wait_ge(h_out[k], raised(32 * (9 - k)))

        def seen(n, k, each):
            if isinstance(n, int):
                return each * ((n - k) // 2 + 1)
            return each // 2 * (n - k) + each

        @block.gpsimd
        def _(pool):
            for c in range(DC):
                pool.wait_ge(w_hi, raised(c + 1))
                pool.tensor_tensor(wl[:, c], wr[:, c % 2], wh[:, c].bitcast(F32), ALU.subtract).then_inc(w_lo, 1)
            pool.wait_ge(prep, raised(9))

            def slot(n, k):
                m, km = n + 1, 1 - k
                if some(m):
                    r = rows_of(m)
                    if r == P:
                        pool.wait_ge(mix_in[km], raised(seen(m, km, 64)))
                        for p in (1, 2):
                            o = ob[:, km, p].rearrange("p (h e) -> p h e", h=B_HEADS)
                            last = pool.tensor_tensor(o, o, wg[:, p, ds(m, 1), :].rearrange("p o h -> p (o h)")
                                                      .rearrange("p (h o) -> p h o", o=1).to_broadcast([P, B_HEADS, 64]),
                                                      ALU.mult)
                        last.then_inc(b_part, 1)
                        pool.wait_ge(b_part, raised(m + 1))
                        pool.tensor_tensor(ob[:, km, 1], ob[:, km, 1], ob[:, km, 2], ALU.add).then_inc(b_rest, 1)
                    pool.wait_ge(scaled, raised(m + 1))
                    pool.tensor_tensor(cm[0:r, km], cm[0:r, km], gmix[0:r], ALU.mult).then_inc(mixed, 1)
                m = n - 1
                if some(m):
                    r = rows_of(m)
                    pool.wait_ge(z_ok, raised(m + 1))
                    pool.wait_ge(x_in[km], raised(seen(m, km, 16)))
                    if not isinstance(m, int) or m >= 2:
                        pool.wait_ge(x1_out[km], raised(seen(m - 2, km, 16)))
                    pool.tensor_tensor(x1[0:r, km], zn[0:r], xt[0:r, km], ALU.add).then_inc(x1_ok, 1)

            pipeline(pool, slot)

        @block.scalar
        def _(act):
            act.wait_ge(prep, raised(4))
            act.activation(wt[:], wt[:], ACT.Exp).then_inc(prep, 1)
            for c in range(DC):
                act.wait_ge(w_in[c % 2], raised(16 * (c // 2 + 1)))
                act.activation(wh[:, c], wr[:, c % 2], ACT.Copy).then_inc(w_hi, 1)

            def slot(n, k):
                if some(n):
                    r = rows_of(n)
                    if not isinstance(n, int) or n >= 2:
                        act.wait_ge(mul, raised(n - 1))
                    for half in range(2):
                        act.wait_ge(turned, raised(2 * n + half + 1))
                        act.activation(mTh[:, k, 4 * half:4 * half + 4, 0:r],
                                       t1[half][:].rearrange("p (c x) -> p c x", c=4)[:, :, 0:r],
                                       ACT.Copy).then_inc(high, 1)
                m, km = n + 1, 1 - k
                if some(m):
                    r = rows_of(m)
                    act.wait_ge(b_sum, raised(m + 1))
                    if r == NS:
                        act.wait_ge(mix_in[km], raised(64 * 8 + 16))
                    act.activation(sq[0:r], cm[0:r, km], ACT.Square).then_inc(squared, 1)
                    act.wait_ge(ss_ok, raised(m + 1))
                    act.activation(sd[0:r, km, 0:4], ss[0:r, km, 0:4], ACT.Sqrt, scale=1.0 / P, bias=eps[0:r])
                    act.activation(sd[0:r, km, 4:12], ss[0:r, km, 4:12], ACT.Sqrt, scale=1.0 / 64,
                                   bias=eps[0:r]).then_inc(sd_ok, 1)
                m = n - 1
                if some(m):
                    r = rows_of(m)
                    act.wait_ge(mul, raised(m + 1))
                    for half in range(2):
                        last = act.activation(sq[0:r, 512 * half:512 * half + 512], zb[km][half][0:r, :], ACT.Square,
                                              accum_out=zs[0:r, km, half:half + 1])
                    last.then_inc(z_sq, 1)
                    act.wait_ge(z_ss, raised(m + 1))
                    act.activation(z1[0:r, 1:2], z1[0:r, 0:1], ACT.Sqrt, scale=1.0 / D, bias=eps[0:r]).then_inc(z_sd, 1)
                    act.wait_ge(x1_ok, raised(m + 1))
                    act.activation(sq[0:r], x1[0:r, km], ACT.Square, accum_out=z1[0:r, 3:4]).then_inc(x_sq, 1)
                    act.wait_ge(x_sq, raised(m + 1))
                    act.activation(z1[0:r, 4:5], z1[0:r, 3:4], ACT.Sqrt, scale=1.0 / D, bias=eps[0:r]).then_inc(x_sd, 1)
                m = n - 2
                if some(m):
                    r = rows_of(m)
                    if not isinstance(m, int) or m >= 2:
                        act.wait_ge(h_out[k], raised(seen(m - 2, k, 32)))
                    for half in range(2):
                        act.wait_ge(turned2, raised(2 * m + half + 1))
                        act.activation(hh[:, k, 4 * half:4 * half + 4, 0:r],
                                       t2[half][:].rearrange("p (c x) -> p c x", c=4)[:, :, 0:r],
                                       ACT.Copy).then_inc(high2, 1)

            pipeline(act, slot)

        @block.vector
        def _(dve):
            dve.memset(eps[:], EPS).then_inc(prep, 1)
            st5 = st[:].rearrange("p n b (h k) -> p n b h k", k=2)
            m_, l_ = st5[:, :, :, :, 0], st5[:, :, :, :, 1]
            dve.wait_ge(st_in, raised(16 * NPAT))
            dve.tensor_tensor(mm_[:], m_[:, 0], m_[:, 1], ALU.max).then_inc(prep, 1)
            dve.wait_ge(prep, raised(2))
            dve.tensor_tensor(mm_[:], mm_[:], m_[:, 2], ALU.max).then_inc(prep, 1)
            dve.wait_ge(prep, raised(3))
            for p in range(NPAT):
                last = dve.tensor_tensor(wt[:, p], m_[:, p], mm_[:], ALU.subtract)
            last.then_inc(prep, 1)
            dve.wait_ge(prep, raised(5))
            for p in range(NPAT):
                last = dve.tensor_tensor(wg[:, p], wt[:, p], l_[:, p], ALU.mult)
            last.then_inc(prep, 1)
            dve.wait_ge(prep, raised(6))
            dve.tensor_reduce(dn[:], wg[:].rearrange("p n b h -> p b h n"), AX.X, ALU.add).then_inc(prep, 1)
            dve.wait_ge(prep, raised(7))
            dve.reciprocal(dn[:], dn[:]).then_inc(prep, 1)
            dve.wait_ge(prep, raised(8))
            for p in range(NPAT):
                last = dve.tensor_tensor(wg[:, p], wt[:, p], dn[:], ALU.mult)
            dve.wait_ge(const_in, raised(16 * (1 + A_HEADS + B_HEADS + 2)))
            dve.tensor_scalar(gmix[:, 0:512], gmix[:, 0:512], 1.0 - LAM_INIT, None, ALU.mult).then_inc(prep, 1)
            dve.wait_ge(prep, raised(9))

            def slot(n, k):
                if some(n):
                    r = rows_of(n)
                    for half in range(2):
                        dve.wait_ge(high, raised(2 * n + half + 1))
                        dve.tensor_tensor(mTl[:, k, 4 * half:4 * half + 4, 0:r],
                                          t1[half][:].rearrange("p (c x) -> p c x", c=4)[:, :, 0:r],
                                          mTh[:, k, 4 * half:4 * half + 4, 0:r].bitcast(F32),
                                          ALU.subtract).then_inc(low, 1)
                m, km = n + 1, 1 - k
                if some(m):
                    r = rows_of(m)
                    if r == P:
                        dve.wait_ge(mix_in[km], raised(seen(m, km, 64)))
                        o = ob[:, km, 0].rearrange("p (h e) -> p h e", h=B_HEADS)
                        w = wg[:, 0, ds(m, 1), :].rearrange("p o h -> p (o h)").rearrange("p (h o) -> p h o", o=1)
                        dve.tensor_tensor(o, o, w.to_broadcast([P, B_HEADS, 64]), ALU.mult).then_inc(b_part2, 1)
                        dve.wait_ge(b_part2, raised(m + 1))
                        dve.wait_ge(b_rest, raised(m + 1))
                        dve.tensor_tensor(cm[:, km, 512:D], ob[:, km, 0], ob[:, km, 1], ALU.add).then_inc(b_sum, 1)
                    else:
                        dve.sem_inc(b_sum, 1)
                    dve.wait_ge(squared, raised(m + 1))
                    dve.tensor_reduce(ss[0:r, km, 0:4], sq[0:r, 0:512].rearrange("p (h e) -> p h e", h=A_HEADS), AX.X, ALU.add)
                    dve.tensor_reduce(ss[0:r, km, 4:12], sq[0:r, 512:D].rearrange("p (h e) -> p h e", h=B_HEADS), AX.X,
                                      ALU.add).then_inc(ss_ok, 1)
                    dve.wait_ge(sd_ok, raised(m + 1))
                    dve.reciprocal(rs[0:r, km], sd[0:r, km]).then_inc(rs_ok, 1)
                    dve.wait_ge(rs_ok, raised(m + 1))
                    for c0, c1, heads, r0 in ((0, 512, A_HEADS, 0), (512, D, B_HEADS, 4)):
                        e = (c1 - c0) // heads
                        y = cm[0:r, km, c0:c1].rearrange("p (h e) -> p h e", h=heads)
                        last = dve.tensor_tensor(y, y, rs[0:r, km, r0:r0 + heads].rearrange("p (h o) -> p h o", o=1)
                                                 .to_broadcast([r, heads, e]), ALU.mult)
                    last.then_inc(scaled, 1)
                m = n - 1
                if some(m):
                    r = rows_of(m)
                    dve.wait_ge(z_sq, raised(m + 1))
                    dve.tensor_tensor(z1[0:r, 0:1], zs[0:r, km, 0:1], zs[0:r, km, 1:2], ALU.add).then_inc(z_ss, 1)
                    dve.wait_ge(z_sd, raised(m + 1))
                    dve.reciprocal(z1[0:r, 2:3], z1[0:r, 1:2]).then_inc(z_rs, 1)
                    dve.wait_ge(z_rs, raised(m + 1))
                    if not isinstance(m, int) or m >= 1:
                        dve.wait_ge(x1_ok, raised(m))
                    for half in range(2):
                        c = slice(512 * half, 512 * half + 512)
                        last = dve.scalar_tensor_tensor(zn[0:r, c], zb[km][half][0:r, :], z1[0:r, 2:3], gpost[0:r, c],
                                                        ALU.mult, ALU.mult)
                    last.then_inc(z_ok, 1)
                    dve.wait_ge(x_sd, raised(m + 1))
                    dve.reciprocal(z1[0:r, 5:6], z1[0:r, 4:5]).then_inc(x_rs, 1)
                    dve.wait_ge(x_rs, raised(m + 1))
                    if not isinstance(m, int) or m >= 2:
                        dve.wait_ge(turned2, raised(2 * m - 2))
                    dve.scalar_tensor_tensor(h2[0:r, km], x1[0:r, km], z1[0:r, 5:6], gffn[0:r],
                                             ALU.mult, ALU.mult).then_inc(h_ok, 1)
                m = n - 2
                if some(m):
                    r = rows_of(m)
                    for half in range(2):
                        dve.wait_ge(high2, raised(2 * m + half + 1))
                        dve.tensor_tensor(hl[:, k, 4 * half:4 * half + 4, 0:r],
                                          t2[half][:].rearrange("p (c x) -> p c x", c=4)[:, :, 0:r],
                                          hh[:, k, 4 * half:4 * half + 4, 0:r].bitcast(F32),
                                          ALU.subtract).then_inc(low2, 1)

            pipeline(dve, slot)

        @block.tensor
        def _(pe):
            pe.wait_ge(const_in, raised(16 * (1 + A_HEADS + B_HEADS + 2)))

            def turn(src, k, dst, r, done_, low_, n):
                for half in range(2):
                    pe.wait_ge(low_, raised(2 * n + half + 1))
                    for c in range(4):
                        cc = 4 * half + c
                        last = pe.transpose(dst[half][:, c * P:c * P + r], src[0:r, k, cc * P:(cc + 1) * P],
                                            ident[0:r, 0:r])
                    last.then_inc(done_, 1)

            def slot(n, k):
                km = 1 - k
                if some(n):
                    pe.wait_ge(mixed, raised(n + 1))
                    turn(cm, k, t1, rows_of(n), turned, low, n)
                m = n - 1
                if some(m):
                    r = rows_of(m)
                    pe.wait_ge(low, raised(2 * m + 2 + 2))
                    if isinstance(m, int) and m == 0:
                        pe.wait_ge(w_lo, raised(DC))
                    if not isinstance(m, int) or m >= 2:
                        pe.wait_ge(z_ok, raised(m - 1))
                    for c in range(DC):
                        for x, (a, b) in enumerate(((mTh, wh), (mTh, wl), (mTl, wh))):
                            for half in range(2):
                                last = pe.matmul(zb[km][half][0:r, :], a[:, km, c, 0:r], b[:, c, 512 * half:512 * half + 512],
                                                 start=c == 0 and x == 0, stop=c == DC - 1 and x == 2)
                    last.then_inc(mul, 1)
                m = n - 2
                if some(m):
                    pe.wait_ge(h_ok, raised(m + 1))
                    turn(h2, k, t2, rows_of(m), turned2, low2, m)

            pipeline(pe, slot)
TAPS = 3
SLOTS = 4
D_PARTS = [6, 6, 5, 5]
HEAD = 4


def ffn(nc, t):
    with Stage(nc, "ff") as s:
        hh = s.sb("hh", [P, 2, DC, GRP], F32R)
        hs = s.sb("hs", [P, 2, DC, NS], F32R)
        wr = s.sb("wr", [P, SLOTS, DC, P])
        wh = s.sb("wh", [P, 2, DC, P], F32R)
        wl = s.sb("wl", [P, 2, DC, P], F32R)
        ah = s.sb("ah", [P, FT, GRP], F32R)
        al = s.sb("al", [P, FT, GRP], F32R)
        sh = s.sb("sh", [P, FT, NS], F32R)
        sl = s.sb("sl", [P, FT, NS], F32R)
        gb = s.sb("gb", [P, 2, GRP + 2])
        gs = s.sb("gs", [P, 2, DEC_B, DEC_T + 2])
        ca = s.sb("ca", [P, GRP])
        cb = s.sb("cb", [P, GRP])
        sa = s.sb("sa", [P, 2, NS])
        sb2 = s.sb("sb2", [P, 2, NS])
        carry = s.sb("carry", [P, FT, 2])
        tail = s.sb("tail", [P, FT, DEC_B, 2])
        cw = s.sb("cw", [P, TAPS + 1, FT])
        yT = s.sb("yT", [P, GRP])
        yTs = s.sb("yTs", [P, NS])
        yn = s.sb("yn", [P, TPG, D])
        ys = s.sb("ys", [NS, D])
        xt = s.sb("xt", [P, D])
        gain = s.sb("gain", [P, D])
        junk = s.sb("junk", [P, 512])
        s4 = s.sb("s4", [P, 5, 8])
        eps = s.sb("eps", [P, 1])
        ident = s.sb("ident", [P, P])
        gp = [s.ps(f"g{i}") for i in range(2)]
        up = [s.ps(f"u{i}") for i in range(2)]
        dp = [s.ps(f"d{i}") for i in range(2)]
        tp = [s.ps(f"t{i}") for i in range(2)]
        const_in, prep, pre_t, pre_r = (s.sem(n) for n in ("const_in", "prep", "pre_t", "pre_r"))
        w_in = [s.sem(f"w_in{i}") for i in range(SLOTS)]
        h_in, hs_in = s.sem("h_in"), s.sem("hs_in")
        x_in = s.soft_sem("x_in")
        y_out, y_sent, last_out = s.soft_sem("y_out"), s.sem("y_sent"), s.sem("last_out")
        (w_hi, w_lo, mm, g_read, conv1, conv2, conv_ok, gelu_ok, a_ok, a_hi, a_lo, d_read, y_turned, y_ok, y_sq, y_sum,
         y_sd, y_rs, y_norm, y_add, gs_read, cs1, cs2, convs_ok, gelus_ok, as_ok, as_hi, as_lo, ds_read, fin_t, fin_r) = (
            s.sem(n) for n in (
                "w_hi", "w_lo", "mm", "g_read", "conv1", "conv2", "conv_ok", "gelu_ok", "a_ok", "a_hi", "a_lo",
                "d_read", "y_turned", "y_ok", "y_sq", "y_sum", "y_sd", "y_rs", "y_norm", "y_add", "gs_read", "cs1",
                "cs2", "convs_ok", "gelus_ok", "as_ok", "as_hi", "as_lo", "ds_read", "fin_t", "fin_r"))
        carried, carried_s, y_half = s.sem("carried"), s.sem("carried_s"), s.sem("y_half")
        s.credit(mm, 2)
        s.credit(w_lo, SLOTS)
        s.credit(g_read, 2)
        s.credit(d_read, 2)
        s.credit(gs_read, 1)
        s.credit(ds_read, 2)
        s.credit(conv_ok, 1)
        s.credit(convs_ok, 1)
        s.credit(a_ok, 2)
        s.credit(as_ok, 1)
        s.credit(y_ok, 2)
        block = s.block()
        UNITS = 2 * FT + SLOTS * DC
        wg_view = t["w_gate"].rearrange("(c p) f -> p c f", p=P)
        wu_view = t["w_up"].rearrange("(c p) f -> p c f", p=P)
        wd_view = t["w_down"].rearrange("(c p) f -> p c f", p=P)

        def groups(eng, f_tile, d_tile, beside, d_first=lambda g: None):
            def head(g, last):
                for f in range(HEAD):
                    f_tile(g, f, f % 2, DC, last)
                    if not isinstance(g, int) or g > 0:
                        beside(g - 1, f, False)

            def rest(g, last):
                with eng.Fori(HEAD // 2, FT // 2 - 1) as i:
                    for k in range(2):
                        f_tile(g, 2 * i + k, k, DC, last)
                f_tile(g, FT - 2, 0, DC, last)
                f_tile(g, FT - 1, 1, D_PARTS[0], last)
                d_tile(g, 0, 0, D_PARTS[0], last)
                if not last:
                    d_first(g)
                d_tile(g, 1, 1, D_PARTS[0], last)
                with eng.Fori(1, DC // 2 - 1) as i:
                    for k in range(2):
                        d_tile(g, 2 * i + k, k, D_PARTS[0], last)
                d_tile(g, DC - 2, 0, D_PARTS[0], last)
                d_tile(g, DC - 1, 1, 0 if last else DC, last)

            head(0, False)
            with eng.Fori(0, NG - 2) as g:
                rest(g, False)
                head(g + 1, False)
            rest(NG - 2, False)
            head(NG - 1, True)
            rest(NG - 1, True)
            for f in range(HEAD):
                beside(NG - 1, f, True)

        @block.sync
        def _(sp):
            passed = s.sem("passed_sp")
            sp.dma_start(ident[:], t["c_ident"]).then_inc(const_in, 16)
            sp.dma_start(junk[0:TAPS * FT, 0:P], t["w_conv"].rearrange("j (f p) -> (j f) p", p=P)).then_inc(const_in, 16)
            sp.dma_start(junk[TAPS * FT:(TAPS + 1) * FT, 0:P], t["b_conv"].rearrange("(f p) -> f p", p=P)).then_inc(const_in, 16)
            sp.dma_start(gain[:], t["norm_ffn_post"].partition_broadcast(P)).then_inc(const_in, 16)
            sp.dma_start(yn[0:2 * DEC_B].rearrange("p a d -> p (a d)")[:, 0:D_FF], t["state_conv"]).then_inc(const_in, 16)
            for part in range(2):
                sp.dma_start(hs[:, part].bitcast(F32), t["h2T"][part][:, :, SEQ:TOK]).then_inc(hs_in, 16)

            def load_w(n, slot, src):
                sp.wait_ge(w_lo, raised(n + 1))
                sp.sem_inc(passed, 1)
                sp.dma_start(wr[:, slot, 0:src.shape[1]], src).then_inc(w_in[slot], 16)

            def f_tile(g, f, k, after, last):
                n = UNITS * g + 2 * f
                load_w(n, 2 * k, wg_view[:, :, ds(f * P, P)])
                load_w(n + 1, 2 * k + 1, wu_view[:, :, ds(f * P, P)])

            def d_tile(g, d, k, after, last):
                n = UNITS * g + 2 * FT + SLOTS * d
                for j, size in enumerate(D_PARTS):
                    c0 = sum(D_PARTS[:j])
                    load_w(n + j, j, wd_view[:, c0:c0 + size, ds(d * P, P)])

            def load_h(g):
                sp.wait_ge(mm, raised(UNITS * g + 2 * FT + 2))
                sp.sem_inc(passed, 1)
                for part in range(2):
                    sp.dma_start(hh[:, part].bitcast(F32), t["h2T"][part][:, :, ds((g + 1) * GRP, GRP)]).then_inc(h_in, 16)

            for part in range(2):
                sp.dma_start(hh[:, part].bitcast(F32), t["h2T"][part][:, :, 0:GRP]).then_inc(h_in, 16)
            groups(sp, f_tile, d_tile, lambda g, f, last: None, load_h)
            sp.wait_ge(fin_r, raised((FT + 3) // 4))
            flat = yn[:].rearrange("p a d -> p (a d)")
            sp.dma_start(t["conv_prompt"], flat[0:2, 0:D_FF]).then_inc(last_out, 16)
            sp.dma_start(t["conv_sample"], flat[32:32 + 2 * DEC_B, 0:D_FF]).then_inc(last_out, 16)
            sp.wait_ge(last_out, raised(32))

        @block.gpsimd
        def _(pool):
            passed = s.sem("passed_pool")
            pool.memset(carry[:], 0.0).then_inc(prep, 1)
            def place(g, b):
                r = P if b < TPG else NS
                return r, (yn[:, b] if b < TPG else ys[:]), TPG * g + b, (
                    ds((TPG * g + b) * P, P) if b < TPG else slice(SEQ, TOK))

            def load_x(g, b):
                r, y, n, at = place(g, b)
                pool.dma_start(xt[0:r], t["x1"][at, :]).then_inc(x_in, 16)

            def add_rest(g, last):
                load_x(g, 0)
                for b in range(TPG + last):
                    r, y, n, at = place(g, b)
                    pool.wait_ge(y_norm, raised(n + 1))
                    pool.wait_ge(x_in, 16 * (n + 1))
                    pool.tensor_tensor(y, y, xt[0:r], ALU.add).then_inc(y_add, 1)
                    pool.wait_ge(y_add, raised(n + 1))
                    pool.sem_inc(passed, 1)
                    dst = t["y_prompt"][at, :] if b < TPG else t["y_sample"]
                    pool.dma_start(dst, y).then_inc(y_out, 16)
                    if b + 1 < TPG + last:
                        load_x(g, b + 1)
                pool.wait_ge(y_out, 16 * (TPG * (g + 1) + last))
                pool.sem_inc(passed, 1)
                pool.sem_inc(y_sent, 1)

            with pool.Fori(0, NG - 1) as g:
                add_rest(g, False)
            add_rest(NG - 1, True)

        @block.tensor
        def _(pe):
            pe.wait_ge(const_in, raised(16 * 5))
            pe.transpose(tp[0][:, 0:(TAPS + 1) * FT], junk[0:(TAPS + 1) * FT, 0:P],
                         ident[0:(TAPS + 1) * FT, 0:(TAPS + 1) * FT]).then_inc(pre_t, 1)
            old = yn[0:2 * DEC_B].rearrange("p a d -> p (a d)")
            for f in range(FT):
                m = pe.transpose(tp[1][:, f * 16:f * 16 + 16], old[:, f * P:(f + 1) * P], ident[0:16, 0:16])
            m.then_inc(pre_t, 1)

            def products(n, k, dst, c0, size, src, dst_s, src_s, first, stop_, last):
                for c in range(size):
                    for x, (w, part) in enumerate(((wh, 0), (wh, 1), (wl, 0))):
                        a, b = first and c == 0 and x == 0, stop_ and c == size - 1 and x == 2
                        m = pe.matmul(dst[:], w[:, k, c], src[part][:, c0 + c], start=a, stop=b)
                        if last:
                            m = pe.matmul(dst_s[:, 0:NS], w[:, k, c], src_s[part][:, c0 + c], start=a, stop=b)
                m.then_inc(mm, 1)

            def f_tile(g, f, k, after, last):
                n = UNITS * g + 2 * f
                if isinstance(f, int) and f == 0:
                    pe.wait_ge(h_in, raised(32 * (g + 1)))
                if last:
                    pe.wait_ge(hs_in, raised(32))
                pe.wait_ge(w_lo, raised(n + 1 + SLOTS))
                pe.wait_ge(g_read, raised(FT * g + f + 1))
                if last:
                    pe.wait_ge(gs_read, raised(f + 1))
                    pe.wait_ge(y_ok, raised(DC * g + 2))
                products(n, 0, gp[k], 0, DC, (hh[:, 0], hh[:, 1]), tp[0], (hs[:, 0], hs[:, 1]), True, True, last)
                pe.wait_ge(w_lo, raised(n + 2 + SLOTS))
                pe.wait_ge(a_ok, raised(FT * g + f + 1))
                if last:
                    pe.wait_ge(as_ok, raised(f + 1))
                products(n + 1, 1, up[k], 0, DC, (hh[:, 0], hh[:, 1]), tp[1], (hs[:, 0], hs[:, 1]), True, True, last)

            def d_tile(g, d, k, after, last):
                n = UNITS * g + 2 * FT + SLOTS * d
                pe.wait_ge(a_lo, raised(FT * (g + 1)))
                pe.wait_ge(d_read, raised(DC * g + d + 1))
                if last:
                    pe.wait_ge(as_lo, raised(FT))
                    pe.wait_ge(g_read, raised(FT * (g + 1) + 2))
                    pe.wait_ge(ds_read, raised(d + 1))
                for j, size in enumerate(D_PARTS):
                    pe.wait_ge(w_lo, raised(n + j + 1 + SLOTS))
                    products(n + j, j % 2, dp[k], sum(D_PARTS[:j]), size, (ah, al), gp[k], (sh, sl), j == 0,
                             j == SLOTS - 1, last)
                    if j == 0 and not (isinstance(d, int) and d == 0):
                        turn_back(g, d - 1, 1 - k, last)
                if isinstance(d, int) and d == DC - 1:
                    turn_back(g, d, k, last)

            def turn_back(g, d, k, last):
                pe.wait_ge(d_read, raised(DC * g + d + 1 + 2))
                pe.wait_ge(y_ok, raised(DC * g + d + 1))
                for b in range(TPG):
                    m = pe.transpose(tp[k][:, b * P:(b + 1) * P], yT[:, b * P:(b + 1) * P], ident[:])
                if last:
                    pe.wait_ge(ds_read, raised(d + 1 + 2))
                    m = pe.transpose(up[k][0:NS, 0:P], yTs[:], ident[:])
                m.then_inc(y_turned, 1)

            groups(pe, f_tile, d_tile, lambda g, f, last: None)
            pe.wait_ge(y_ok, raised(DC * NG + 2))
            pe.wait_ge(g_read, raised(2 + FT * NG))
            for f in range(FT):
                if f % 4 == 0 and f >= 8:
                    pe.wait_ge(fin_r, raised(f // 4 - 1))
                bank = (gp, up)[f // 4 % 2][0]
                pe.transpose(bank[0:2, (f % 4) * P:(f % 4 + 1) * P], carry[:, f], ident[:])
                m = pe.transpose((gp, up)[f // 4 % 2][1][0:2 * DEC_B, (f % 4) * P:(f % 4 + 1) * P],
                                 tail[:, f].rearrange("p b j -> p (b j)"), ident[:])
                if f % 4 == 3 or f == FT - 1:
                    m.then_inc(fin_t, 1)

        @block.scalar
        def _(act):

            def weights_high(n, slot, size):
                if size:
                    act.wait_ge(w_in[slot], raised(16 // SLOTS * (n - slot) + 16))
                    act.wait_ge(mm, raised(n + 1))
                    act.activation(wh[:, slot % 2, 0:size], wr[:, slot, 0:size], ACT.Copy).then_inc(w_hi, 1)

            weights_high(0, 0, DC)
            weights_high(1, 1, DC)

            def f_tile(g, f, k, after, last):
                n, q = UNITS * g + 2 * f, FT * g + f
                weights_high(n + 2, (2 * k + 2) % SLOTS, after)
                act.wait_ge(mm, raised(n + 1 + 2))
                act.wait_ge(conv_ok, raised(q))
                act.activation(gb[:, k, 2:], gp[k][:], ACT.Copy).then_inc(g_read, 1)
                if last:
                    act.wait_ge(convs_ok, raised(f))
                    act.activation(gs[:, k, :, 2:], tp[0][:, 0:NS].rearrange("p (b j) -> p b j", b=DEC_B),
                                   ACT.Copy).then_inc(gs_read, 1)
                act.wait_ge(conv_ok, raised(q + 1 + 1))
                act.activation(ca[:], ca[:], ACT.Gelu_apprx_tanh).then_inc(gelu_ok, 1)
                if last:
                    act.wait_ge(convs_ok, raised(f + 1 + 1))
                    act.activation(sa[:, k], sa[:, k], ACT.Gelu_apprx_tanh).then_inc(gelus_ok, 1)
                weights_high(n + 3, (2 * k + 3) % SLOTS, after)

            def d_tile(g, d, k, after, last):
                n, q = UNITS * g + 2 * FT + SLOTS * d, DC * g + d
                weights_high(n + 2, 2, D_PARTS[2])
                weights_high(n + 3, 3, D_PARTS[3])
                weights_high(n + 4, 0, after)
                weights_high(n + 5, 1, after)
                act.wait_ge(mm, raised(n + SLOTS + 2))
                act.wait_ge(y_turned, raised(q))
                act.activation(yT[:], dp[k][:], ACT.Copy).then_inc(d_read, 1)
                if last:
                    act.activation(yTs[:], gp[k][:, 0:NS], ACT.Copy).then_inc(ds_read, 1)

            def beside(g, f, last):
                if f > 0:
                    return
                act.wait_ge(y_ok, raised(DC * (g + 1) + 2))
                for b in range(TPG + last):
                    r = P if b < TPG else NS
                    y = yn[:, b] if b < TPG else ys[:]
                    n = TPG * g + b
                    if b > 0:
                        act.wait_ge(y_sq, raised(n))
                    else:
                        act.wait_ge(y_norm, raised(TPG * g))
                    for half in range(2):
                        if half:
                            act.wait_ge(y_half, raised(n + 1))
                        m = act.activation(junk[0:r], y[:, 512 * half:512 * half + 512], ACT.Square,
                                           accum_out=s4[0:r, b, half:half + 1])
                        m.then_inc(y_sq if half else y_half, 1)
                for b in range(TPG + last):
                    r = P if b < TPG else NS
                    n = TPG * g + b
                    act.wait_ge(y_sum, raised(n + 1))
                    act.activation(s4[0:r, b, 3:4], s4[0:r, b, 2:3], ACT.Sqrt, scale=1.0 / D, bias=eps[0:r]).then_inc(y_sd, 1)

            groups(act, f_tile, d_tile, beside)

        @block.vector
        def _(dve):
            passed = s.sem("passed_dve")
            dve.memset(eps[:], EPS)
            dve.wait_ge(prep, raised(1))
            dve.wait_ge(pre_t, raised(1))
            dve.tensor_copy(cw[:], tp[0][:, 0:(TAPS + 1) * FT].rearrange("p (j f) -> p j f", f=FT)).then_inc(pre_r, 1)
            dve.wait_ge(pre_t, raised(2))
            dve.tensor_copy(tail[:], tp[1][:, 0:FT * 16].rearrange("p (f b j) -> p f b j", f=FT, b=DEC_B)).then_inc(pre_r, 1)
            dve.wait_ge(pre_r, raised(2))

            def tap(j, f):
                return cw[:, j, ds(f, 1)]

            def weights_low(n, slot, size):
                if size:
                    dve.wait_ge(w_hi, raised(n + 1))
                    dve.tensor_tensor(wl[:, slot % 2, 0:size], wr[:, slot, 0:size], wh[:, slot % 2, 0:size].bitcast(F32),
                                       ALU.subtract).then_inc(w_lo, 1)

            weights_low(0, 0, DC)
            weights_low(1, 1, DC)

            def convolve(src, a, b, f, first, second, done_, q, w, c0):
                dve.tensor_scalar(a, src(0), tap(0, f), tap(TAPS, f), ALU.mult, ALU.add).then_inc(first, 1)
                dve.wait_ge(first, raised(q + 1))
                dve.scalar_tensor_tensor(b, src(1), tap(1, f), a, ALU.mult, ALU.add).then_inc(second, 1)
                dve.wait_ge(second, raised(q + 1))
                dve.scalar_tensor_tensor(a, src(2), tap(2, f), b, ALU.mult, ALU.add).then_inc(done_, 1)

            def f_tile(g, f, k, after, last):
                q = FT * g + f
                n = UNITS * g + 2 * f
                weights_low(n + 2, (2 * k + 2) % SLOTS, after)
                dve.tensor_copy(gb[:, k, 0:2], carry[:, ds(f, 1), :].rearrange("p o j -> p (o j)")).then_inc(carried, 1)
                dve.wait_ge(g_read, raised(q + 1 + 2))
                dve.wait_ge(carried, raised(2 * q + 1))
                convolve(lambda j: gb[:, k, j:j + GRP], ca[:], cb[:], f, conv1, conv2, conv_ok, q, GRP, 0)
                dve.tensor_copy(carry[:, ds(f, 1), :].rearrange("p o j -> p (o j)"), gb[:, k, GRP:]).then_inc(carried, 1)
                if last:
                    shape = lambda x: x[:, k].rearrange("p (b j) -> p b j", b=DEC_B)
                    dve.tensor_copy(gs[:, k, :, 0:2], tail[:, ds(f, 1)].rearrange("p o b j -> p (o b) j")).then_inc(carried_s, 1)
                    dve.wait_ge(gs_read, raised(f + 1 + 1))
                    dve.wait_ge(carried_s, raised(2 * f + 1))
                    convolve(lambda j: gs[:, k, :, j:j + DEC_T], shape(sa), shape(sb2), f, cs1, cs2, convs_ok, f, NS, 0)
                    dve.tensor_copy(tail[:, ds(f, 1)].rearrange("p o b j -> p (o b) j"), gs[:, k, :, DEC_T:]).then_inc(carried_s, 1)
                weights_low(n + 3, (2 * k + 3) % SLOTS, after)
                dve.wait_ge(mm, raised(UNITS * g + 2 * f + 2 + 2))
                dve.wait_ge(gelu_ok, raised(q + 1))
                dve.tensor_tensor(cb[:], ca[:], up[k][:], ALU.mult).then_inc(a_ok, 1)
                dve.wait_ge(a_ok, raised(q + 1 + 2))
                dve.sem_inc(passed, 1)
                hi = ah[:, ds(f, 1), :].rearrange("p o x -> p (o x)")
                dve.tensor_copy(hi, cb[:]).then_inc(a_hi, 1)
                dve.wait_ge(a_hi, raised(q + 1))
                dve.tensor_tensor(al[:, ds(f, 1), :].rearrange("p o x -> p (o x)"), cb[:], hi.bitcast(F32),
                                  ALU.subtract).then_inc(a_lo, 1)
                if last:
                    dve.wait_ge(gelus_ok, raised(f + 1))
                    dve.tensor_tensor(sb2[:, k], sa[:, k], tp[1][:, 0:NS], ALU.mult).then_inc(as_ok, 1)
                    dve.wait_ge(as_ok, raised(f + 1 + 1))
                    dve.sem_inc(passed, 1)
                    hi = sh[:, ds(f, 1), :].rearrange("p o x -> p (o x)")
                    dve.tensor_copy(hi, sb2[:, k]).then_inc(as_hi, 1)
                    dve.wait_ge(as_hi, raised(f + 1))
                    dve.tensor_tensor(sl[:, ds(f, 1), :].rearrange("p o x -> p (o x)"), sb2[:, k], hi.bitcast(F32),
                                      ALU.subtract).then_inc(as_lo, 1)

            def d_tile(g, d, k, after, last):
                q = DC * g + d
                n = UNITS * g + 2 * FT + SLOTS * d
                weights_low(n + 2, 2, D_PARTS[2])
                weights_low(n + 3, 3, D_PARTS[3])
                weights_low(n + 4, 0, after)
                weights_low(n + 5, 1, after)
                dve.wait_ge(y_sent, raised(g))
                dve.wait_ge(y_turned, raised(q + 1))
                dve.sem_inc(passed, 1)
                if last:
                    dve.tensor_copy(ys[:, ds(d * P, P)], up[k][0:NS, 0:P])
                dve.tensor_copy(yn[:, :, ds(d * P, P)], tp[k][:].rearrange("p (b x) -> p b x", b=TPG)).then_inc(y_ok, 1)

            def beside(g, f, last):
                if f > 0:
                    return
                for b in range(TPG + last):
                    r = P if b < TPG else NS
                    n = TPG * g + b
                    dve.wait_ge(y_sq, raised(n + 1))
                    dve.tensor_tensor(s4[0:r, b, 2:3], s4[0:r, b, 0:1], s4[0:r, b, 1:2], ALU.add).then_inc(y_sum, 1)
                for b in range(TPG + last):
                    r = P if b < TPG else NS
                    y = yn[:, b] if b < TPG else ys[:]
                    n = TPG * g + b
                    dve.wait_ge(y_sd, raised(n + 1))
                    dve.reciprocal(s4[0:r, b, 4:5], s4[0:r, b, 3:4]).then_inc(y_rs, 1)
                    dve.wait_ge(y_rs, raised(n + 1))
                    dve.scalar_tensor_tensor(y, y, s4[0:r, b, 4:5], gain[0:r], ALU.mult, ALU.mult).then_inc(y_norm, 1)

            groups(dve, f_tile, d_tile, beside)
            for n in range((FT + 3) // 4):
                dve.wait_ge(fin_t, raised(n + 1))
                w = min(4, FT - 4 * n) * P
                src = (gp, up)[n % 2]
                if n == 0:
                    dve.wait_ge(y_sent, raised(NG))
                flat = yn[:].rearrange("p a d -> p (a d)")
                dve.tensor_copy(flat[0:2, 512 * n:512 * n + w], src[0][0:2, 0:w])
                dve.tensor_copy(flat[32:32 + 2 * DEC_B, 512 * n:512 * n + w], src[1][0:2 * DEC_B, 0:w]).then_inc(fin_r, 1)
def program(nc, a, out):
    (y_prompt, y_sample, a_k_prompt, a_v_prompt, a_k_sample, a_v_sample, win_k_prompt, win_v_prompt,
     win_k_sample, win_v_sample, conv_prompt, conv_sample) = out

    def rows(x):
        return x[0].rearrange("n s h e -> (n s) (h e)")

    def by_sequence(x):
        return x[0].rearrange("n s h e -> n s (h e)")

    def scratch(name, shape):
        return nc.dram_tensor(f"scratch_{name}", shape, F32).ap()

    t = {name: a[name][0] for name in (
        "norm_mix_pre", "w_in", "lambda_q1", "lambda_k1", "lambda_q2", "lambda_k2", "subln_a", "norm_b_out", "w_out",
        "norm_mix_post", "norm_ffn_pre", "w_gate", "w_up", "w_conv", "b_conv", "w_down", "norm_ffn_post", "x_prompt")}
    t |= {name: x for name, x in a.items() if name.startswith("c_")}
    t["x_sample"] = a["x_sample"].rearrange("s t d -> (s t) d")
    t["page_table"] = a["page_table"].rearrange("(o s) n -> o (s n)", o=1)
    t["n_phys"] = a["cache_a_k"].shape[1]
    t["cache_k"] = {"a": by_sequence(a["cache_a_k"]), "b": by_sequence(a["cache_win_k"])}
    t["cache_v"] = {"a": by_sequence(a["cache_a_v"]), "b": by_sequence(a["cache_win_v"])}
    t["win_cache"] = [t["cache_k"]["b"], t["cache_v"]["b"]]
    t["state_conv"] = a["state_conv"][0].rearrange("s j f -> (s j) f")
    t["kv_out"] = [rows(a_k_prompt), rows(a_v_prompt), rows(win_k_prompt), rows(win_v_prompt)]
    t["a_out"] = [rows(a_k_sample), rows(a_v_sample)]
    t["win_out"] = [by_sequence(win_k_sample), by_sequence(win_v_sample)]
    t["y_prompt"], t["y_sample"] = y_prompt[0], y_sample.rearrange("s t d -> (s t) d")
    t["conv_prompt"], t["conv_sample"] = conv_prompt[0, 0], conv_sample[0].rearrange("s j f -> (s j) f")
    t["qT"] = scratch("qT", [2, 8, P, SEQ])
    t["kT"] = scratch("kT", [2, 8, P, SEQ])
    t["v_split"] = scratch("v_split", [2, 2, SEQ, 512])
    t["s_feat"] = scratch("s_feat", [2, 8, P, NS])
    t["s_rows"] = scratch("s_rows", [4, NS, 512])
    t["oa"] = scratch("oa", [SEQ, 512])
    t["ob"] = scratch("ob", [NPAT, SEQ, 512])
    t["stats"] = scratch("stats", [NPAT, SEQ, 2 * B_HEADS])
    t["nlam"] = scratch("nlam", [P, 1])
    t["s_mix"] = scratch("s_mix", [NS, D])
    t["x1"] = scratch("x1", [TOK, D])
    t["h2T"] = scratch("h2T", [2, P, DC, TOK])
    stage_norm_project(nc, t)
    attend_a(nc, t)
    attend_b(nc, t)
    attend_sample(nc, t)
    mix(nc, t)
    ffn(nc, t)


def constants():
    import numpy as np

    f32 = np.float32
    slope_a = 2.0 ** (-8.0 * (np.arange(A_HEADS) + 1) / A_HEADS)
    slope_b = 2.0 ** (-8.0 * (np.arange(B_HEADS) + 1) / B_HEADS)

    def bias(slope, dist, ok):
        return np.where(ok, -slope * dist, MASKED).astype(f32)

    p = np.arange(P)
    dist = p[:, None] - (np.arange(SEQ)[None] - (SEQ - P))
    c = {"c_ident": np.eye(P, dtype=f32), "c_bias_a": np.stack([bias(s, dist, dist >= 0) for s in slope_a])}
    steps = p[:, None] + P - np.arange(2 * P)[None]
    ok = (steps >= 0) & (steps <= P)
    c["c_bias_b"] = np.stack([np.stack([bias(s, d * steps, ok) for d in DILS]) for s in slope_b])
    col = np.arange(32)
    j, m, tok = col // QC, col % QC // DEC_T, col % DEC_T
    new = PAST + p[:, None]
    paged = np.concatenate([P * np.arange(PAGES)[None] + p[:, None], new], 1)
    old = 16 * (32 * np.arange(W_OLD)[None] + (p % 32)[:, None]) + (p // 32)[:, None]
    recent = PAST - 512 + P * np.arange(W_NEW)[None] + p[:, None]
    window = np.concatenate([old, recent, new], 1)
    back = lambda pos: PAST + tok[None, None] - pos[:, :, None]
    real = lambda pos: (pos < PAST + DEC_T)[:, :, None]
    c["c_bias_da"] = bias(slope_a[j], back(paged), (back(paged) >= 0) & real(paged))
    d = back(window)
    count = sum(((d >= 0) & (d <= P * dil) & (d % dil == 0)).astype(int) for dil in DILS) * real(window)
    c["c_bias_db"] = bias(slope_b[2 * j + m], d, count > 0)
    c["c_count"] = count.astype(f32)
    return c


_INS = ["x_prompt", "x_sample", "cache_a_k", "cache_a_v", "page_table", "cache_win_k", "cache_win_v", "state_conv",
        "norm_mix_pre", "w_in", "lambda_q1", "lambda_k1", "lambda_q2", "lambda_k2", "subln_a", "norm_b_out", "w_out",
        "norm_mix_post", "norm_ffn_pre", "w_gate", "w_up", "w_conv", "b_conv", "w_down", "norm_ffn_post"]
_OUTS = [(1, SEQ, D), (DEC_B, DEC_T, D), (1, 1, SEQ, A_HEADS, P), (1, 1, SEQ, A_HEADS, P),
         (1, DEC_B, DEC_T, A_HEADS, P), (1, DEC_B, DEC_T, A_HEADS, P), (1, 1, SEQ, B_HEADS, 64),
         (1, 1, SEQ, B_HEADS, 64), (1, DEC_B, PAST, B_HEADS, 64), (1, DEC_B, PAST, B_HEADS, 64),
         (1, 1, 2, D_FF), (1, DEC_B, 2, D_FF)]


def kernel(**inputs):
    import numpy as _np
    import concourse.bacc as _bacc
    from concourse.bass_utils import run_bass_kernel_spmd as _run

    nc = _bacc.Bacc("TRN2", target_bir_lowering=False, num_devices=1)
    arrays, args = {}, {}
    given = {name: _np.ascontiguousarray(inputs[name]) for name in _INS} | constants()
    for name, x in given.items():
        arrays[f"in_{name}"] = x
        args[name] = nc.dram_tensor(f"in_{name}", x.shape, mybir.dt.from_np(x.dtype), kind="ExternalInput").ap()
    outs = [nc.dram_tensor(f"out_{i}", shape, F32, kind="ExternalOutput").ap() for i, shape in enumerate(_OUTS)]
    program(nc, args, outs)
    r = _run(nc, [arrays], core_ids=[0])
    return tuple(r.results[0][f"out_{i}"] for i in range(len(_OUTS)))
```
